# Optimizing a Trainium2 kernel written in Bass

```python
import math
import jax, jax.numpy as jnp
from jax import lax
import numpy as np

D_MODEL = 1024
BATCH = 1
SEQ = 512
DEPTH = 2
DEC_BATCH = 8
DEC_SEQ = 4
PAST_LEN = 512
PAGE_SIZE = 128

N_A_LAYERS = DEPTH // 2
N_B_LAYERS = DEPTH - N_A_LAYERS
A_INNER = 2 * D_MODEL
A_HEADS = 4
A_HEAD_DIM = A_INNER // A_HEADS
A_CONV = 4
A_QKV_BLOCK = 4
A_N_QKV_BLOCKS = A_INNER // A_QKV_BLOCK
A_CHUNK = 64
B_HEADS = 16
B_HEAD_DIM = 64
B_KV_HEADS = 4
B_HPG = B_HEADS // B_KV_HEADS
B_ATT = B_HEADS * B_HEAD_DIM
N_KV_SLOTS = 6
N_CACHE_SLOTS = 4
CMP_LEN = 32
CMP_STRIDE = 16
CMP_HIDDEN = 4 * B_HEAD_DIM
SEL_LEN = 64
SEL_TOPN = 16
WINDOW = 512
Q_BLOCK = 64
FORCE_BONUS = 1.0e3
NEG = -1.0e30
EPS = 1e-6

kernel_name = 'mlstm_nsa_yoco_step'

def _rmsnorm(x, w):
    xf = x.astype(jnp.float32)
    y = xf * lax.rsqrt(jnp.mean(xf * xf, axis=-1, keepdims=True) + EPS)
    return (y * w.astype(jnp.float32)).astype(x.dtype)

def _headnorm(h, w):
    mu = jnp.mean(h, axis=-1, keepdims=True)
    var = jnp.mean(jnp.square(h - mu), axis=-1, keepdims=True)
    hn = (h - mu) * lax.rsqrt(var + EPS)
    return hn.reshape(h.shape[0], h.shape[1], -1) * w.astype(jnp.float32)

def _masked_softmax(s, mask):
    s = jnp.where(mask, s.astype(jnp.float32), NEG)
    return jnp.where(mask, jax.nn.softmax(s, axis=-1), 0.0)

def _headwise(x, w):
    b, s, _ = x.shape
    xb = x.reshape(b, s, A_N_QKV_BLOCKS, A_QKV_BLOCK)
    return jnp.einsum('bsnc,ncd->bsnd', xb, w).reshape(b, s, A_INNER)

def _mlstm_chunk(carry, inp):
    c_st, n_st, m_st = carry
    q, k, v, ig, lf = inp
    L = q.shape[2]
    b = jnp.cumsum(lf, axis=-1)
    causal = np.tril(np.ones((L, L), dtype=bool))
    d = jnp.where(causal, b[..., :, None] - b[..., None, :] + ig[..., None, :], NEG)
    m_inter = b + m_st[..., None]
    m_t = jnp.maximum(m_inter, jnp.max(d, axis=-1))
    s = jnp.einsum('bhtd,bhsd->bhts', q, k) * jnp.exp(d - m_t[..., None])
    w_inter = jnp.exp(m_inter - m_t)
    num = jnp.einsum('bhts,bhse->bhte', s, v) + w_inter[..., None] * jnp.einsum('bhtd,bhde->bhte', q, c_st)
    den = jnp.sum(s, axis=-1) + w_inter * jnp.einsum('bhtd,bhd->bht', q, n_st)
    h = num / jnp.maximum(jnp.abs(den), jnp.exp(-m_t))[..., None]
    m_new = m_t[..., -1]
    w_row = jnp.exp(b[..., -1:] - b + ig - m_new[..., None])
    decay = jnp.exp(b[..., -1] + m_st - m_new)
    c_new = decay[..., None, None] * c_st + jnp.einsum('bhs,bhsd,bhse->bhde', w_row, k, v)
    n_new = decay[..., None] * n_st + jnp.einsum('bhs,bhsd->bhd', w_row, k)
    return (c_new, n_new, m_new), h

def _mlstm_cell(q, k, v, ig, lf, c0, n0, m0, chunk):
    bsz, nh, s, dh = q.shape
    nc = s // chunk

    def split(a):
        return jnp.moveaxis(a.reshape(a.shape[:2] + (nc, chunk) + a.shape[3:]), 2, 0)

    (c, n, m), h = lax.scan(_mlstm_chunk, (c0, n0, m0), (split(q), split(k), split(v), split(ig), split(lf)))
    h = jnp.moveaxis(h, 0, 2).reshape(bsz, nh, s, dh)
    return h, c, n, m

def _mlstm_layer(x, c0, n0, m0, conv0, chunk, norm_pre, w_up, conv_w, conv_b, w_q, w_k, w_v,
                 w_if, b_if, mh_w, skip, w_down, norm_post):
    f32 = jnp.float32
    bsz, s, _ = x.shape
    h = _rmsnorm(x, norm_pre)
    up = h @ w_up
    xm, z = up[..., :A_INNER], up[..., A_INNER:]
    xpad = jnp.concatenate([conv0.astype(xm.dtype), xm], axis=1)
    xconv = conv_b + xpad[:, 0:s] * conv_w[0]
    for j in range(1, A_CONV):
        xconv = xconv + xpad[:, j:j + s] * conv_w[j]
    xc = jax.nn.silu(xconv)
    conv_new = xpad[:, s:]
    q = _headwise(xc, w_q)
    k = _headwise(xc, w_k)
    v = _headwise(xm, w_v)
    gates = (jnp.concatenate([q, k, v], axis=-1) @ w_if + b_if).astype(f32)
    ig = jnp.transpose(gates[..., :A_HEADS], (0, 2, 1))
    lf = jnp.transpose(jax.nn.log_sigmoid(gates[..., A_HEADS:]), (0, 2, 1))

    def heads(a):
        return a.reshape(bsz, s, A_HEADS, A_HEAD_DIM).transpose(0, 2, 1, 3).astype(f32)

    hcell, c, n, m = _mlstm_cell(heads(q), heads(k) * (A_HEAD_DIM ** -0.5), heads(v), ig, lf,
                                 c0.astype(f32), n0.astype(f32), m0.astype(f32), chunk)
    hn = _headnorm(hcell.transpose(0, 2, 1, 3), mh_w)
    out = ((hn + skip.astype(f32) * xc.astype(f32)) * jax.nn.silu(z.astype(f32))).astype(x.dtype)
    y = _rmsnorm(out @ w_down, norm_post)
    return x + y, c.astype(c0.dtype), n.astype(n0.dtype), m.astype(m0.dtype), conv_new.astype(conv0.dtype)

def _shared_kv(x, kv_norm, w_kv):
    bsz, s, _ = x.shape
    return (_rmsnorm(x, kv_norm) @ w_kv).reshape(bsz, s, N_KV_SLOTS, B_KV_HEADS, B_HEAD_DIM)

def _compress(rows, pos, w1, b1, w2, b2):
    bsz, t, g, dh = rows.shape
    nc = (t - CMP_LEN) // CMP_STRIDE + 1
    idx = np.arange(nc)[:, None] * CMP_STRIDE + np.arange(CMP_LEN)[None, :]
    blk = rows[:, idx] + pos[:, None, :]
    flat = blk.transpose(0, 1, 3, 2, 4).reshape(bsz, nc, g, CMP_LEN * dh)
    return jax.nn.silu(flat @ w1 + b1) @ w2 + b2

def _sel_blocks(rows):
    bsz, t, g, dh = rows.shape
    ns = -(-t // SEL_LEN)
    rows = jnp.pad(rows, ((0, 0), (0, ns * SEL_LEN - t), (0, 0), (0, 0)))
    return rows.reshape(bsz, ns, SEL_LEN, g, dh).transpose(0, 3, 1, 2, 4)

def _nsa_context(kv4, cmp_pos, cmp_w1, cmp_b1, cmp_w2, cmp_b2):
    kcmp = _compress(kv4[:, :, 0], cmp_pos[0], cmp_w1[0], cmp_b1[0], cmp_w2[0], cmp_b2[0])
    vcmp = _compress(kv4[:, :, 1], cmp_pos[1], cmp_w1[1], cmp_b1[1], cmp_w2[1], cmp_b2[1])
    return kcmp, vcmp, _sel_blocks(kv4[:, :, 2]), _sel_blocks(kv4[:, :, 3])

def _nsa_core(q, qpos, kcmp, vcmp, ks_blk, vs_blk, kwin, vwin, wpos):
    bsz, nq = q.shape[:2]
    qg = q.reshape(bsz, nq, B_KV_HEADS, B_HPG, B_HEAD_DIM)
    scale = B_HEAD_DIM ** -0.5
    nc = kcmp.shape[1]
    ns = ks_blk.shape[2]
    cmp_start = np.arange(nc) * CMP_STRIDE
    cmp_end = cmp_start + CMP_LEN - 1
    s = jnp.einsum('bqghd,bngd->bghqn', qg, kcmp) * scale
    p_cmp = _masked_softmax(s, cmp_end[None, :] <= qpos[:, None])
    o_cmp = jnp.einsum('bghqn,bngd->bqghd', p_cmp.astype(vcmp.dtype), vcmp)
    sel_start = np.arange(ns) * SEL_LEN
    cover = ((cmp_start[:, None] < sel_start[None, :] + SEL_LEN)
             & (cmp_end[:, None] >= sel_start[None, :])).astype(np.float32)
    imp = jnp.einsum('bgqn,ns->bgqs', jnp.sum(p_cmp, axis=2), cover)
    cur = qpos // SEL_LEN
    jb = np.arange(ns)
    forced = (jb[None, :] == 0) | (jb[None, :] == cur[:, None]) | (jb[None, :] == cur[:, None] - 1)
    valid = sel_start[None, :] <= qpos[:, None]
    score = jnp.where(valid, imp + jnp.where(forced, FORCE_BONUS, 0.0), NEG)
    n_top = min(SEL_TOPN, ns)
    _, idx = lax.top_k(score, n_top)
    bi = jnp.arange(bsz)[:, None, None, None]
    gi = jnp.arange(B_KV_HEADS)[None, :, None, None]
    kb = ks_blk[bi, gi, idx].reshape(bsz, B_KV_HEADS, nq, n_top * SEL_LEN, B_HEAD_DIM)
    vb = vs_blk[bi, gi, idx].reshape(bsz, B_KV_HEADS, nq, n_top * SEL_LEN, B_HEAD_DIM)
    kpos = (idx[..., None] * SEL_LEN + jnp.arange(SEL_LEN)).reshape(bsz, B_KV_HEADS, nq, n_top * SEL_LEN)
    s = jnp.einsum('bqghd,bgqkd->bghqk', qg, kb) * scale
    p = _masked_softmax(s, (kpos <= qpos[None, None, :, None])[:, :, None])
    o_sel = jnp.einsum('bghqk,bgqkd->bqghd', p.astype(vb.dtype), vb)
    s = jnp.einsum('bqghd,bkgd->bghqk', qg, kwin) * scale
    wmask = ((wpos[None, :] <= qpos[:, None]) & (wpos[None, :] > qpos[:, None] - WINDOW)
             & (wpos[None, :] >= 0))
    p = _masked_softmax(s, wmask)
    o_win = jnp.einsum('bghqk,bkgd->bqghd', p.astype(vwin.dtype), vwin)
    o = jnp.stack([o_cmp, o_sel, o_win], axis=2)
    return o.reshape(bsz, nq, 3, B_HEADS, B_HEAD_DIM)

def _nsa_prompt_attend(q, ctx, kwin_full, vwin_full):
    bsz, s, nh, dh = q.shape
    nqb = s // Q_BLOCK
    kcmp, vcmp, ksb, vsb = ctx
    pad = ((0, 0), (WINDOW, 0), (0, 0), (0, 0))
    kwp = jnp.pad(kwin_full, pad)
    vwp = jnp.pad(vwin_full, pad)
    qb = jnp.moveaxis(q.reshape(bsz, nqb, Q_BLOCK, nh, dh), 1, 0)

    def one(args):
        qi, n = args
        q0 = n * Q_BLOCK
        qpos = q0 + jnp.arange(Q_BLOCK)
        kw = lax.dynamic_slice_in_dim(kwp, q0, Q_BLOCK + WINDOW, axis=1)
        vw = lax.dynamic_slice_in_dim(vwp, q0, Q_BLOCK + WINDOW, axis=1)
        wpos = q0 - WINDOW + jnp.arange(Q_BLOCK + WINDOW)
        return _nsa_core(qi, qpos, kcmp, vcmp, ksb, vsb, kw, vw, wpos)

    o = lax.map(one, (qb, jnp.arange(nqb)))
    return jnp.moveaxis(o, 0, 1).reshape(bsz, s, 3, nh, dh)

def _nsa_layer(x, attend, norm_pre, w_in, w_out, norm_post):
    f32 = jnp.float32
    bsz, s, _ = x.shape
    p = _rmsnorm(x, norm_pre) @ w_in
    q = p[..., :B_ATT].reshape(bsz, s, B_HEADS, B_HEAD_DIM)
    z = p[..., B_ATT:4 * B_ATT].reshape(bsz, s, 3, B_ATT)
    g = jax.nn.sigmoid(p[..., 4 * B_ATT:].astype(f32)).reshape(bsz, s, 3, B_HEADS)
    o = attend(q)
    y = (o.astype(f32) * g[..., None]).reshape(bsz, s, 3, B_ATT) * jax.nn.silu(z.astype(f32))
    y = jnp.sum(y, axis=2).astype(x.dtype) @ w_out
    return x + _rmsnorm(y, norm_post)

def setup_inputs(seed: int = 0) -> dict:
    key = jax.random.key(seed)
    ks = jax.random.split(key, 40)
    f32 = jnp.float32
    n_pages = PAST_LEN // PAGE_SIZE
    n_used = DEC_BATCH * n_pages
    n_pool = n_used + n_used // 4
    wb = min(WINDOW, PAST_LEN)

    def nrm(k, shape, scale):
        return jax.random.normal(k, shape, f32) * scale

    x_prompt = nrm(ks[0], (BATCH, SEQ, D_MODEL), 1.0)
    x_sample = nrm(ks[1], (DEC_BATCH, DEC_SEQ, D_MODEL), 1.0)
    cache_kv = nrm(ks[2], (n_pool, PAGE_SIZE, N_CACHE_SLOTS, B_KV_HEADS, B_HEAD_DIM), 1.0)
    page_table = jax.random.permutation(ks[3], n_pool)[:n_used].reshape(DEC_BATCH, n_pages).astype(jnp.int32)
    cache_win = nrm(ks[4], (DEC_BATCH, wb, 2, B_KV_HEADS, B_HEAD_DIM), 1.0)
    state_C = nrm(ks[5], (N_A_LAYERS, DEC_BATCH, A_HEADS, A_HEAD_DIM, A_HEAD_DIM), 0.02)
    state_n = nrm(ks[6], (N_A_LAYERS, DEC_BATCH, A_HEADS, A_HEAD_DIM), 0.1)
    state_m = nrm(ks[7], (N_A_LAYERS, DEC_BATCH, A_HEADS), 0.5)
    state_conv = nrm(ks[8], (N_A_LAYERS, DEC_BATCH, A_CONV - 1, A_INNER), 1.0)

    a_norm_pre = 1.0 + nrm(ks[9], (N_A_LAYERS, D_MODEL), 0.02)
    a_w_up = nrm(ks[10], (N_A_LAYERS, D_MODEL, 2 * A_INNER), D_MODEL ** -0.5)
    a_conv_w = nrm(ks[11], (N_A_LAYERS, A_CONV, A_INNER), A_CONV ** -0.5)
    a_conv_b = nrm(ks[12], (N_A_LAYERS, A_INNER), 0.02)
    a_w_q = nrm(ks[13], (N_A_LAYERS, A_N_QKV_BLOCKS, A_QKV_BLOCK, A_QKV_BLOCK), A_QKV_BLOCK ** -0.5)
    a_w_k = nrm(ks[14], (N_A_LAYERS, A_N_QKV_BLOCKS, A_QKV_BLOCK, A_QKV_BLOCK), A_QKV_BLOCK ** -0.5)
    a_w_v = nrm(ks[15], (N_A_LAYERS, A_N_QKV_BLOCKS, A_QKV_BLOCK, A_QKV_BLOCK), A_QKV_BLOCK ** -0.5)
    a_w_if = nrm(ks[16], (N_A_LAYERS, 3 * A_INNER, 2 * A_HEADS), (3 * A_INNER) ** -0.5)
    a_b_if = jnp.concatenate([nrm(ks[17], (N_A_LAYERS, A_HEADS), 0.1),
                              3.0 + 3.0 * jax.random.uniform(ks[18], (N_A_LAYERS, A_HEADS), f32)], axis=-1)
    a_mh_w = 1.0 + nrm(ks[19], (N_A_LAYERS, A_INNER), 0.02)
    a_skip = 1.0 + nrm(ks[20], (N_A_LAYERS, A_INNER), 0.02)
    a_w_down = nrm(ks[21], (N_A_LAYERS, A_INNER, D_MODEL), A_INNER ** -0.5)
    a_norm_post = 1.0 + nrm(ks[22], (N_A_LAYERS, D_MODEL), 0.02)

    kv_norm = 1.0 + nrm(ks[23], (D_MODEL,), 0.02)
    w_kv = nrm(ks[24], (D_MODEL, N_KV_SLOTS * B_KV_HEADS * B_HEAD_DIM), D_MODEL ** -0.5)
    cmp_pos = nrm(ks[25], (2, CMP_LEN, B_HEAD_DIM), 0.1)
    cmp_w1 = nrm(ks[26], (2, CMP_LEN * B_HEAD_DIM, CMP_HIDDEN), (CMP_LEN * B_HEAD_DIM) ** -0.5)
    cmp_b1 = nrm(ks[27], (2, CMP_HIDDEN), 0.02)
    cmp_w2 = nrm(ks[28], (2, CMP_HIDDEN, B_HEAD_DIM), 1.7 * CMP_HIDDEN ** -0.5)
    cmp_b2 = nrm(ks[29], (2, B_HEAD_DIM), 0.02)

    b_norm_pre = 1.0 + nrm(ks[30], (N_B_LAYERS, D_MODEL), 0.02)
    b_w_in = nrm(ks[31], (N_B_LAYERS, D_MODEL, 4 * B_ATT + 3 * B_HEADS), D_MODEL ** -0.5)
    b_w_out = nrm(ks[32], (N_B_LAYERS, B_ATT, D_MODEL), B_ATT ** -0.5)
    b_norm_post = 1.0 + nrm(ks[33], (N_B_LAYERS, D_MODEL), 0.02)

    return {'x_prompt': x_prompt, 'x_sample': x_sample, 'cache_kv': cache_kv, 'page_table': page_table,
            'cache_win': cache_win, 'state_C': state_C, 'state_n': state_n, 'state_m': state_m,
            'state_conv': state_conv,
            'a_norm_pre': a_norm_pre, 'a_w_up': a_w_up, 'a_conv_w': a_conv_w, 'a_conv_b': a_conv_b,
            'a_w_q': a_w_q, 'a_w_k': a_w_k, 'a_w_v': a_w_v, 'a_w_if': a_w_if, 'a_b_if': a_b_if,
            'a_mh_w': a_mh_w, 'a_skip': a_skip, 'a_w_down': a_w_down, 'a_norm_post': a_norm_post,
            'kv_norm': kv_norm, 'w_kv': w_kv, 'cmp_pos': cmp_pos, 'cmp_w1': cmp_w1, 'cmp_b1': cmp_b1,
            'cmp_w2': cmp_w2, 'cmp_b2': cmp_b2,
            'b_norm_pre': b_norm_pre, 'b_w_in': b_w_in, 'b_w_out': b_w_out, 'b_norm_post': b_norm_post}

def reference(x_prompt, x_sample, cache_kv, page_table, cache_win, state_C, state_n, state_m, state_conv,
              a_norm_pre, a_w_up, a_conv_w, a_conv_b, a_w_q, a_w_k, a_w_v, a_w_if, a_b_if,
              a_mh_w, a_skip, a_w_down, a_norm_post,
              kv_norm, w_kv, cmp_pos, cmp_w1, cmp_b1, cmp_w2, cmp_b2,
              b_norm_pre, b_w_in, b_w_out, b_norm_post):
    bp, sp = x_prompt.shape[0], x_prompt.shape[1]
    bs, ds = x_sample.shape[0], x_sample.shape[1]
    past_len = page_table.shape[1] * cache_kv.shape[1]
    xp, xs = x_prompt, x_sample
    cp_l, cs_l, np_l, ns_l, mp_l, ms_l, vp_l, vs_l = [], [], [], [], [], [], [], []
    for layer in range(DEPTH):
        if layer < N_A_LAYERS:
            a = (a_norm_pre[layer], a_w_up[layer], a_conv_w[layer], a_conv_b[layer], a_w_q[layer],
                 a_w_k[layer], a_w_v[layer], a_w_if[layer], a_b_if[layer], a_mh_w[layer], a_skip[layer],
                 a_w_down[layer], a_norm_post[layer])
            c0 = jnp.zeros((bp, A_HEADS, A_HEAD_DIM, A_HEAD_DIM), state_C.dtype)
            n0 = jnp.zeros((bp, A_HEADS, A_HEAD_DIM), state_n.dtype)
            m0 = jnp.full((bp, A_HEADS), NEG, state_m.dtype)
            v0 = jnp.zeros((bp, A_CONV - 1, A_INNER), state_conv.dtype)
            xp, c1, n1, m1, v1 = _mlstm_layer(xp, c0, n0, m0, v0, A_CHUNK, *a)
            xs, c2, n2, m2, v2 = _mlstm_layer(xs, state_C[layer], state_n[layer], state_m[layer],
                                              state_conv[layer], ds, *a)
            cp_l.append(c1); np_l.append(n1); mp_l.append(m1); vp_l.append(v1)
            cs_l.append(c2); ns_l.append(n2); ms_l.append(m2); vs_l.append(v2)
        else:
            if layer == N_A_LAYERS:
                kvp = _shared_kv(xp, kv_norm, w_kv)
                kvs = _shared_kv(xs, kv_norm, w_kv)
                past = cache_kv[page_table].reshape(bs, past_len, N_CACHE_SLOTS, B_KV_HEADS, B_HEAD_DIM)
                full_s = jnp.concatenate([past, kvs[:, :, :N_CACHE_SLOTS].astype(past.dtype)], axis=1)
                ctx_p = _nsa_context(kvp[:, :, :N_CACHE_SLOTS], cmp_pos, cmp_w1, cmp_b1, cmp_w2, cmp_b2)
                ctx_s = _nsa_context(full_s, cmp_pos, cmp_w1, cmp_b1, cmp_w2, cmp_b2)
                wb = cache_win.shape[1]
                win_all = jnp.concatenate([cache_win, kvs[:, :, N_CACHE_SLOTS:].astype(cache_win.dtype)], axis=1)
                qpos_s = past_len + jnp.arange(ds)
                wpos_s = past_len - wb + jnp.arange(wb + ds)
                kv_rows_prompt = kvp[:, :, :N_CACHE_SLOTS]
                kv_rows_sample = kvs[:, :, :N_CACHE_SLOTS]
                win_prompt = kvp[:, sp - min(WINDOW, sp):, N_CACHE_SLOTS:]
                win_sample = win_all[:, ds:]
            lb = layer - N_A_LAYERS
            bw = (b_norm_pre[lb], b_w_in[lb], b_w_out[lb], b_norm_post[lb])
            xp = _nsa_layer(xp, lambda q: _nsa_prompt_attend(q, ctx_p, kvp[:, :, 4], kvp[:, :, 5]), *bw)
            xs = _nsa_layer(xs, lambda q: _nsa_core(q, qpos_s, ctx_s[0], ctx_s[1], ctx_s[2], ctx_s[3],
                                                    win_all[:, :, 0], win_all[:, :, 1], wpos_s), *bw)
    y_prompt, y_sample = xp, xs
    C_prompt, C_sample = jnp.stack(cp_l), jnp.stack(cs_l)
    n_prompt, n_sample = jnp.stack(np_l), jnp.stack(ns_l)
    m_prompt, m_sample = jnp.stack(mp_l), jnp.stack(ms_l)
    conv_prompt, conv_sample = jnp.stack(vp_l), jnp.stack(vs_l)
    return (y_prompt, y_sample, kv_rows_prompt, kv_rows_sample, win_prompt, win_sample,
            C_prompt, C_sample, n_prompt, n_sample, m_prompt, m_sample, conv_prompt, conv_sample)


_drawn_inputs = setup_inputs


def setup_inputs(seed=0):
    import zlib

    import numpy as np

    out = dict(_drawn_inputs(seed))
    spreads = {}
    factors = {'a_mh_w': 3.917,
     'a_skip': 6.25,
     'a_norm_post': 3.203,
     'kv_norm': 2.91,
     'b_norm_pre': 3.866,
     'b_norm_post': 16.879,
     'cmp_b1': 5.551,
     'cmp_b2': 7.21}
    for name, (base, spread) in spreads.items():
        noise = np.random.default_rng([zlib.crc32(name.encode()), seed]).standard_normal(out[name].shape)
        drawn = base * np.exp(spread * noise) if base else spread * noise
        out[name] = __import__('jax').numpy.asarray(drawn.astype(out[name].dtype))
    for name, factor in factors.items():
        out[name] = (out[name] * factor).astype(out[name].dtype)
    return out
```

```python
import concourse.bass as bass
from concourse import mybir
from contextlib import ExitStack

F32 = mybir.dt.float32
BF16 = mybir.dt.bfloat16
I32 = mybir.dt.int32
ALU = mybir.AluOpType
ACT = mybir.ActivationFunctionType
AX = mybir.AxisListType

D = 1024
KD = D // 128
T = 512
NT = T // 128
SB, SI = 8, 4
S = SB * SI
TA = T + S
HALF = [(0, 256), (256, TA)]
INNER = 2048
FT = INNER // 128
AH, AD = 4, 512
HF = AD // 128
CONV = 4
XPW = CONV - 1 + T + SB * (CONV - 1 + SI)
XPS = CONV - 1 + T
H, DH, G = 16, 64, 4
HPG = H // G
ATT = H * DH
PAST = 512
SLOT = G * DH
NCMP = (T - 32) // 16 + 1
NEG = -1.0e30
EPS = 1e-6
NRING = 7
NW = 2
WCH = 8 * 512


class Ctx:
    pass


def weight_chunks(k):
    def cols(w, c0, n):
        return w[:, c0:c0 + n].rearrange("(kt p) n -> p kt n", p=128)
    out = [cols(k.w_up, 512 * c, 512) for c in range(8)]
    for n in range(2):
        for half in range(2):
            out.append(cols(k.w_down[1024 * half:1024 * half + 1024, :], 512 * n, 512))
    out += [cols(k.w_kv, 512 * c, 512) for c in range(3)]
    out += [k.cmp_w1[s].rearrange("(j p) n -> p j n", p=128) for s in range(2)]
    out += [cols(k.w_in, 0, 512), cols(k.w_in, 512, 512), cols(k.w_in, 4096, 48)]
    out += [cols(k.w_in, 512 * c, 512) for c in range(2, 8)]
    out += [cols(k.w_out, 512 * c, 512) for c in range(2)]
    return out


CH_UP, CH_DOWN, CH_KV, CH_CMP, CH_IN, CH_OUT, CH_END = 0, 8, 12, 15, 17, 26, 28


def load_chunks(sp, k, lo, hi):
    for c in range(lo, min(hi, CH_END)):
        src = k.chunks[c]
        n = src.shape[1] * src.shape[2]
        dst = k.wring[:, c % NW, 0:n].rearrange("p (a b) -> p a b", b=src.shape[2])
        if c >= NW:
            bank, n_full = k.chunk_last[c - NW]
            sp.wait_ge(k.half_done if bank == "half" else k.bank_full[bank], n_full)
        sp.dma_start(dst, src).then_inc(k.chunk_here[c % NW], 16)


def chunk(pe, k, c):
    src = k.chunks[c]
    pe.wait_ge(k.chunk_here[c % NW], 16 * (c // NW + 1))
    n = src.shape[1] * src.shape[2]
    return k.wring[:, c % NW, 0:n].rearrange("p (a b) -> p a b", b=src.shape[2])


def open_bank(pe, k, key):
    bank = k.turns % k.nring
    k.turns += 1
    n = k.bank_turns[bank]
    if n:
        pe.wait_ge(k.bank_free[bank], n)
    k.bank_turns[bank] = n + 1
    k.bank_of[key] = (bank, n + 1)
    return k.ps[:, bank], k.bank_full[bank]


def full_bank(eng, k, key):
    bank, n = k.bank_of[key]
    eng.wait_ge(k.bank_full[bank], n)
    return k.ps[:, bank], k.bank_free[bank]


def drained(eng, k, key):
    bank, n = k.bank_of[key]
    eng.wait_ge(k.bank_free[bank], n)


class Steps:

    def __init__(self, eng, sem, k, name):
        self.eng, self.sem, self.k, self.name = eng, sem, k, name

    def then(self, ins):
        self.k.steps[self.name] = n = self.k.steps.get(self.name, 0) + 1
        ins.then_inc(self.sem, 1)
        self.eng.wait_ge(self.sem, n)


def head_blocks(pool, k, r):
    for m3 in range(3):
        pool.tensor_tensor(k.bd[:, m3, :, :].rearrange("p f (n d) -> p f n d", d=4),
                           k.wraw[:, m3, 4 * r:4 * r + 4, :].unsqueeze(2).to_broadcast([128, 4, 32, 4]),
                           k.mask32[:, :].unsqueeze(1).unsqueeze(3).to_broadcast([128, 4, 32, 4]),
                           ALU.mult).then_inc(k.bd_ready, 1)


def stage_norm_in(nc, k, ctx):
    def sb(name, shape, dt=F32):
        return ctx.enter_context(nc.sbuf_tensor(name, shape, dt))
    xt = sb("xt", [128, NT + 1, D])
    sq = sb("sq_junk", [128, D])
    ssq = sb("ssq", [128, NT + 1])
    rstd = sb("rstd", [128, NT + 1])
    v1raw = sb("v1raw", [112, 128])
    v2raw = sb("v2raw", [28, 128])
    block = ctx.enter_context(nc.Block())

    @block.tensor
    def _(pe):
        pe.wait_ge(k.ident_ready, 1)
        pe.wait_ge(k.vec_here, 8 * 16)
        for key, src, n in (("v1", v1raw, 112), ("v2", v2raw, 28)):
            b, full = open_bank(pe, k, key)
            pe.transpose(b[:, 0:n], src[:, :], k.ident[0:n, 0:n]).then_inc(full, 1)
        pe.wait_ge(k.xn_tok, NT + 1)
        for kt in range(KD):
            b, full = open_bank(pe, k, ("xT", kt))
            for i in range(NT):
                m = pe.transpose(b[:, 128 * i:128 * i + 128], xt[:, i, 128 * kt:128 * kt + 128], k.ident[:, :])
            m.then_inc(full, 1)
        b, full = open_bank(pe, k, "xTs")
        for kt in range(KD):
            m = pe.transpose(b[:, S * kt:S * kt + S], xt[0:S, NT, 128 * kt:128 * kt + 128], k.ident[0:S, 0:S])
        m.then_inc(full, 1)

    @block.sync
    def _(sp):
        sp.dma_start(xt[:, 0:NT, :], k.x_prompt[0].rearrange("(i p) d -> p i d", p=128)).then_inc(k.x_here, 16)
        sp.dma_start(xt[0:S, NT, :], k.x_sample.rearrange("b i d -> (b i) d")).then_inc(k.x_here, 16)
        for j, (src, n) in enumerate([(k.conv_w, 4 * FT), (k.conv_b, FT), (k.mh_w, FT), (k.skip, FT)]):
            row = [0, 64, 80, 96][j]
            sp.dma_start(v1raw[row:row + n, :], src.rearrange("(a p) -> a p", p=128)).then_inc(k.vec_here, 16)
        for j, (src, n) in enumerate([(k.a_norm_pre, 8), (k.kv_norm, 8), (k.b_norm_pre, 8), (k.cmp_b1, 4)]):
            row = 8 * j
            sp.dma_start(v2raw[row:row + n, :], src.rearrange("(a p) -> a p", p=128)).then_inc(k.vec_here, 16)
        load_chunks(sp, k, 0, NW)

    @block.gpsimd
    def _(pool):
        st = Steps(pool, k.pool_step, k, "pool")

        def make(t, fill, *selects):
            st.then(pool.memset(t, fill))
            for value, op, base, pattern, cm in selects:
                st.then(pool.affine_select(out=t, in_=t, compare_op=op, fill=value, base=base,
                                           pattern=pattern, channel_multiplier=cm))
        make(k.ident[:, :], 0.0, (1.0, ALU.not_equal, 0, [[-1, 128]], 1))
        pool.memset(k.ones[:, :], 1.0).then_inc(k.ident_ready, 1)
        make(k.mask32[:, :], 1.0, (0.0, ALU.is_ge, 0, [[-4, 32]], 1), (0.0, ALU.is_ge, 3, [[4, 32]], -1))
        make(k.maskT[:, :], 0.0, (NEG, ALU.is_ge, 0, [[1, 128]], -1))
        make(k.maskS[:, :], 0.0, (NEG, ALU.is_ge, 0, [[4, SB], [1, SI]], -1), (NEG, ALU.is_ge, 0, [[-4, SB], [0, SI]], 1))
        make(k.bmask[:, :, :], 0.0, (1.0, ALU.not_equal, 0, [[1, SB], [-1, SB], [0, SI]], 0))
        make(k.tmask[:, :], 1.0, (0.0, ALU.is_ge, 0, [[-4, SB]], 1), (0.0, ALU.is_ge, 3, [[4, SB]], -1))
        make(k.fold[:, :], 0.0, *[(1.0, ALU.not_equal, -32 * g, [[-1, S]], 1) for g in range(4)])
        make(k.headsel[:, :, :], 0.0, (1.0, ALU.not_equal, 0, [[-1, AH], [0, 128]], 1))
        st.then(pool.memset(k.scan_mul[:, :], 1.0))
        st.then(pool.memset(k.scan_mul[:, T:TA].rearrange("p (b i) -> p b i", i=SI)[:, :, 0:1], 0.0))
        st.then(pool.memset(k.scan_add[:, :], 0.0))
        st.then(pool.memset(k.scan_add[:, T:TA].rearrange("p (b i) -> p b i", i=SI)[:, :, 0:1], -1.0e38))

    @block.scalar
    def _(act):
        act.wait_ge(k.x_here, 32)
        act.wait_ge(k.ssq_clear, 1)
        for i in range(NT + 1):
            r = 128 if i < NT else S
            act.activation(sq[0:r, :], xt[0:r, i, :], ACT.Square, accum_out=ssq[0:r, i:i + 1]).then_inc(k.ssq_ready, 1)
            act.wait_ge(k.ssq_ready, i + 1)
        act.wait_ge(k.ms_ready, 1)
        act.activation(rstd[:, :], ssq[:, :], ACT.Sqrt).then_inc(k.std_ready, 1)
        for kt in range(KD):
            b, free = full_bank(act, k, ("xT", kt))
            act.activation(k.xnT[:, kt, 0:T], b[:, 0:T], ACT.Copy, scale=k.vecs2[:, kt:kt + 1]).then_inc(free, 1)

    @block.vector
    def _(dve):
        st = Steps(dve, k.dve_step, k, "dve")
        dve.memset(ssq[:, :], 1.0).then_inc(k.ssq_clear, 1)
        for key, dst, n in (("v1", k.vecs1, 112), ("v2", k.vecs2, 28)):
            b, free = full_bank(dve, k, key)
            dve.tensor_copy(dst[:, :], b[:, 0:n]).then_inc(free, 1)
        dve.wait_ge(k.ssq_ready, NT + 1)
        dve.tensor_scalar(ssq[:, :], ssq[:, :], 1.0 / D, EPS, ALU.mult, ALU.add).then_inc(k.ms_ready, 1)
        dve.wait_ge(k.std_ready, 1)
        st.then(dve.reciprocal(rstd[:, :], rstd[:, :]))
        for i in range(NT + 1):
            r = 128 if i < NT else S
            dve.tensor_scalar(xt[0:r, i, :], xt[0:r, i, :], rstd[0:r, i:i + 1], None, ALU.mult).then_inc(k.xn_tok, 1)
        b, free = full_bank(dve, k, "xTs")
        dve.tensor_tensor(k.xnT[:, :, T:TA], b[:, 0:KD * S].rearrange("p (a b) -> p a b", b=S),
                          k.vecs2[:, 0:KD].unsqueeze(2).to_broadcast([128, KD, S]), ALU.mult).then_inc(free, 1)


def stage_up(nc, k, ctx):
    def sb(name, shape, dt=F32):
        return ctx.enter_context(nc.sbuf_tensor(name, shape, dt))
    wif = sb("wif", [128, 3 * FT, 8])
    crow = sb("crow", [27, INNER])
    convt = sb("convt", [128, 2, XPW])
    bdt = sb("bdt", [128, 3, FT // 4, 128])
    nraw = sb("nraw", [128, 128])
    wc = sb("wc", [128, 2 * FT, 36])
    tails = sb("tails", [128, FT, 27])
    tail_rows = crow
    block = ctx.enter_context(nc.Block())
    RUN = XPW - 3
    q4 = FT // 4

    @block.tensor
    def _(pe):
        pe.wait_ge(k.crow_here, 16)
        b, full = open_bank(pe, k, "cs")
        for f in range(FT):
            m = pe.transpose(b[:, 24 * f:24 * f + 24], crow[0:24, 128 * f:128 * f + 128], k.ident[0:24, 0:24])
        m.then_inc(full, 1)
        pe.wait_ge(k.nraw_here, 16)
        b, full = open_bank(pe, k, "nT")
        pe.transpose(b[:, 0:128], nraw[:, :], k.ident[:, :]).then_inc(full, 1)
        drained(pe, k, ("xT", KD - 1))
        drained(pe, k, "xTs")
        for c in range(4):
            w = chunk(pe, k, CH_UP + c)
            for m4 in range(4):
                f = 4 * c + m4
                for hf, (t0, t1) in enumerate(HALF):
                    b, full = open_bank(pe, k, ("up", f, hf))
                    for kt in range(KD):
                        m = pe.matmul(b[:, 0:t1 - t0], w[:, kt, 128 * m4:128 * m4 + 128], k.xnT[:, kt, t0:t1],
                                      start=kt == 0, stop=kt == KD - 1)
                    m.then_inc(full, 1)
            k.chunk_last[CH_UP + c] = k.bank_of[("up", f, 1)]
            if c == 3:
                pe.wait_ge(k.wif_here, 16)
                for r in range(4):
                    pe.wait_ge(k.bd_ready, 3 * r + 3)
                    for m3 in range(3):
                        b, full = open_bank(pe, k, ("bdt", r, m3))
                        for g in range(q4):
                            m = pe.transpose(b[:, 128 * g:128 * g + 128], k.bd[:, m3, g, :], k.ident[:, :])
                        m.then_inc(full, 1)
                    b, full = open_bank(pe, k, ("wc", r))
                    drained(pe, k, ("bdt", r, 2))
                    for g in range(q4):
                        f = q4 * r + g
                        pe.matmul(b[:, 8 * g:8 * g + 8], bdt[:, 0, g, :], wif[:, f, :], start=True, stop=False)
                        pe.matmul(b[:, 8 * g:8 * g + 8], bdt[:, 1, g, :], wif[:, FT + f, :], start=False, stop=True)
                        m = pe.matmul(b[:, 32 + 8 * g:40 + 8 * g], bdt[:, 2, g, :], wif[:, 2 * FT + f, :],
                                      start=True, stop=True)
                    m.then_inc(full, 1)
        for r in range(4):
            drained(pe, k, ("wc", r))
        pe.wait_ge(k.xc_ready, FT)
        for hf, (t0, t1) in enumerate(HALF):
            b, full = open_bank(pe, k, ("gate", hf))
            for f in range(FT):
                pe.matmul(b[0:36, 0:t1 - t0], wc[:, f, :], k.xcT[:, f, t0:t1], start=f == 0, stop=False)
            for f in range(FT):
                if hf == 0:
                    m = pe.matmul(b[0:36, 0:256], wc[:, FT + f, :], k.xp[:, f, 3:259], start=False, stop=f == FT - 1)
                else:
                    pe.matmul(b[0:36, 0:256], wc[:, FT + f, :], k.xp[:, f, 259:515], start=False, stop=False)
                    m = pe.matmul(b[0:36, 256:288].rearrange("p (b i) -> p b i", i=SI), wc[:, FT + f, :],
                                  k.xs[:, f, :, 3:7], start=False, stop=f == FT - 1)
            m.then_inc(full, 1)
        pe.wait_ge(k.tails_ready, 2)
        for r in range(4):
            b, full = open_bank(pe, k, ("tail", r))
            for g in range(4):
                m = pe.transpose(b[0:27, 128 * g:128 * g + 128], tails[:, 4 * r + g, :], k.ident[:, :])
            m.then_inc(full, 1)

    @block.sync
    def _(sp):
        load_chunks(sp, k, NW, CH_UP + 4)

    @block.gpsimd
    def _(pool):
        pool.dma_start(crow[0:24, :], k.state_conv.rearrange("b j c -> (b j) c")).then_inc(k.crow_here, 16)
        for m3, w in enumerate((k.w_q, k.w_k, k.w_v)):
            pool.dma_start(k.wraw[:, m3, :, :], w.rearrange("(f n) c d -> (n c) f d", f=FT)).then_inc(k.wraw_here, 16)
        pool.dma_start(wif[:, :, :], k.w_if.rearrange("(a p) j -> p a j", p=128)).then_inc(k.wif_here, 16)
        pool.dma_start(k.bif[0:4, :], k.b_if[0:4].unsqueeze(1)).then_inc(k.bif_here, 16)
        pool.dma_start(k.bif[32:36, :], k.b_if[4:8].unsqueeze(1)).then_inc(k.bif_here, 16)
        pool.dma_start(k.m0[:, :], k.state_m.rearrange("b h -> h b"), allow_slow_non_contiguous=True).then_inc(k.m0_here, 16)
        pool.dma_start(nraw[:, :], k.state_n.rearrange("b h (f p) -> (b h f) p", p=128)).then_inc(k.nraw_here, 16)
        pool.wait_ge(k.wraw_here, 48)
        for r in range(4):
            if r:
                drained(pool, k, ("bdt", r - 1, 2))
            head_blocks(pool, k, r)
        drained(pool, k, ("tail", 3))
        pool.dma_start(k.o_conv_p, tail_rows[0:3, :]).then_inc(k.stored, 16)
        pool.dma_start(k.o_conv_s.rearrange("b j c -> (b j) c"), tail_rows[3:27, :]).then_inc(k.stored, 16)
        pool.wait_ge(k.stored, 32)

    @block.scalar
    def _(act):
        act.wait_ge(k.pad_clear, 2)
        for f in range(FT + 1):
            if f < FT:
                for hf in range(2):
                    b, free = full_bank(act, k, ("up", f, hf))
                    m = act.activation(k.xp[:, f, 3 + 256 * hf:259 + 256 * hf], b[:, 0:256], ACT.Copy)
                    if hf == 1:
                        m = act.activation(k.xs[:, f, :, 3:7], b[:, 256:288].rearrange("p (b i) -> p b i", i=SI), ACT.Copy)
                    m.then_inc(free, 1)
            if f:
                act.wait_ge(k.conv_ready, f)
                act.activation(k.xcT[:, f - 1, 0:T], convt[:, (f - 1) % 2, 0:T], ACT.Silu)
                act.activation(k.xcT[:, f - 1, T:TA].rearrange("p (b i) -> p b i", i=SI),
                               convt[:, (f - 1) % 2, 515:515 + 7 * SB].rearrange("p (b j) -> p b j", j=7)[:, :, 0:SI],
                               ACT.Silu).then_inc(k.xc_ready, 1)

    @block.vector
    def _(dve):
        st = Steps(dve, k.dve_step, k, "dve")
        dve.memset(k.xp[:, :, 0:3], 0.0).then_inc(k.pad_clear, 1)
        dve.memset(wc[:, :, :], 0.0).then_inc(k.pad_clear, 1)
        b, free = full_bank(dve, k, "cs")
        dve.tensor_copy(k.xs[:, :, :, 0:3], b[:, 0:24 * FT].rearrange("p (f b j) -> p f b j", b=SB, j=3)).then_inc(free, 1)
        dve.wait_ge(k.pad_clear, 2)
        drained(dve, k, "cs")
        b, free = full_bank(dve, k, "nT")
        dve.tensor_copy(k.nT[:, :], b[:, 0:128]).then_inc(free, 1)

        def conv(f):
            drained(dve, k, ("up", f, 1))
            if f >= 2:
                dve.wait_ge(k.xc_ready, f - 1)
            row = k.xrow[:, f, :]
            out = convt[:, f % 2, 0:RUN]
            st.then(dve.tensor_scalar(out, row[:, 0:RUN], k.vecs1[:, f:f + 1], k.vecs1[:, 64 + f:65 + f], ALU.mult, ALU.add))
            for j in range(1, 4):
                m = dve.scalar_tensor_tensor(out=out, in0=row[:, j:j + RUN], scalar=k.vecs1[:, 16 * j + f:16 * j + f + 1],
                                             in1=out, op0=ALU.mult, op1=ALU.add)
                if j < 3:
                    st.then(m)
                else:
                    m.then_inc(k.conv_ready, 1)

        def gate_weights(r):
            for m3 in range(3):
                b, free = full_bank(dve, k, ("bdt", r, m3))
                dve.tensor_copy(bdt[:, m3, :, :], b.rearrange("p (g c) -> p g c", c=128)).then_inc(free, 1)
            b, free = full_bank(dve, k, ("wc", r))
            for part in range(2):
                src = b[:, 32 * part:32 * part + 32].rearrange("p (g j) -> p g j", j=8)
                rows = wc[:, FT * part + q4 * r:FT * part + q4 * r + q4, :]
                dve.tensor_copy(rows[:, :, 0:4], src[:, :, 0:4])
                m = dve.tensor_copy(rows[:, :, 32:36], src[:, :, 4:8])
            m.then_inc(free, 1)
        for f in range(FT):
            conv(f)
        for r in range(4):
            gate_weights(r)
        dve.wait_ge(k.bif_here, 32)
        for hf, (t0, t1) in enumerate(HALF):
            b, free = full_bank(dve, k, ("gate", hf))
            dve.tensor_scalar(k.gates[:, 0, t0:t1], b[0:4, 0:t1 - t0], k.bif[0:4, :], None, ALU.add)
            dve.tensor_scalar(k.gates[:, 1, t0:t1], b[32:36, 0:t1 - t0], k.bif[32:36, :], None, ALU.add).then_inc(free, 1)
        dve.tensor_copy(k.xms[:, :, :].rearrange("p f (b i) -> p f b i", i=SI), k.xs[:, :, :, 3:7])
        dve.tensor_copy(tails[:, :, 0:3], k.xp[:, :, T:T + 3]).then_inc(k.tails_ready, 1)
        dve.tensor_copy(tails[:, :, 3:27].rearrange("p f (b j) -> p f b j", j=3), k.xs[:, :, :, 4:7]).then_inc(k.tails_ready, 1)
        for r in range(4):
            b, free = full_bank(dve, k, ("tail", r))
            dve.tensor_copy(tail_rows[:, 512 * r:512 * r + 512], b[0:27, :]).then_inc(free, 1)


def stage_gates(nc, k, ctx):
    def sb(name, shape, dt=F32):
        return ctx.enter_context(nc.sbuf_tensor(name, shape, dt))
    e = sb("e", [AH, TA])
    b_sum = sb("b_sum", [AH, TA])
    a_max = sb("a_max", [AH, TA])
    m_tok = sb("m_tok", [AH, TA])
    rows = sb("rows", [96, TA])
    dif = sb("dif", [AH, TA])
    block = ctx.enter_context(nc.Block())
    ig, fg = k.gates[:, 0, :], k.gates[:, 1, :]

    def per_seq(t):
        return t.rearrange("p (b i) -> p b i", i=SI)

    @block.tensor
    def _(pe):
        pe.wait_ge(k.rows_ready, 1)
        pe.wait_ge(k.wrow_ready, 3)
        b, full = open_bank(pe, k, "cols")
        for i in range(NT + 1):
            n = 128 if i < NT else S
            m = pe.transpose(b[0:n, 96 * i:96 * i + 96], rows[:, 128 * i:128 * i + n], k.ident[0:96, 0:96])
        m.then_inc(full, 1)

    @block.vector
    def _(dve):
        st = Steps(dve, k.dve_step, k, "dve")
        st.then(dve.memset(rows[:, :], 0.0))
        dve.scalar_tensor_tensor(out=e[:, :], in0=fg, scalar=-1.0, in1=fg, op0=ALU.mult, op1=ALU.max).then_inc(k.absf_ready, 1)
        dve.wait_ge(k.softplus_ready, 2)
        st.then(dve.scalar_tensor_tensor(out=fg, in0=fg, scalar=0.0, in1=e[:, :], op0=ALU.min, op1=ALU.subtract))
        st.then(dve.tensor_tensor_scan(b_sum[:, :], k.scan_mul[:, :], fg, 0.0, ALU.mult, ALU.add))
        st.then(dve.tensor_tensor(ig, ig, b_sum[:, :], ALU.subtract))
        dve.tensor_copy(rows[0:AH, :], ig)
        st.then(dve.tensor_copy(e[:, :], ig))
        starts = per_seq(e[:, T:TA])[:, :, 0]
        dve.wait_ge(k.m0_here, 16)
        st.then(dve.tensor_tensor(starts, starts, k.m0[:, :], ALU.max))
        st.then(dve.tensor_tensor_scan(a_max[:, :], k.scan_add[:, :], e[:, :], NEG, ALU.add, ALU.max))
        dve.tensor_scalar(k.brow[:, 0:TA], a_max[:, :], -1.0, None, ALU.mult)
        last = per_seq(a_max[:, T:TA])[:, :, SI - 1]
        dve.tensor_tensor(per_seq(k.brow[:, TA:TA + S]), k.m0[:, :].unsqueeze(2).to_broadcast([AH, SB, SI]),
                          per_seq(a_max[:, T:TA]), ALU.subtract)
        dve.tensor_tensor(k.brow[:, TA + S:TA + S + SB], k.m0[:, :], last, ALU.subtract)
        dve.tensor_scalar(dif[:, 0:T], ig[:, 0:T], a_max[:, T - 1:T], None, ALU.subtract)
        dve.tensor_tensor(per_seq(dif[:, T:TA]), per_seq(ig[:, T:TA]), last.unsqueeze(2).to_broadcast([AH, SB, SI]), ALU.subtract)
        dve.tensor_tensor(m_tok[:, :], b_sum[:, :], a_max[:, :], ALU.add).then_inc(k.rows_ready, 1)
        b, free = full_bank(dve, k, "cols")
        dve.tensor_copy(k.cols[:, 0:NT, :], b[:, 0:96 * NT].rearrange("p (i c) -> p i c", c=96))
        dve.tensor_copy(k.cols[0:S, NT, :], b[0:S, 96 * NT:96 * NT + 96]).then_inc(free, 1)

    @block.scalar
    def _(act):
        act.wait_ge(k.absf_ready, 1)
        act.activation(e[:, :], e[:, :], ACT.Exp, scale=-1.0).then_inc(k.softplus_ready, 1)
        act.wait_ge(k.softplus_ready, 1)
        act.activation(e[:, :], e[:, :], ACT.Ln, bias=1.0).then_inc(k.softplus_ready, 1)
        act.wait_ge(k.rows_ready, 1)
        act.activation(k.brow[:, TA:TA + S + SB], k.brow[:, TA:TA + S + SB], ACT.Exp).then_inc(k.wrow_ready, 1)
        act.activation(rows[32:36, :], m_tok[:, :], ACT.Exp, scale=-1.0).then_inc(k.wrow_ready, 1)
        act.activation(rows[64:68, :], dif[:, :], ACT.Exp).then_inc(k.wrow_ready, 1)

    @block.sync
    def _(sp):
        sp.wait_ge(k.rows_ready, 1)
        sp.dma_start(k.o_mp[0, 0].unsqueeze(1), m_tok[:, T - 1:T]).then_inc(k.stored_m, 16)
        sp.dma_start(k.o_ms[0].rearrange("b h -> h b"), per_seq(m_tok[:, T:TA])[:, :, SI - 1],
                     allow_slow_non_contiguous=True).then_inc(k.stored_m, 16)
        sp.wait_ge(k.stored_m, 32)


COL_A, COL_EM, COL_W = 0, 32, 64
NCS = 3


def stage_cell(nc, k, ctx):
    def sb(name, shape, dt=F32):
        return ctx.enter_context(nc.sbuf_tensor(name, shape, dt))
    qT = sb("qT", [128, HF, TA])
    kT = sb("kT", [128, HF, TA])
    kw = sb("kw", [128, NT + 1, AD])
    vt = sb("vt", [128, NT + 1, AD])
    nb = sb("nb", [128, T])
    nbw = sb("nbw", [128, 2 * S + SB])
    nbd = sb("nbd", [128, NT, 128])
    nbds = sb("nbds", [S, S])
    num4 = sb("num4", [128, AD])
    qw = sb("qw", [128, HF, S])
    qm = sb("qm", [128, HF, SB, S])
    prod = sb("prod", [128, HF, S])
    pS = sb("pS", [S, S])
    kwm = sb("kwm", [S, 2, AD])
    cst = sb("cst", [128, 2, AD])
    nP = sb("nP", [128, AH * HF])
    stat = sb("stat", [128, NT, 6])
    mv = sb("mv", [128, NT, 2])
    rr = sb("rr", [128, 4, NT])
    ntmp = sb("ntmp", [128, HF, SB])
    nrows = sb("nrows", [128, 128])
    nprow = sb("nprow", [AH * HF, 128])
    flat = k.wring[:, :, :].rearrange("p a b -> p (a b)")
    cs = flat[:, 0:NCS * HF * AD].rearrange("p (s f e) -> p s f e", s=NCS, f=HF)
    P = flat[:, NCS * HF * AD:(NCS + 1) * HF * AD].rearrange("p (j t) -> p j t", j=NT)
    acc = k.ps[:, NRING]
    block = ctx.enter_context(nc.Block())
    KSCALE = float(AD) ** -0.5

    def hn_of(h):
        return k.xrow[:, HF * h:HF * h + HF, :].rearrange("p f x -> p (f x)")[:, 0:NT * AD].rearrange("p (i e) -> p i e", i=NT)

    def nT_of(t, h):
        return t[:, :].rearrange("p (b h f) -> p h f b", b=SB, h=AH)[:, h]

    def tok(t, f, i):
        return t[:, f, 128 * i:128 * i + 128] if i < NT else t[:, f, T:TA]

    @block.tensor
    def _(pe):
        for h in range(AH):
            b, full = open_bank(pe, k, ("nm", h))
            pe.matmul(b[:, 0:T], k.headsel[:, h, :], k.brow[:, 0:T], start=True, stop=True).then_inc(full, 1)
            b, full = open_bank(pe, k, ("nw", h))
            pe.matmul(b[:, 0:2 * S + SB], k.headsel[:, h, :], k.brow[:, T:TA + S + SB], start=True, stop=True).then_inc(full, 1)
            pe.wait_ge(k.bd_ready, 12 + 3 * h + 3)
            for m3 in range(2):
                for ft in range(HF):
                    for hf, (t0, t1) in enumerate(HALF):
                        b, full = open_bank(pe, k, ("qk", h, m3, ft, hf))
                        pe.matmul(b[:, 0:t1 - t0], k.bd[:, m3, ft, :], k.xcT[:, HF * h + ft, t0:t1],
                                  start=True, stop=True).then_inc(full, 1)
            for i in range(NT + 1):
                n = 128 if i < NT else S
                b, full = open_bank(pe, k, ("ktok", h, i))
                for ft in range(HF):
                    m = pe.matmul(b[0:n, 128 * ft:128 * ft + 128], tok(k.xcT, HF * h + ft, i), k.bd[:, 1, ft, :],
                                  start=True, stop=True)
                m.then_inc(full, 1)
            for i in range(NT + 1):
                n = 128 if i < NT else S
                b, full = open_bank(pe, k, ("vtok", h, i))
                for ft in range(HF):
                    f = HF * h + ft
                    x = k.xp[:, f, 3 + 128 * i:131 + 128 * i] if i < NT else k.xms[:, f, :]
                    m = pe.matmul(b[0:n, 128 * ft:128 * ft + 128], x, k.bd[:, 2, ft, :], start=True, stop=True)
                m.then_inc(full, 1)
            drained(pe, k, ("qk", h, 1, HF - 1, 1))
            for j in range(NT):
                b, full = open_bank(pe, k, ("S", h, j))
                for ft in range(HF):
                    m = pe.matmul(b[:, 128 * j:T], kT[:, ft, 128 * j:128 * j + 128], qT[:, ft, 128 * j:T],
                                  start=ft == 0, stop=ft == HF - 1)
                m.then_inc(full, 1)
            b, full = open_bank(pe, k, ("Ss", h))
            for ft in range(HF):
                m = pe.matmul(b[0:S, 0:S], kT[:, ft, T:TA], qT[:, ft, T:TA], start=ft == 0, stop=ft == HF - 1)
            m.then_inc(full, 1)
            drained(pe, k, ("ktok", h, NT))
            drained(pe, k, ("vtok", h, NT))
            for ft in range(HF):
                b, full = open_bank(pe, k, ("Cp", h, ft))
                for j in range(NT):
                    m = pe.matmul(b[:, :], kw[:, j, 128 * ft:128 * ft + 128], vt[:, j, :], start=j == 0, stop=j == NT - 1)
                m.then_inc(full, 1)
            b, full = open_bank(pe, k, ("nn", h))
            for ft in range(HF):
                for j in range(NT):
                    pe.matmul(b[:, 9 * ft:9 * ft + 1], kw[:, j, 128 * ft:128 * ft + 128], k.ones[:, 0:1],
                              start=j == 0, stop=j == NT - 1)
                m = pe.matmul(b[:, 9 * ft + 1:9 * ft + 9], kw[0:S, NT, 128 * ft:128 * ft + 128], k.tmask[:, :],
                              start=True, stop=True)
            m.then_inc(full, 1)
            pe.wait_ge(k.p_ready, 5 * h + 4)
            b, full = open_bank(pe, k, ("den", h))
            for i in range(NT):
                for j in range(i + 1):
                    m = pe.matmul(b[:, i:i + 1], P[:, j, 128 * i:128 * i + 128], k.ones[:, 0:1], start=j == 0, stop=j == i)
            m.then_inc(full, 1)
            for i in range(NT):
                b, full = open_bank(pe, k, ("num", h, i))
                for j in range(i + 1):
                    m = pe.matmul(b[:, :], P[:, j, 128 * i:128 * i + 128], vt[:, j, :], start=j == 0, stop=j == i)
                m.then_inc(full, 1)
            pe.wait_ge(k.qm_ready, HF * (h + 1))
            if h:
                pe.wait_ge(k.acc_free, h)
            for s in range(SB):
                u = SB * h + s
                pe.wait_ge(k.c_here[u % NCS], 16 * (u // NCS + 1))
                for ft in range(HF):
                    m = pe.matmul(acc[32 * ft:32 * ft + 32, :], qm[:, ft, s, :], cs[:, u % NCS, ft, :],
                                  start=s == 0, stop=s == SB - 1)
                if s == SB - 1:
                    m.then_inc(k.acc_full, 1)
                pe.wait_ge(k.kwm_ready, u + 1)
                for ft in range(HF):
                    b, full = open_bank(pe, k, ("up", h, s, ft))
                    pe.matmul(b[:, :], kwm[:, s % 2, 128 * ft:128 * ft + 128], vt[0:S, NT, :],
                              start=True, stop=True).then_inc(full, 1)
            for i in range(NT):
                pe.wait_ge(k.hn_ready, (NT + 1) * h + i + 1)
                b, full = open_bank(pe, k, ("tr", h, i))
                for ft in range(HF):
                    m = pe.transpose(b[:, 128 * ft:128 * ft + 128], hn_of(h)[:, i, 128 * ft:128 * ft + 128], k.ident[:, :])
                m.then_inc(full, 1)
            pe.wait_ge(k.num4_ready, h + 1)
            b, full = open_bank(pe, k, ("nums", h))
            pe.matmul(b[0:S, :], k.fold[:, :], num4[:, :], start=True, stop=False)
            pe.wait_ge(k.p_ready, 5 * h + 5)
            pe.matmul(b[0:S, :], pS[:, :], vt[0:S, NT, :], start=False, stop=True).then_inc(full, 1)
            pe.wait_ge(k.prod_ready, h + 1)
            b, full = open_bank(pe, k, ("dens", h))
            for ft in range(HF):
                pe.matmul(b[0:S, 0:1], prod[:, ft, :], k.ones[:, 0:1], start=ft == 0, stop=False)
            pe.matmul(b[0:S, 0:1], pS[:, :], k.ones[0:S, 0:1], start=False, stop=True).then_inc(full, 1)
            pe.wait_ge(k.hn_ready, (NT + 1) * (h + 1))
            b, full = open_bank(pe, k, ("tr", h, NT))
            for ft in range(HF):
                m = pe.transpose(b[:, S * ft:S * ft + S], hn_of(h)[0:S, 0, 128 * ft:128 * ft + 128], k.ident[0:S, 0:S])
            m.then_inc(full, 1)
        pe.wait_ge(k.n_ready, AH)
        b, full = open_bank(pe, k, "nrows")
        pe.transpose(b[:, 0:128], k.nT[:, :], k.ident[:, :])
        pe.transpose(b[0:16, 128:256], nP[:, :], k.ident[:, :]).then_inc(full, 1)

    @block.sync
    def _(sp):
        for u in range(AH * SB):
            h, s = u // SB, u % SB
            if u >= NCS:
                sp.wait_ge(k.c_stored[u % NCS], 16 * (u // NCS))
            sp.dma_start(cs[:, u % NCS, :, :], k.state_C[s, h].rearrange("(f p) e -> p f e", p=128)).then_inc(k.c_here[u % NCS], 16)

    @block.gpsimd
    def _(pool):
        def store_state(u):
            pool.wait_ge(k.c_updated, HF * (u + 1))
            pool.dma_start(k.o_cs[0, u % SB, u // SB].rearrange("(f p) e -> p f e", p=128),
                           cs[:, u % NCS, :, :]).then_inc(k.c_stored[u % NCS], 16)
        for h in range(AH):
            if h:
                bank, n = k.bank_of[("vtok", h - 1, NT)]
                pool.wait_ge(k.bank_full[bank], n)
            head_blocks(pool, k, h)
            drained(pool, k, ("nw", h))
            pool.tensor_tensor(nbd[:, :, :], nb[:, :].rearrange("p (j t) -> p j t", j=NT),
                               k.maskT[:, :].unsqueeze(1).to_broadcast([128, NT, 128]), ALU.add).then_inc(k.nbd_ready, 1)
            pool.tensor_tensor(nbds[:, :], nbw[0:S, 0:S], k.maskS[:, :], ALU.add).then_inc(k.nbd_ready, 1)
            pool.wait_ge(k.qw_ready, h + 1)
            for ft in range(HF):
                pool.tensor_tensor(qm[:, ft, :, :], qw[:, ft, :].unsqueeze(1).to_broadcast([128, SB, S]),
                                   k.bmask[:, :, :], ALU.mult).then_inc(k.qm_ready, 1)
            drained(pool, k, ("ktok", h, NT))
            for ft in range(HF):
                f = HF * h + ft
                pool.tensor_scalar(k.xcT[:, f, :], k.xcT[:, f, :], k.vecs1[:, 96 + f:97 + f], None, ALU.mult).then_inc(k.skip_ready, 1)
            for ft in range(HF):
                pool.wait_ge(k.cst_ready, HF * h + ft + 1)
                pool.dma_start(k.o_cp[0, 0, h, 128 * ft:128 * ft + 128, :], cst[:, ft % 2, :]).then_inc(k.cst_stored[ft % 2], 16)
            for s in range(SB):
                u = SB * h + s
                if u >= 2:
                    bank, n = k.bank_of[("up", (u - 2) // SB, (u - 2) % SB, HF - 1)]
                    pool.wait_ge(k.bank_full[bank], n)
                pool.tensor_scalar(kwm[:, s % 2, :], kw[0:S, NT, :], k.tmask[:, s:s + 1], None, ALU.mult).then_inc(k.kwm_ready, 1)
                if s:
                    store_state(u - 1)
            store_state(SB * h + SB - 1)
        drained(pool, k, "nrows")
        pool.dma_start(k.o_ns[0].rearrange("b h (f p) -> (b h f) p", p=128), nrows[:, :]).then_inc(k.stored_n, 16)
        pool.dma_start(k.o_np[0, 0].rearrange("h (f p) -> (h f) p", p=128), nprow[:, :]).then_inc(k.stored_n, 16)
        pool.wait_ge(k.stored_n, 32)
        for c in range(NCS):
            pool.wait_ge(k.c_stored[c], 16 * ((AH * SB - c + NCS - 1) // NCS))
        for c in range(2):
            pool.wait_ge(k.cst_stored[c], 16 * 2 * AH)

    @block.scalar
    def _(act):
        for h in range(AH):
            for m3, dst in ((0, qT), (1, kT)):
                for ft in range(HF):
                    for hf, (t0, t1) in enumerate(HALF):
                        b, free = full_bank(act, k, ("qk", h, m3, ft, hf))
                        act.activation(dst[:, ft, t0:t1], b[:, 0:t1 - t0], ACT.Copy, scale=1.0 if m3 == 0 else KSCALE).then_inc(free, 1)
            for i in range(NT + 1):
                n = 128 if i < NT else S
                b, free = full_bank(act, k, ("vtok", h, i))
                act.activation(vt[0:n, i, :], b[0:n, :], ACT.Copy).then_inc(free, 1)
            act.wait_ge(k.nbd_ready, 2 * h + 2)
            for j in range(NT):
                a = k.cols[:, j, COL_A + h:COL_A + h + 1]
                m = act.activation(P[:, j, 128 * j:128 * j + 128], nbd[:, j, :], ACT.Exp, bias=a)
                if j < NT - 1:
                    m = act.activation(P[:, j, 128 * j + 128:T], nb[:, 128 * j + 128:T], ACT.Exp, bias=a)
                m.then_inc(k.w_ready, 1)
            act.activation(pS[:, :], nbds[:, :], ACT.Exp, bias=k.cols[0:S, NT, COL_A + h:COL_A + h + 1]).then_inc(k.w_ready, 1)
            for ft in range(HF):
                b, free = full_bank(act, k, ("Cp", h, ft))
                c = 2 * h + ft // 2
                if c:
                    act.wait_ge(k.cst_stored[ft % 2], 16 * c)
                act.activation(cst[:, ft % 2, :], b[:, :], ACT.Copy).then_inc(free, 1)
                drained(act, k, ("Cp", h, ft))
                act.sem_inc(k.cst_ready, 1)
            act.wait_ge(k.var_ready, 2 * h + 1)
            act.activation(rr[:, 2, :], rr[:, 1, :], ACT.Sqrt).then_inc(k.sd_ready, 1)
            act.wait_ge(k.acc_full, h + 1)
            act.activation(num4[:, :], acc[:, :], ACT.Copy).then_inc(k.acc_free, 1)
            act.wait_ge(k.acc_free, h + 1)
            act.sem_inc(k.num4_ready, 1)
            act.wait_ge(k.var_ready, 2 * h + 2)
            act.activation(rr[0:S, 2, 0:1], rr[0:S, 1, 0:1], ACT.Sqrt).then_inc(k.sd_ready, 1)

    @block.vector
    def _(dve):
        st = Steps(dve, k.dve_step, k, "dve")
        for h in range(AH):
            b, free = full_bank(dve, k, ("nm", h))
            dve.tensor_copy(nb[:, :], b[:, :]).then_inc(free, 1)
            b, free = full_bank(dve, k, ("nw", h))
            dve.tensor_copy(nbw[:, :], b[:, 0:2 * S + SB]).then_inc(free, 1)
            drained(dve, k, ("nw", h))
            drained(dve, k, ("qk", h, 0, HF - 1, 1))
            st.then(dve.tensor_tensor(qw[:, :, :], qT[:, :, T:TA], nbw[:, S:2 * S].unsqueeze(1).to_broadcast([128, HF, S]), ALU.mult))
            dve.sem_inc(k.qw_ready, 1)
            dve.tensor_tensor(prod[:, :, :].rearrange("p f (b i) -> p f b i", i=SI),
                              qw[:, :, :].rearrange("p f (b i) -> p f b i", i=SI),
                              nT_of(k.nT, h).unsqueeze(3).to_broadcast([128, HF, SB, SI]), ALU.mult).then_inc(k.prod_ready, 1)
            for i in range(NT + 1):
                n = 128 if i < NT else S
                b, free = full_bank(dve, k, ("ktok", h, i))
                dve.tensor_scalar(kw[0:n, i, :], b[0:n, :], KSCALE, k.cols[0:n, i, COL_W + h:COL_W + h + 1],
                                  ALU.mult, ALU.mult).then_inc(free, 1)
            for j in range(NT):
                dve.wait_ge(k.w_ready, 5 * h + j + 1)
                b, free = full_bank(dve, k, ("S", h, j))
                st.then(dve.tensor_tensor(P[:, j, 128 * j:T], P[:, j, 128 * j:T], b[:, 128 * j:T], ALU.mult))
                dve.sem_inc(free, 1)
                dve.sem_inc(k.p_ready, 1)
            dve.wait_ge(k.w_ready, 5 * h + 5)
            b, free = full_bank(dve, k, ("Ss", h))
            st.then(dve.tensor_tensor(pS[:, :], pS[:, :], b[0:S, 0:S], ALU.mult))
            dve.sem_inc(free, 1)
            dve.sem_inc(k.p_ready, 1)
            b, free = full_bank(dve, k, ("nn", h))
            nn = b[:, 0:9 * HF].rearrange("p (f c) -> p f c", c=9)
            dve.tensor_copy(nP[:, HF * h:HF * h + HF], nn[:, :, 0])
            dve.wait_ge(k.prod_ready, h + 1)
            st.then(dve.tensor_tensor(ntmp[:, :, :], nT_of(k.nT, h), nbw[:, 2 * S:2 * S + SB].unsqueeze(1).to_broadcast([128, HF, SB]), ALU.mult))
            st.then(dve.tensor_tensor(nT_of(k.nT, h), ntmp[:, :, :], nn[:, :, 1:9], ALU.add))
            dve.sem_inc(free, 1)
            dve.sem_inc(k.n_ready, 1)
            em = k.cols[:, 0:NT, COL_EM + h]
            b, free = full_bank(dve, k, ("den", h))
            st.then(dve.tensor_scalar(rr[:, 0, :], b[:, 0:NT], -1.0, None, ALU.mult))
            st.then(dve.tensor_tensor(rr[:, 0, :], rr[:, 0, :], b[:, 0:NT], ALU.max))
            dve.sem_inc(free, 1)
            st.then(dve.tensor_tensor(rr[:, 0, :], rr[:, 0, :], em, ALU.max))
            st.then(dve.reciprocal(rr[:, 0, :], rr[:, 0, :]))
            for i in range(NT):
                b, free = full_bank(dve, k, ("num", h, i))
                st.then(dve.bn_stats(stat[:, i, :], b[:, :]))
                st.then(dve.bn_aggr(mv[:, i, :], stat[:, i, :]))
            st.then(dve.tensor_tensor(rr[:, 1, :], mv[:, :, 1], rr[:, 0, :], ALU.mult))
            st.then(dve.tensor_tensor(rr[:, 1, :], rr[:, 1, :], rr[:, 0, :], ALU.mult))
            dve.tensor_scalar(rr[:, 1, :], rr[:, 1, :], EPS, None, ALU.add).then_inc(k.var_ready, 1)
            dve.wait_ge(k.sd_ready, 2 * h + 1)
            st.then(dve.reciprocal(rr[:, 2, :], rr[:, 2, :]))
            st.then(dve.tensor_tensor(rr[:, 3, :], rr[:, 2, :], rr[:, 0, :], ALU.mult))
            for i in range(NT):
                b, free = full_bank(dve, k, ("num", h, i))
                st.then(dve.tensor_scalar(hn_of(h)[:, i, :], b[:, :], mv[:, i, 0:1], rr[:, 3, i:i + 1], ALU.subtract, ALU.mult))
                dve.sem_inc(free, 1)
                dve.sem_inc(k.hn_ready, 1)
            for s in range(SB):
                u = SB * h + s
                for ft in range(HF):
                    b, free = full_bank(dve, k, ("up", h, s, ft))
                    c = cs[:, u % NCS, ft, :]
                    st.then(dve.scalar_tensor_tensor(out=c, in0=c, scalar=nbw[:, 2 * S + s:2 * S + s + 1], in1=b[:, :],
                                                     op0=ALU.mult, op1=ALU.add))
                    dve.sem_inc(free, 1)
                    dve.sem_inc(k.c_updated, 1)
            dve.wait_ge(k.skip_ready, HF * (h + 1))

            def mix(i):
                n = 128 if i < NT else S
                b, free = full_bank(dve, k, ("tr", h, i))
                for ft in range(HF):
                    f = HF * h + ft
                    m = dve.scalar_tensor_tensor(out=tok(k.xcT, f, i), in0=b[:, n * ft:n * ft + n], scalar=k.vecs1[:, 80 + f:81 + f],
                                                 in1=tok(k.xcT, f, i), op0=ALU.mult, op1=ALU.add)
                m.then_inc(free, 1)
            for i in range(NT):
                mix(i)
            b, free = full_bank(dve, k, ("nums", h))
            st.then(dve.bn_stats(stat[0:S, 0, :], b[0:S, :]))
            st.then(dve.bn_aggr(mv[0:S, 0, :], stat[0:S, 0, :]))
            bd, freed = full_bank(dve, k, ("dens", h))
            st.then(dve.tensor_scalar(rr[0:S, 0, 0:1], bd[0:S, 0:1], -1.0, k.cols[0:S, NT, COL_EM + h:COL_EM + h + 1], ALU.mult, ALU.max))
            st.then(dve.tensor_tensor(rr[0:S, 0, 0:1], rr[0:S, 0, 0:1], bd[0:S, 0:1], ALU.max))
            dve.sem_inc(freed, 1)
            st.then(dve.reciprocal(rr[0:S, 0, 0:1], rr[0:S, 0, 0:1]))
            st.then(dve.tensor_tensor(rr[0:S, 1, 0:1], mv[0:S, 0, 1:2], rr[0:S, 0, 0:1], ALU.mult))
            st.then(dve.tensor_tensor(rr[0:S, 1, 0:1], rr[0:S, 1, 0:1], rr[0:S, 0, 0:1], ALU.mult))
            dve.tensor_scalar(rr[0:S, 1, 0:1], rr[0:S, 1, 0:1], EPS, None, ALU.add).then_inc(k.var_ready, 1)
            dve.wait_ge(k.sd_ready, 2 * h + 2)
            st.then(dve.reciprocal(rr[0:S, 2, 0:1], rr[0:S, 2, 0:1]))
            st.then(dve.tensor_tensor(rr[0:S, 3, 0:1], rr[0:S, 2, 0:1], rr[0:S, 0, 0:1], ALU.mult))
            st.then(dve.tensor_scalar(hn_of(h)[0:S, 0, :], b[0:S, :], mv[0:S, 0, 0:1], rr[0:S, 3, 0:1], ALU.subtract, ALU.mult))
            dve.sem_inc(free, 1)
            dve.sem_inc(k.hn_ready, 1)
            mix(NT)
        b, free = full_bank(dve, k, "nrows")
        dve.tensor_copy(nrows[:, :], b[:, 0:128])
        dve.tensor_copy(nprow[:, :], b[0:16, 128:256]).then_inc(free, 1)


def stage_gate(nc, k, ctx):
    zt = ctx.enter_context(nc.sbuf_tensor("zt", [128, 4, 288], F32))
    block = ctx.enter_context(nc.Block())

    @block.tensor
    def _(pe):
        for c in range(4, 8):
            w = chunk(pe, k, CH_UP + c)
            for m4 in range(4):
                f = 4 * (c - 4) + m4
                for hf, (t0, t1) in enumerate(HALF):
                    b, full = open_bank(pe, k, ("z", f, hf))
                    for kt in range(KD):
                        m = pe.matmul(b[:, 0:t1 - t0], w[:, kt, 128 * m4:128 * m4 + 128], k.xnT[:, kt, t0:t1],
                                      start=kt == 0, stop=kt == KD - 1)
                    m.then_inc(full, 1)
            k.chunk_last[CH_UP + c] = k.bank_of[("z", f, 1)]

    @block.sync
    def _(sp):
        load_chunks(sp, k, CH_UP + 4, CH_DOWN + NW)

    @block.scalar
    def _(act):
        for u in range(2 * FT):
            f, hf = u // 2, u % 2
            n = HALF[hf][1] - HALF[hf][0]
            b, free = full_bank(act, k, ("z", f, hf))
            if u >= 4:
                act.wait_ge(k.gated, u - 3)
            act.activation(zt[:, u % 4, 0:n], b[:, 0:n], ACT.Silu).then_inc(free, 1)

    @block.vector
    def _(dve):
        for u in range(2 * FT):
            f, hf = u // 2, u % 2
            t0, t1 = HALF[hf]
            drained(dve, k, ("z", f, hf))
            dve.tensor_tensor(k.xcT[:, f, t0:t1], k.xcT[:, f, t0:t1], zt[:, u % 4, 0:t1 - t0], ALU.mult).then_inc(k.gated, 1)


def project_rows(pe, k, key, xT, c0, halves):
    banks = []
    for i in range(NT + 1):
        banks.append(open_bank(pe, k, (key, i)))
    for half in range(halves):
        w = chunk(pe, k, c0 + half)
        for i in range(NT + 1):
            n = 128 if i < NT else S
            b, full = banks[i]
            for kt in range(8):
                m = pe.matmul(b[0:n, 0:w.shape[2]], xT[:, 8 * half + kt, 128 * i:128 * i + n], w[:, kt, :],
                              start=half == 0 and kt == 0, stop=half == halves - 1 and kt == 7)
            if half == halves - 1:
                m.then_inc(full, 1)
        if half < halves - 1:
            m.then_inc(k.half_done, 1)
            k.halves += 1
            k.chunk_last[c0 + half] = ("half", k.halves)
        else:
            k.chunk_last[c0 + half] = k.bank_of[(key, NT)]


def norm_residual(k, dve, st, y, xr, npost, rstd, i):
    r = 128 if i < NT else S
    st.then(dve.scalar_tensor_tensor(out=y[0:r, i, :], in0=y[0:r, i, :], scalar=rstd[0:r, i:i + 1], in1=npost[0:r, :],
                                     op0=ALU.mult, op1=ALU.mult))
    st.then(dve.tensor_tensor(xr[0:r, i, :], xr[0:r, i, :], y[0:r, i, :], ALU.add))
    dve.sem_inc(k.res_ready, 1)


def row_rms(dve, st, k, ssq, rstd):
    dve.tensor_scalar(ssq[:, :], ssq[:, :], 1.0 / D, EPS, ALU.mult, ALU.add).then_inc(k.ms_ready, 1)
    k.rms += 1
    dve.wait_ge(k.std_ready, k.rms)
    st.then(dve.reciprocal(rstd[:, :], rstd[:, :]))


def stage_down(nc, k, ctx):
    def sb(name, shape, dt=F32):
        return ctx.enter_context(nc.sbuf_tensor(name, shape, dt))
    y = sb("y_down", [128, NT + 1, D])
    npost = sb("npost", [128, D])
    sq = sb("sq2", [128, D])
    ssq = sb("ssq2", [128, NT + 1])
    rstd = sb("rstd2", [128, NT + 1])
    x1 = k.x1
    block = ctx.enter_context(nc.Block())
    DK = D // 512
    k.rms = 1

    @block.tensor
    def _(pe):
        for n in range(DK):
            project_rows(pe, k, ("down", n), k.xcT, CH_DOWN + 2 * n, 2)
        pe.wait_ge(k.xn_tok, 2 * (NT + 1))
        for kt in range(KD):
            b, full = open_bank(pe, k, ("x1T", kt))
            for i in range(NT):
                m = pe.transpose(b[:, 128 * i:128 * i + 128], y[:, i, 128 * kt:128 * kt + 128], k.ident[:, :])
            m.then_inc(full, 1)
        b, full = open_bank(pe, k, "x1Ts")
        for kt in range(KD):
            m = pe.transpose(b[:, S * kt:S * kt + S], y[0:S, NT, 128 * kt:128 * kt + 128], k.ident[0:S, 0:S])
        m.then_inc(full, 1)

    @block.sync
    def _(sp):
        sp.dma_start(x1[:, 0:NT, :], k.x_prompt[0].rearrange("(i p) d -> p i d", p=128)).then_inc(k.x_here, 16)
        sp.dma_start(x1[0:S, NT, :], k.x_sample.rearrange("b i d -> (b i) d")).then_inc(k.x_here, 16)
        sp.dma_start(npost[:, :], k.a_norm_post.partition_broadcast(128)).then_inc(k.x_here, 16)
        load_chunks(sp, k, CH_DOWN + NW, CH_KV + NW)
        sp.wait_ge(k.res_ready, NT + 1)
        sp.dma_start(k.o_yp[0].rearrange("(i p) d -> p i d", p=128), x1[:, 0:NT, :]).then_inc(k.stored_x1, 16)
        sp.dma_start(k.o_ys.rearrange("b i d -> (b i) d"), x1[0:S, NT, :]).then_inc(k.stored_x1, 16)
        sp.wait_ge(k.stored_x1, 32)

    @block.scalar
    def _(act):
        for n in range(DK):
            for i in range(NT + 1):
                r = 128 if i < NT else S
                b, free = full_bank(act, k, (("down", n), i))
                act.activation(y[0:r, i, 512 * n:512 * n + 512], b[0:r, :], ACT.Copy).then_inc(free, 1)
        act.wait_ge(k.ssq_clear, 2)
        for src, base in ((y, 0), (x1, 1)):
            if base:
                act.wait_ge(k.res_ready, NT + 1)
            for i in range(NT + 1):
                r = 128 if i < NT else S
                if not base:
                    drained(act, k, (("down", 1), i))
                act.activation(sq[0:r, :], src[0:r, i, :], ACT.Square, accum_out=ssq[0:r, i:i + 1]).then_inc(k.ssq_ready, 1)
                act.wait_ge(k.ssq_ready, (NT + 1) * (1 + base) + i + 1)
            act.wait_ge(k.ms_ready, 2 + base)
            act.activation(rstd[:, :], ssq[:, :], ACT.Sqrt).then_inc(k.std_ready, 1)

    @block.vector
    def _(dve):
        st = Steps(dve, k.dve_step, k, "dve")
        dve.memset(ssq[:, :], 1.0).then_inc(k.ssq_clear, 1)
        dve.wait_ge(k.x_here, 32 + 48)
        dve.wait_ge(k.ssq_ready, 2 * (NT + 1))
        row_rms(dve, st, k, ssq, rstd)
        for i in range(NT + 1):
            norm_residual(k, dve, st, y, x1, npost, rstd, i)
        dve.wait_ge(k.ssq_ready, 3 * (NT + 1))
        row_rms(dve, st, k, ssq, rstd)
        for i in range(NT + 1):
            r = 128 if i < NT else S
            dve.tensor_scalar(y[0:r, i, :], x1[0:r, i, :], rstd[0:r, i:i + 1], None, ALU.mult).then_inc(k.xn_tok, 1)
        for kt in range(KD):
            b, free = full_bank(dve, k, ("x1T", kt))
            dve.tensor_scalar(k.kvT[:, kt, 0:T], b[:, 0:T], k.vecs2[:, 8 + kt:9 + kt], None, ALU.mult)
            dve.tensor_scalar(k.xnT[:, kt, 0:T], b[:, 0:T], k.vecs2[:, 16 + kt:17 + kt], None, ALU.mult).then_inc(free, 1)
        b, free = full_bank(dve, k, "x1Ts")
        src = b[:, 0:KD * S].rearrange("p (a b) -> p a b", b=S)
        dve.tensor_tensor(k.kvT[:, :, T:TA], src, k.vecs2[:, 8:16].unsqueeze(2).to_broadcast([128, KD, S]), ALU.mult)
        dve.tensor_tensor(k.xnT[:, :, T:TA], src, k.vecs2[:, 16:24].unsqueeze(2).to_broadcast([128, KD, S]), ALU.mult).then_inc(free, 1)


def stage_kv(nc, k, ctx):
    kvt = ctx.enter_context(nc.sbuf_tensor("kvt", [128, 2, NT + 1, 2 * SLOT], F32))
    block = ctx.enter_context(nc.Block())

    @block.tensor
    def _(pe):
        for c in range(3):
            project_rows(pe, k, ("kv", c), k.kvT, CH_KV + c, 1)
            if c:
                for gp in range(2):
                    b, full = open_bank(pe, k, ("KT", c, gp))
                    for i in range(NT):
                        pe.wait_ge(k.kv_here, (NT + 1) * c + i + 1)
                        m = pe.transpose(b[:, 128 * i:128 * i + 128], kvt[:, c % 2, i, 128 * gp:128 * gp + 128], k.ident[:, :])
                    m.then_inc(full, 1)
                b, full = open_bank(pe, k, ("KTs", c))
                pe.wait_ge(k.kv_here, (NT + 1) * (c + 1))
                for gp in range(2):
                    m = pe.transpose(b[:, S * gp:S * gp + S], kvt[0:S, c % 2, NT, 128 * gp:128 * gp + 128], k.ident[0:S, 0:S])
                m.then_inc(full, 1)

    @block.sync
    def _(sp):
        load_chunks(sp, k, CH_KV + NW, CH_CMP + NW)

    @block.gpsimd
    def _(pool):
        for s in range(SB):
            pool.dma_start(k.o_ws[s, 0:512 - SI].rearrange("t a g d -> t (a g d)"),
                           k.cache_win[s, SI:512].rearrange("t a g d -> t (a g d)")).then_inc(k.stored_win, 16)
        for c in range(3):
            pool.wait_ge(k.kv_here, (NT + 1) * (c + 1))
            if c < 2:
                pool.dma_start(k.o_kvp[0].rearrange("(i p) s g d -> p i (s g d)", p=128)[:, :, 512 * c:512 * c + 512],
                               kvt[:, c % 2, 0:NT, :]).then_inc(k.stored_kv, 16)
                pool.dma_start(k.o_kvs.rearrange("b i s g d -> (b i) (s g d)")[:, 512 * c:512 * c + 512],
                               kvt[0:S, c % 2, NT, :]).then_inc(k.stored_kv, 16)
            else:
                pool.dma_start(k.o_wp[0].rearrange("(i p) s g d -> p i (s g d)", p=128), kvt[:, c % 2, 0:NT, :]).then_inc(k.stored_kv, 16)
                for s in range(SB):
                    pool.dma_start(k.o_ws[s, 512 - SI:512].rearrange("t a g d -> t (a g d)"),
                                   kvt[SI * s:SI * s + SI, c % 2, NT, :]).then_inc(k.stored_kv, 16)
            if c == 0:
                pool.wait_ge(k.stored_kv, 32)
                pool.sem_inc(k.kvt_free, 1)
        pool.wait_ge(k.stored_kv, 16 * (5 + SB))
        pool.wait_ge(k.stored_win, 16 * SB)

    @block.scalar
    def _(act):
        for c in range(3):
            if c == 2:
                act.wait_ge(k.kvt_free, 1)
            for i in range(NT + 1):
                r = 128 if i < NT else S
                b, free = full_bank(act, k, (("kv", c), i))
                act.activation(kvt[0:r, c % 2, i, :], b[0:r, :], ACT.Copy).then_inc(free, 1)
                drained(act, k, (("kv", c), i))
                act.sem_inc(k.kv_here, 1)

    @block.vector
    def _(dve):
        for c in (1, 2):
            for gp in range(2):
                b, free = full_bank(dve, k, ("KT", c, gp))
                dve.tensor_copy(k.KT[:, c - 1, gp, 0:T], b[:, 0:T]).then_inc(free, 1)
            b, free = full_bank(dve, k, ("KTs", c))
            dve.tensor_copy(k.KT[:, c - 1, :, T:TA], b[:, 0:2 * S].rearrange("p (a b) -> p a b", b=S)).then_inc(free, 1)
            for i in range(NT + 1):
                r = 128 if i < NT else S
                dve.wait_ge(k.kv_here, (NT + 1) * c + i + 1)
                dve.tensor_copy(k.V[0:r, c - 1, i, :], kvt[0:r, c % 2, i, SLOT:2 * SLOT])


def stage_compress(nc, k, ctx):
    def sb(name, shape, dt=F32):
        return ctx.enter_context(nc.sbuf_tensor(name, shape, dt))
    NS = SB + 1
    pages = sb("pages", [1, SB * 4], I32)
    raw = sb("craw", [128, 2, 2, 2, 512])
    pair = sb("cpair", [128, 2, 2, G, 2, DH])
    R = sb("cR", [128, 2, G, 256])
    hid = sb("chid", [128, 2, 2, G * NCMP])
    w2 = sb("cw2", [128, 2, 2, DH])
    b2k = sb("cb2k", [128, 1])
    b2v = sb("cb2v", [NCMP, DH])
    posr = sb("posr", [32, 128])
    posT = sb("posT", [128, 32])
    pb = sb("cpb", [128, 4])
    block = ctx.enter_context(nc.Block())

    @block.tensor
    def _(pe):
        w1 = [chunk(pe, k, CH_CMP + s) for s in range(2)]
        pe.wait_ge(k.cw_here, 16 * 6)
        b, full = open_bank(pe, k, "posT")
        pe.transpose(b[:, 0:32], posr[:, :], k.ident[0:32, 0:32]).then_inc(full, 1)
        drained(pe, k, "posT")
        b, full = open_bank(pe, k, "pb")
        for s in range(2):
            for hh in range(2):
                for j in range(16):
                    m = pe.matmul(b[:, 2 * s + hh:2 * s + hh + 1], w1[s][:, j, 128 * hh:128 * hh + 128],
                                  posT[:, 16 * s + j:16 * s + j + 1], start=j == 0, stop=j == 15)
        m.then_inc(full, 1)
        for q in range(NS):
            pe.wait_ge(k.pair_ready, 2 * (q + 1))
            for s in range(2):
                for gp in range(2):
                    b, full = open_bank(pe, k, ("R", q, s, gp))
                    for g in range(2):
                        for j in range(2):
                            m = pe.transpose(b[:, 256 * g + 128 * j:256 * g + 128 * j + 128],
                                             pair[:, j, s, 2 * gp + g, :, :].rearrange("p a d -> p (a d)"), k.ident[:, :])
                    m.then_inc(full, 1)
            for s in range(2):
                drained(pe, k, ("R", q, s, 0))
                drained(pe, k, ("R", q, s, 1))
                b, full = open_bank(pe, k, ("hid", q, s))
                for hh in range(2):
                    for j in range(16):
                        m = pe.matmul(b[:, G * NCMP * hh:G * NCMP * (hh + 1)].rearrange("p (g n) -> p g n", g=G),
                                      w1[s][:, j, 128 * hh:128 * hh + 128],
                                      R[:, s, :, j:j + 8 * (NCMP - 1) + 1:8], start=j == 0, stop=j == 15)
                m.then_inc(full, 1)
            k.chunk_last[CH_CMP], k.chunk_last[CH_CMP + 1] = k.bank_of[("hid", q, 0)], k.bank_of[("hid", q, 1)]
            drained(pe, k, ("hid", q, 1))
            drained(pe, k, ("hid", q, 0))
            b, full = open_bank(pe, k, ("kc", q))
            for g in range(G):
                p0 = 64 * (g % 2)
                for hh in range(2):
                    m = pe.matmul(b[p0:p0 + DH, NCMP * (g // 2):NCMP * (g // 2) + NCMP], w2[:, 0, hh, :],
                                  hid[:, 0, hh, NCMP * g:NCMP * g + NCMP], start=hh == 0, stop=hh == 1)
            m.then_inc(full, 1)
            b, full = open_bank(pe, k, ("vc", q))
            for g in range(G):
                for hh in range(2):
                    m = pe.matmul(b[0:NCMP, DH * g:DH * g + DH], hid[:, 1, hh, NCMP * g:NCMP * g + NCMP], w2[:, 1, hh, :],
                                  start=hh == 0, stop=hh == 1)
            m.then_inc(full, 1)

    @block.sync
    def _(sp):
        sp.dma_start(pages[:, :], k.page_table.rearrange("b p -> (b p)").unsqueeze(0)).then_inc(k.pages_here, 16)
        sp.wait_ge(k.pages_here, 16)
        for q in range(NS):
            if q >= 2:
                sp.wait_ge(k.pair_ready, 2 * (q - 1))
            if q < SB:
                for pg in range(4):
                    page = sp.value_load(pages[0:1, 4 * q + pg:4 * q + pg + 1], min_val=0, max_val=k.cache_kv.shape[0] - 1)
                    src = k.cache_kv[bass.ds(page, 1)].rearrange("o (t a) s g d -> (o t) a (s g d)", a=2)[:, :, 0:512]
                    sp.dma_start(raw[64 * (pg % 2):64 * (pg % 2) + 64, q % 2, pg // 2, :, :], src).then_inc(k.raw_here[q % 2], 16)
            else:
                for j in range(2):
                    src = k.o_kvp[0, 256 * j:256 * j + 256].rearrange("(t a) s g d -> t a (s g d)", a=2)[:, :, 0:512]
                    sp.dma_start(raw[:, q % 2, j, :, :], src).then_inc(k.raw_here[q % 2], 32)
        load_chunks(sp, k, CH_CMP + NW, CH_IN + NW)

    @block.scalar
    def _(act):
        act.dma_start(posr[:, :], k.cmp_pos.rearrange("s (j a) d -> (s j) (a d)", a=2)).then_inc(k.cw_here, 16)
        act.dma_start(w2[:, 0, :, :], k.cmp_w2[0].rearrange("(h p) d -> p h d", p=128)).then_inc(k.cw_here, 16)
        act.dma_start(w2[:, 1, :, :], k.cmp_w2[1].rearrange("(h p) d -> p h d", p=128)).then_inc(k.cw_here, 16)
        act.dma_start(b2k[0:64, :], k.cmp_b2[0].unsqueeze(1)).then_inc(k.cw_here, 16)
        act.dma_start(b2k[64:128, :], k.cmp_b2[0].unsqueeze(1)).then_inc(k.cw_here, 16)
        act.dma_start(b2v[:, :], k.cmp_b2[1].partition_broadcast(NCMP)).then_inc(k.cw_here, 16)
        drained(act, k, "pb")
        for q in range(NS):
            for s in range(2):
                b, free = full_bank(act, k, ("hid", q, s))
                for hh in range(2):
                    m = act.activation(hid[:, s, hh, :], b[:, G * NCMP * hh:G * NCMP * (hh + 1)], ACT.Silu,
                                       bias=pb[:, 2 * s + hh:2 * s + hh + 1])
                m.then_inc(free, 1)

    @block.vector
    def _(dve):
        dve.wait_ge(k.cw_here, 16 * 6)
        b, free = full_bank(dve, k, "posT")
        dve.tensor_copy(posT[:, :], b[:, 0:32]).then_inc(free, 1)
        b, free = full_bank(dve, k, "pb")
        dve.tensor_tensor(pb[:, :], b[:, 0:4], k.vecs2[:, 24:28], ALU.add).then_inc(free, 1)
        dve.memset(k.VBD[:, :, :], 0.0).then_inc(k.vbd_clear, 1)
        dve.wait_ge(k.vbd_clear, 1)

        def pairs(q):
            dve.wait_ge(k.raw_here[q % 2], 64 * (q // 2 + 1))
            if q:
                bank, n = k.bank_of[("R", q - 1, 1, 1)]
                dve.wait_ge(k.bank_full[bank], n)
            for s in range(2):
                src = raw[:, q % 2, :, :, 256 * s:256 * s + 256]
                for a in range(2):
                    m = dve.tensor_copy(pair[:, :, s, :, a, :], src[:, :, a, :].rearrange("p j (g d) -> p j g d", g=G))
                m.then_inc(k.pair_ready, 1)

        pairs(0)
        for q in range(NS):
            for s in range(2):
                if q:
                    bank, n = k.bank_of[("hid", q - 1, s)]
                    dve.wait_ge(k.bank_full[bank], n)
                for gp in range(2):
                    b, free = full_bank(dve, k, ("R", q, s, gp))
                    dve.tensor_copy(R[:, s, 2 * gp:2 * gp + 2, :], b.rearrange("p (g t) -> p g t", g=2)).then_inc(free, 1)
            if q + 1 < NS:
                pairs(q + 1)
            b, free = full_bank(dve, k, ("kc", q))
            dve.tensor_scalar(k.kcT[:, q, :, :], b[:, 0:2 * NCMP].rearrange("p (a n) -> p a n", a=2), b2k[:, :], None, ALU.add).then_inc(free, 1)
            b, free = full_bank(dve, k, ("vc", q))
            bias = b2v[:, :].unsqueeze(1).to_broadcast([NCMP, G, DH])
            src = b[0:NCMP, 0:SLOT].rearrange("p (g d) -> p g d", g=G)
            if q < SB:
                p0 = 32 * (q % 4)
                dve.tensor_tensor(k.vcS[p0:p0 + NCMP, q // 4, :].rearrange("p (g d) -> p g d", g=G), src, bias, ALU.add).then_inc(free, 1)
            else:
                for hh in range(HPG):
                    m = dve.tensor_tensor(k.VBD[32 * hh:32 * hh + NCMP, :, DH * hh:DH * hh + DH], src, bias, ALU.add)
                m.then_inc(free, 1)


def stage_query(nc, k, ctx):
    block = ctx.enter_context(nc.Block())
    SCALE = float(DH) ** -0.5

    @block.tensor
    def _(pe):
        for c in range(2):
            w = chunk(pe, k, CH_IN + c)
            for m4 in range(4):
                for hf, (t0, t1) in enumerate(HALF):
                    b, full = open_bank(pe, k, ("q", 4 * c + m4, hf))
                    for kt in range(KD):
                        m = pe.matmul(b[:, 0:t1 - t0], w[:, kt, 128 * m4:128 * m4 + 128], k.xnT[:, kt, t0:t1],
                                      start=kt == 0, stop=kt == KD - 1)
                    m.then_inc(full, 1)
            k.chunk_last[CH_IN + c] = k.bank_of[("q", 4 * c + 3, 1)]
        project_rows(pe, k, "bg", k.xnT, CH_IN + 2, 1)

    @block.sync
    def _(sp):
        load_chunks(sp, k, CH_IN + NW, CH_IN + 3 + NW)

    @block.gpsimd
    def _(pool):
        st = Steps(pool, k.pool_step, k, "pool")
        st.then(pool.memset(k.cmask[:, :, :], 0.0))
        st.then(pool.affine_select(out=k.cmask[:, :, :], in_=k.cmask[:, :, :], compare_op=ALU.is_ge, fill=NEG, base=-31,
                                   pattern=[[128, NT], [-16, 32]], channel_multiplier=1))
        st.then(pool.memset(k.mtmp[:, :], 0.0))
        st.then(pool.affine_select(out=k.mtmp[:, 0:128], in_=k.mtmp[:, 0:128], compare_op=ALU.is_ge, fill=NEG, base=0,
                                   pattern=[[-1, 128]], channel_multiplier=1))
        new = k.mtmp[0:32, 128:128 + SB * S].rearrange("p (b t) -> p b t", b=SB)
        st.then(pool.affine_select(out=new, in_=new, compare_op=ALU.is_ge, fill=NEG, base=0,
                                   pattern=[[-4, SB], [1, S]], channel_multiplier=0))
        st.then(pool.affine_select(out=new, in_=new, compare_op=ALU.is_ge, fill=NEG, base=0,
                                   pattern=[[16, SB], [-4, S]], channel_multiplier=1))
        old = k.mtmp[0:32, 128 + SB * S:132 + SB * S]
        st.then(pool.affine_select(out=old, in_=old, compare_op=ALU.is_ge, fill=NEG, base=-1,
                                   pattern=[[4, 4]], channel_multiplier=-1))
        pool.tensor_copy(k.identb[:, :], k.ident[:, :])
        pool.tensor_copy(k.causb[:, :], k.mtmp[:, 0:128])
        for g in range(G):
            st.then(pool.tensor_copy(k.newb[32 * g:32 * g + 32, :], k.mtmp[0:32, 128:132 + SB * S]))

    @block.scalar
    def _(act):
        act.wait_ge(k.q_clear, 3)
        for m in range(8):
            g = m // 2
            d0 = 64 * (g % 2)
            for hf in range(2):
                b, free = full_bank(act, k, ("q", m, hf))
                for a in range(2):
                    x = act.activation(k.Qp[d0:d0 + 64, 2 * m + a, 256 * hf:256 * hf + 256], b[64 * a:64 * a + 64, 0:256],
                                       ACT.Copy, scale=SCALE)
                    if hf:
                        hh = (2 * m + a) % HPG
                        x = act.activation(k.QS[d0:d0 + 64, :, g, hh:16:HPG],
                                           b[64 * a:64 * a + 64, 256:288].rearrange("p (b i) -> p b i", i=SI), ACT.Copy, scale=SCALE)
                x.then_inc(free, 1)
        for i in range(NT + 1):
            r = 128 if i < NT else S
            b, free = full_bank(act, k, ("bg", i))
            act.activation(k.gt[0:r, i, :], b[0:r, 0:3 * H], ACT.Sigmoid).then_inc(free, 1)

    @block.vector
    def _(dve):
        q = k.Qp[:, :, :].rearrange("p (a g h) t -> p a g (h t)", a=2, g=2)
        dve.memset(q[64:128, :, 0, :], 0.0).then_inc(k.q_clear, 1)
        dve.memset(q[0:64, :, 1, :], 0.0).then_inc(k.q_clear, 1)
        dve.memset(k.QS[:, :, :, :], 0.0).then_inc(k.q_clear, 1)


def z_rows(pe, k, br):
    for c in range(2):
        project_rows(pe, k, ("zb", br, c), k.xnT, CH_IN + 3 + 2 * br + c, 1)


def z_silu(act, k, br):
    for c in range(2):
        for i in range(NT + 1):
            r = 128 if i < NT else S
            b, free = full_bank(act, k, (("zb", br, c), i))
            act.activation(k.z[0:r, i, 512 * c:512 * c + 512], b[0:r, :], ACT.Silu).then_inc(free, 1)


def z_all(eng, k, br):
    for c in range(2):
        for i in range(NT + 1):
            drained(eng, k, (("zb", br, c), i))


def blend(pool, k, st, br, tmp, z, y):
    if br == 0:
        st.then(pool.tensor_tensor(y, tmp, z, ALU.mult))
    else:
        st.then(pool.tensor_tensor(tmp, tmp, z, ALU.mult))
        st.then(pool.tensor_tensor(y, y, tmp, ALU.add))


def sample_rows_out(pool, k, br, osall):
    pool.wait_ge(k.os_stored, k.os_count)
    for s in range(SB):
        pool.dma_start(osall[SI * s:SI * s + SI, :].rearrange("i (g x) -> i g x", g=G),
                       k.scratch[s].rearrange("(g i x) d -> i g (x d)", g=G, i=8)[0:SI]).then_inc(k.os_back, 16)


def stage_cmp_branch(nc, k, ctx):
    def sb(name, shape, dt=F32):
        return ctx.enter_context(nc.sbuf_tensor(name, shape, dt))
    Sc = sb("Sc", [128, 2, H, 32])
    Pc = sb("Pc", [128, 2, H, 32])
    PcT = sb("PcT", [128, 2, 4, 128])
    mx = sb("cmx", [128, 2, H])
    sm = sb("csm", [128, 2, H])
    tmp = sb("ctmp", [128, 2, HPG * DH])
    osb = sb("cos", [128, SB, DH])
    osall = sb("cosall", [S, ATT])
    block = ctx.enter_context(nc.Block())
    k.og0 = k.og

    @block.tensor
    def _(pe):
        z_rows(pe, k, 0)
        for i in range(NT + 1):
            b, full = open_bank(pe, k, ("cS", i))
            if i < NT:
                for h in range(H):
                    m = pe.matmul(b[:, 32 * h:32 * h + NCMP], k.Qp[:, h, 128 * i:128 * i + 128], k.kcT[:, SB, h // 8, :],
                                  start=True, stop=True)
            else:
                for s in range(SB):
                    for g in range(G):
                        m = pe.matmul(b[32 * g:32 * g + 32, 32 * s:32 * s + NCMP], k.QS[:, s, g, :], k.kcT[:, s, g // 2, :],
                                      start=True, stop=True)
            m.then_inc(full, 1)
        for i in range(NT):
            pe.wait_ge(k.cp_ready, i + 1)
            b, full = open_bank(pe, k, ("cT", i))
            for g in range(G):
                m = pe.transpose(b[:, 128 * g:128 * g + 128], Pc[:, i % 2, 4 * g:4 * g + 4, :].rearrange("p h n -> p (h n)"), k.ident[:, :])
            m.then_inc(full, 1)
            drained(pe, k, ("cT", i))
            for g in range(G):
                o = G * i + g
                if k.og0 + o >= 2:
                    pe.wait_ge(k.o_free, k.og0 + o - 1)
                pe.matmul(k.ps[:, 6 + o % 2, 0:256], PcT[:, i % 2, g, :], k.VBD[:, g, :],
                          start=True, stop=True).then_inc(k.o_full, 1)
        pe.wait_ge(k.cp_ready, NT + 1)
        b, full = open_bank(pe, k, ("cT", NT))
        for a in range(2):
            m = pe.transpose(b[:, 128 * a:128 * a + 128], Pc[:, 0, 4 * a:4 * a + 4, :].rearrange("p h n -> p (h n)"), k.ident[:, :])
        m.then_inc(full, 1)
        drained(pe, k, ("cT", NT))
        for r in range(4):
            b, full = open_bank(pe, k, ("cO", r))
            for a in range(2):
                for g in range(G):
                    m = pe.matmul(b[32 * g:32 * g + 32, DH * a:DH * a + DH], PcT[32 * r:32 * r + NCMP, 0, a, 32 * g:32 * g + 32],
                                  k.vcS[32 * r:32 * r + NCMP, a, DH * g:DH * g + DH], start=True, stop=True)
            m.then_inc(full, 1)

    @block.sync
    def _(sp):
        load_chunks(sp, k, CH_IN + 3 + NW, CH_IN + 5 + NW)

    @block.scalar
    def _(act):
        z_silu(act, k, 0)
        for i in range(NT + 1):
            act.wait_ge(k.cs_ready, i + 1)
            if i < NT:
                src, dst = Sc[:, i % 2, :, :], Pc[:, i % 2, :, :]
            else:
                src, dst = Sc[:, 0, 0:SB, :], Pc[:, 0, 0:SB, :]
            act.activation(dst, src, ACT.Exp).then_inc(k.cp_ready, 1)

    @block.vector
    def _(dve):
        st = Steps(dve, k.dve_step, k, "dve")
        st.then(dve.memset(Sc[:, :, :, :], NEG))

        def scores(i):
            b, free = full_bank(dve, k, ("cS", i))
            if i < NT:
                n, s_, m_ = H, Sc[:, i % 2, :, :], mx[:, i % 2, :]
                src = b.rearrange("p (h n) -> p h n", n=32)[:, :, 0:NCMP]
                st.then(dve.tensor_tensor(s_[:, :, 0:NCMP], src, k.cmask[:, i, 0:NCMP].unsqueeze(1).to_broadcast([128, H, NCMP]), ALU.add))
            else:
                n, s_, m_ = SB, Sc[:, 0, 0:SB, :], mx[:, 0, 0:SB]
                src = b[:, 0:32 * SB].rearrange("p (h n) -> p h n", n=32)[:, :, 0:NCMP]
                st.then(dve.tensor_copy(s_[:, :, 0:NCMP], src))
            dve.sem_inc(free, 1)
            st.then(dve.tensor_reduce(out=m_, in_=s_, axis=AX.X, op=ALU.max))
            st.then(dve.tensor_scalar(m_, m_, NEG / 10, None, ALU.max))
            dve.tensor_tensor(s_, s_, m_.unsqueeze(2).to_broadcast([128, n, 32]), ALU.subtract).then_inc(k.cs_ready, 1)

        def sums(i):
            dve.wait_ge(k.cp_ready, i + 1)
            if i < NT:
                p_, m_ = Pc[:, i % 2, :, :], sm[:, i % 2, :]
            else:
                p_, m_ = Pc[:, 0, 0:SB, :], sm[:, 0, 0:SB]
            st.then(dve.tensor_reduce(out=m_, in_=p_, axis=AX.X, op=ALU.add))
            st.then(dve.tensor_scalar(m_, m_, 1.0e-30, None, ALU.max))
            st.then(dve.reciprocal(m_, m_))
            if i < NT:
                st.then(dve.tensor_tensor(m_, m_, k.gt[:, i, 0:H], ALU.mult))
        scores(0)
        for i in range(NT):
            if i + 1 < NT:
                if i:
                    dve.wait_ge(k.cp_ready, i)
                scores(i + 1)
            sums(i)
            b, free = full_bank(dve, k, ("cT", i))
            if i >= 2:
                dve.wait_ge(k.o_full, k.og0 + G * (i - 1))
            dve.tensor_copy(PcT[:, i % 2, :, :], b.rearrange("p (g t) -> p g t", g=G)).then_inc(free, 1)
            for g in range(G):
                o = G * i + g
                dve.wait_ge(k.o_full, k.og0 + o + 1)
                if o >= 2:
                    dve.wait_ge(k.blended, k.og0 + o - 1)
                dve.tensor_tensor(tmp[:, o % 2, :].rearrange("p (h d) -> p h d", h=HPG),
                                  k.ps[:, 6 + o % 2, 0:256].rearrange("p (h d) -> p h d", h=HPG),
                                  sm[:, i % 2, 4 * g:4 * g + 4].unsqueeze(2).to_broadcast([128, HPG, DH]), ALU.mult).then_inc(k.o_free, 1)
        dve.wait_ge(k.cp_ready, NT)
        scores(NT)
        sums(NT)
        b, free = full_bank(dve, k, ("cT", NT))
        dve.wait_ge(k.o_full, k.og0 + G * (NT - 1))
        dve.tensor_copy(PcT[:, 0, 0:2, :], b[:, 0:256].rearrange("p (g t) -> p g t", g=2)).then_inc(free, 1)
        for r in range(4):
            b, free = full_bank(dve, k, ("cO", r))
            dve.tensor_tensor(osb[:, r:SB:4, :], b[:, 0:2 * DH].rearrange("p (a d) -> p a d", d=DH),
                              sm[:, 0, r:SB:4].unsqueeze(2).to_broadcast([128, 2, DH]), ALU.mult).then_inc(free, 1)

    @block.gpsimd
    def _(pool):
        st = Steps(pool, k.pool_step, k, "pool")
        z_all(pool, k, 0)
        for i in range(NT):
            for g in range(G):
                o = G * i + g
                pool.wait_ge(k.o_free, k.og0 + o + 1)
                blend(pool, k, st, 0, tmp[:, o % 2, :], k.z[:, i, 256 * g:256 * g + 256], k.y[:, i, 256 * g:256 * g + 256])
                pool.sem_inc(k.blended, 1)
        for r in range(4):
            drained(pool, k, ("cO", r))
        for s in range(SB):
            pool.dma_start(k.scratch[s], osb[:, s, :]).then_inc(k.os_stored, 16)
        k.os_count += 16 * SB
        sample_rows_out(pool, k, 0, osall)
        finish_samples(pool, k, st, 0, osall)
    k.og += G * NT


def finish_samples(pool, k, st, br, osall):
    k.os_backs += 16 * SB
    pool.wait_ge(k.os_back, k.os_backs)
    st.then(pool.tensor_tensor(osall[:, :].rearrange("p (h d) -> p h d", h=H), osall[:, :].rearrange("p (h d) -> p h d", h=H),
                               k.gt[0:S, NT, H * br:H * br + H].unsqueeze(2).to_broadcast([S, H, DH]), ALU.mult))
    blend(pool, k, st, br, osall[:, :], k.z[0:S, NT, :], k.y[0:S, NT, :])


def stage_key_branch(nc, k, ctx, br):
    def sb(name, shape, dt=F32):
        return ctx.enter_context(nc.sbuf_tensor(f"{name}_{br}", shape, dt))
    P = sb("P", [128, 3, TA])
    PT = sb("PT", [128, 3, T + 128])
    nmx = sb("nmx", [128, 4, 3])
    sm = sb("sm", [128, NT, H])
    rc = sb("rc", [128, 2, HPG])
    ss = sb("ss", [128, 2, 3])
    KTs = sb("KTs", [128, 2, T])
    tmp = sb("tmp", [128, 2, HPG * DH])
    osb = sb("osb", [128, SB, DH])
    pages = sb("pages", [1, SB * 4], I32)
    osall = KTs[0:S, :, :].rearrange("p a t -> p (a t)")
    raw = k.arena[:, (NT + 1) * D:(NT + 1) * D + 4096].rearrange("p (s r x) -> p s r x", s=2, r=4)
    block = ctx.enter_context(nc.Block())
    og0 = k.og
    items = [(i, h) for i in range(NT) for h in range(H)]
    NI = len(items)
    v = br - 1
    n0 = k.key_items

    @block.tensor
    def _(pe):
        z_rows(pe, k, br)
        for n in range(NI + 2):
            if n < NI:
                i, h = items[n]
                w = 128 * (i + 1)
                b, full = open_bank(pe, k, ("A", br, n))
                pe.matmul(b[:, 0:w], k.Qp[:, h, 128 * i:128 * i + 128], k.KT[:, v, h // 8, 0:w], start=True, stop=True)
                pe.matmul(b[:, w - 128:w], k.identb[:, :], k.causb[:, :], start=False, stop=True,
                          skip_group_check=True).then_inc(full, 1)
            if 1 <= n <= NI:
                i, h = items[n - 1]
                drained(pe, k, ("A", br, n - 1))
                b, full = open_bank(pe, k, ("T", br, n - 1))
                for j in range(i + 1):
                    m = pe.transpose(b[:, 128 * j:128 * j + 128], P[:, (n - 1) % 3, 128 * j:128 * j + 128], k.ident[:, :])
                m.then_inc(full, 1)
            if n >= 2:
                i, h = items[n - 2]
                drained(pe, k, ("T", br, n - 2))
                o, hh = (n - 2) // HPG, (n - 2) % HPG
                if hh == 0 and og0 + o >= 2:
                    pe.wait_ge(k.o_free, og0 + o - 1)
                g = h // HPG
                for j in range(i + 1):
                    m = pe.matmul(k.ps[:, 6 + o % 2, DH * hh:DH * hh + DH], PT[:, (n - 2) % 3, 128 * j:128 * j + 128],
                                  k.V[:, v, j, DH * g:DH * g + DH], start=j == 0, stop=j == i)
                m.then_inc(k.pv_done, 1)
        for s in range(SB + 1):
            if s < SB:
                pe.wait_ge(k.raw_slot[(s) % 2], 16 * k.raw_need(br, s))
                for gp in range(2):
                    b, full = open_bank(pe, k, ("sK", br, s, gp))
                    for r in range(4):
                        m = pe.transpose(b[:, 128 * r:128 * r + 128], raw[:, s % 2, r, 128 * gp:128 * gp + 128], k.ident[:, :])
                    m.then_inc(full, 1)
                drained(pe, k, ("sK", br, s, 0))
                drained(pe, k, ("sK", br, s, 1))
                b, full = open_bank(pe, k, ("sA", br, s))
                for g in range(G):
                    m = pe.matmul(b[32 * g:32 * g + 32, :], k.QS[:, s, g, :], KTs[:, g // 2, :], start=True, stop=True)
                if br == 2:
                    m = pe.matmul(b[:, 0:T:128], k.identb[:, :], k.newb[:, SB * S:SB * S + 4], start=False, stop=True,
                                  skip_group_check=True)
                m.then_inc(full, 1)
                b, full = open_bank(pe, k, ("sN", br, s))
                for g in range(G):
                    pe.matmul(b[32 * g:32 * g + 32, 0:S], k.QS[:, s, g, :], k.KT[:, v, g // 2, T:TA], start=True, stop=True)
                pe.matmul(b[:, 0:S], k.identb[:, :], k.newb[:, S * s:S * s + S], start=False, stop=True,
                          skip_group_check=True).then_inc(full, 1)
            if s:
                q = s - 1
                drained(pe, k, ("sN", br, q))
                b, full = open_bank(pe, k, ("sT", br, q))
                for r in range(4):
                    m = pe.transpose(b[:, 128 * r:128 * r + 128], P[:, q % 2, 128 * r:128 * r + 128], k.ident[:, :])
                m.then_inc(full, 1)
                b, full = open_bank(pe, k, ("sTn", br, q))
                pe.transpose(b[0:S, 0:128], P[:, q % 2, T:TA], k.ident[:, :]).then_inc(full, 1)
                drained(pe, k, ("sT", br, q))
                drained(pe, k, ("sTn", br, q))
                b, full = open_bank(pe, k, ("sO", br, q))
                for g in range(G):
                    for r in range(4):
                        pe.matmul(b[32 * g:32 * g + 32, 0:DH], PT[:, q % 2, 128 * r + 32 * g:128 * r + 32 * g + 32],
                                  raw[:, q % 2, r, SLOT + DH * g:SLOT + DH * g + DH], start=r == 0, stop=False)
                    m = pe.matmul(b[32 * g:32 * g + 32, 0:DH], PT[0:S, q % 2, T + 32 * g:T + 32 * g + 32],
                                  k.V[0:S, v, NT, DH * g:DH * g + DH], start=False, stop=True)
                m.then_inc(full, 1)

    @block.sync
    def _(sp):
        load_chunks(sp, k, CH_IN + 3 + 2 * br + NW, CH_IN + 5 + 2 * br + NW)
        if br == 1:
            sp.dma_start(pages[:, :], k.page_table.rearrange("b p -> (b p)").unsqueeze(0)).then_inc(k.pages_here, 16)
            sp.wait_ge(k.pages_here, 32)
        for s in range(SB):
            if s >= 2:
                bank, n = k.bank_of[("sO", br, s - 2)]
                sp.wait_ge(k.bank_full[bank], n)
            if br == 1:
                for pg in range(4):
                    page = sp.value_load(pages[0:1, 4 * s + pg:4 * s + pg + 1], min_val=0, max_val=k.cache_kv.shape[0] - 1)
                    src = k.cache_kv[bass.ds(page, 1)].rearrange("o (t r) s g d -> (o t) r (s g d)", r=4)[:, :, 2 * SLOT:4 * SLOT]
                    sp.dma_start(raw[32 * pg:32 * pg + 32, s % 2, :, :], src).then_inc(k.raw_slot[s % 2], 16)
            else:
                sp.dma_start(raw[:, s % 2, :, :], k.cache_win[s].rearrange("(t r) a g d -> t r (a g d)", r=4)).then_inc(k.raw_slot[s % 2], 16)

    @block.scalar
    def _(act):
        z_silu(act, k, br)
        for n, (i, h) in enumerate(items):
            w = 128 * (i + 1)
            act.wait_ge(k.mx_ready, n0 + n + 1)
            b, free = full_bank(act, k, ("A", br, n))
            if n >= 3:
                bank, c = k.bank_of[("T", br, n - 3)]
                act.wait_ge(k.bank_full[bank], c)
            act.activation(P[:, n % 3, 0:w], b[:, 0:w], ACT.Exp, bias=nmx[:, n % 4, 0:1], accum_out=sm[:, i, h:h + 1]).then_inc(free, 1)
        for s in range(SB):
            act.wait_ge(k.mx_ready, n0 + NI + s + 1)
            if s >= 2:
                bank, c = k.bank_of[("sTn", br, s - 2)]
                act.wait_ge(k.bank_full[bank], c)
            else:
                bank, c = k.bank_of[("T", br, NI - 1)]
                act.wait_ge(k.bank_full[bank], c)
            if s >= 2:
                act.wait_ge(k.ss_used, SB * v + s - 1)
            b, free = full_bank(act, k, ("sA", br, s))
            act.activation(P[:, s % 2, 0:T], b[:, :], ACT.Exp, bias=nmx[:, s % 2, 2:3], accum_out=ss[:, s % 2, 0:1]).then_inc(free, 1)
            b, free = full_bank(act, k, ("sN", br, s))
            act.activation(P[:, s % 2, T:TA], b[:, 0:S], ACT.Exp, bias=nmx[:, s % 2, 2:3], accum_out=ss[:, s % 2, 1:2]).then_inc(free, 1)

    @block.vector
    def _(dve):
        st = Steps(dve, k.dve_step, k, "dve")

        def maximum(n):
            i, h = items[n]
            b, _ = full_bank(dve, k, ("A", br, n))
            if n >= 4:
                drained(dve, k, ("A", br, n - 4))
            dve.tensor_reduce(out=nmx[:, n % 4, 0:1], in_=b[:, 0:128 * (i + 1)], axis=AX.X, op=ALU.max, negate=True).then_inc(k.mx_ready, 1)

        def keep(n):
            i, h = items[n]
            if n >= 3:
                dve.wait_ge(k.pv_done, NI * v + n - 2)
            b, free = full_bank(dve, k, ("T", br, n))
            dve.tensor_copy(PT[:, n % 3, 0:128 * (i + 1)], b[:, 0:128 * (i + 1)]).then_inc(free, 1)

        def out(o):
            i, g = o // G, o % G
            drained(dve, k, ("A", br, HPG * o + HPG - 1))
            st.then(dve.reciprocal(rc[:, o % 2, :], sm[:, i, HPG * g:HPG * g + HPG]))
            st.then(dve.tensor_tensor(rc[:, o % 2, :], rc[:, o % 2, :], k.gt[:, i, H * br + HPG * g:H * br + HPG * g + HPG], ALU.mult))
            dve.wait_ge(k.pv_done, NI * v + HPG * (o + 1))
            if o >= 2:
                dve.wait_ge(k.blended, og0 + o - 1)
            dve.tensor_tensor(tmp[:, o % 2, :].rearrange("p (h d) -> p h d", h=HPG),
                              k.ps[:, 6 + o % 2, 0:256].rearrange("p (h d) -> p h d", h=HPG),
                              rc[:, o % 2, :].unsqueeze(2).to_broadcast([128, HPG, DH]), ALU.mult).then_inc(k.o_free, 1)
        maximum(0)
        for n in range(NI):
            if n + 1 < NI:
                maximum(n + 1)
            keep(n)
            if n % HPG == 0 and n:
                out(n // HPG - 1)
        out(NI // HPG - 1)

        def sample_keys(s):
            for gp in range(2):
                b, free = full_bank(dve, k, ("sK", br, s, gp))
                if s:
                    bank, c = k.bank_of[("sA", br, s - 1)]
                    dve.wait_ge(k.bank_full[bank], c)
                dve.tensor_copy(KTs[:, gp, :], b[:, :]).then_inc(free, 1)
            if s >= 2:
                drained(dve, k, ("sN", br, s - 2))
            b, _ = full_bank(dve, k, ("sA", br, s))
            dve.tensor_reduce(out=nmx[:, s % 2, 0:1], in_=b[:, :], axis=AX.X, op=ALU.max)
            b, _ = full_bank(dve, k, ("sN", br, s))
            st.then(dve.tensor_reduce(out=nmx[:, s % 2, 1:2], in_=b[:, 0:S], axis=AX.X, op=ALU.max))
            dve.tensor_reduce(out=nmx[:, s % 2, 2:3], in_=nmx[:, s % 2, 0:2], axis=AX.X, op=ALU.max, negate=True).then_inc(k.mx_ready, 1)

        def sample_out(s):
            if s < 2:
                dve.wait_ge(k.pv_done, NI * (v + 1))
            if s >= 2:
                bank, c = k.bank_of[("sO", br, s - 2)]
                dve.wait_ge(k.bank_full[bank], c)
            b, free = full_bank(dve, k, ("sT", br, s))
            dve.tensor_copy(PT[:, s % 2, 0:T], b[:, :]).then_inc(free, 1)
            b, free = full_bank(dve, k, ("sTn", br, s))
            dve.tensor_copy(PT[0:S, s % 2, T:T + 128], b[0:S, 0:128]).then_inc(free, 1)
            drained(dve, k, ("sN", br, s))
            st.then(dve.tensor_tensor(ss[:, s % 2, 2:3], ss[:, s % 2, 0:1], ss[:, s % 2, 1:2], ALU.add))
            st.then(dve.reciprocal(ss[:, s % 2, 2:3], ss[:, s % 2, 2:3]))
            b, free = full_bank(dve, k, ("sO", br, s))
            st.then(dve.tensor_scalar(osb[:, s, :], b[:, 0:DH], ss[:, s % 2, 2:3], None, ALU.mult))
            dve.sem_inc(free, 1)
            dve.sem_inc(k.ss_used, 1)
        for s in range(SB + 1):
            if s < SB:
                sample_keys(s)
            if s:
                sample_out(s - 1)

    @block.gpsimd
    def _(pool):
        st = Steps(pool, k.pool_step, k, "pool")
        z_all(pool, k, br)
        for o in range(NI // HPG):
            i, g = o // G, o % G
            pool.wait_ge(k.o_free, og0 + o + 1)
            blend(pool, k, st, br, tmp[:, o % 2, :], k.z[:, i, 256 * g:256 * g + 256], k.y[:, i, 256 * g:256 * g + 256])
            pool.sem_inc(k.blended, 1)
        for s in range(SB):
            drained(pool, k, ("sO", br, s))
            pool.dma_start(k.scratch[s], osb[:, s, :]).then_inc(k.os_stored, 16)
        k.os_count += 16 * SB
        bank, c = k.bank_of[("sN", br, SB - 1)]
        pool.wait_ge(k.bank_full[bank], c)
        sample_rows_out(pool, k, br, osall)
        finish_samples(pool, k, st, br, osall)
    k.og += NI // HPG
    k.key_items += NI + SB


def stage_out(nc, k, ctx):
    def sb(name, shape, dt=F32):
        return ctx.enter_context(nc.sbuf_tensor(name, shape, dt))
    yT = sb("yT", [128, KD, TA])
    yo = sb("yo", [128, NT + 1, D])
    xr = sb("xr", [128, NT + 1, D])
    npost = sb("npost2", [128, D])
    sq = sb("sq3", [128, D])
    ssq = sb("ssq3", [128, NT + 1])
    rstd = sb("rstd3", [128, NT + 1])
    block = ctx.enter_context(nc.Block())

    @block.tensor
    def _(pe):
        for kt in range(KD):
            b, full = open_bank(pe, k, ("yT", kt))
            for i in range(NT):
                m = pe.transpose(b[:, 128 * i:128 * i + 128], k.y[:, i, 128 * kt:128 * kt + 128], k.ident[:, :])
            m.then_inc(full, 1)
        b, full = open_bank(pe, k, "yTs")
        for kt in range(KD):
            m = pe.transpose(b[:, S * kt:S * kt + S], k.y[0:S, NT, 128 * kt:128 * kt + 128], k.ident[0:S, 0:S])
        m.then_inc(full, 1)
        for kt in range(KD):
            drained(pe, k, ("yT", kt))
        drained(pe, k, "yTs")
        for n in range(D // 512):
            project_rows(pe, k, ("o", n), yT, CH_OUT + n, 1)

    @block.sync
    def _(sp):
        sp.dma_start(xr[:, 0:NT, :], k.o_yp[0].rearrange("(i p) d -> p i d", p=128)).then_inc(k.x_here, 16)
        sp.dma_start(xr[0:S, NT, :], k.o_ys.rearrange("b i d -> (b i) d")).then_inc(k.x_here, 16)
        sp.dma_start(npost[:, :], k.b_norm_post.partition_broadcast(128)).then_inc(k.x_here, 16)
        for i in range(NT + 1):
            sp.wait_ge(k.res_ready, NT + 1 + i + 1)
            if i < NT:
                sp.dma_start(k.o_yp[0, 128 * i:128 * i + 128, :], xr[:, i, :]).then_inc(k.stored_y, 16)
            else:
                sp.dma_start(k.o_ys.rearrange("b i d -> (b i) d"), xr[0:S, NT, :]).then_inc(k.stored_y, 16)
        sp.wait_ge(k.stored_y, 16 * (NT + 1))

    @block.scalar
    def _(act):
        for n in range(D // 512):
            for i in range(NT + 1):
                r = 128 if i < NT else S
                b, free = full_bank(act, k, (("o", n), i))
                act.activation(yo[0:r, i, 512 * n:512 * n + 512], b[0:r, :], ACT.Copy).then_inc(free, 1)
        act.wait_ge(k.ssq_clear, 3)
        for i in range(NT + 1):
            r = 128 if i < NT else S
            drained(act, k, (("o", 1), i))
            act.activation(sq[0:r, :], yo[0:r, i, :], ACT.Square, accum_out=ssq[0:r, i:i + 1]).then_inc(k.ssq_ready, 1)
            act.wait_ge(k.ssq_ready, (NT + 1) * 3 + i + 1)
        act.wait_ge(k.ms_ready, 4)
        act.activation(rstd[:, :], ssq[:, :], ACT.Sqrt).then_inc(k.std_ready, 1)

    @block.vector
    def _(dve):
        st = Steps(dve, k.dve_step, k, "dve")
        dve.memset(ssq[:, :], 1.0).then_inc(k.ssq_clear, 1)
        for kt in range(KD):
            b, free = full_bank(dve, k, ("yT", kt))
            dve.tensor_copy(yT[:, kt, 0:T], b[:, 0:T]).then_inc(free, 1)
        b, free = full_bank(dve, k, "yTs")
        dve.tensor_copy(yT[:, :, T:TA], b[:, 0:KD * S].rearrange("p (a b) -> p a b", b=S)).then_inc(free, 1)
        dve.wait_ge(k.x_here, 16 * 8)
        dve.wait_ge(k.ssq_ready, 4 * (NT + 1))
        row_rms(dve, st, k, ssq, rstd)
        for i in range(NT + 1):
            norm_residual(k, dve, st, yo, xr, npost, rstd, i)


def stage_attention(nc, k, sb, ctx):
    k.raw_need = lambda br, s: (4 if br == 1 else 1) * (s // 2 + 1) + (0 if br == 1 else 16)
    k.nring = 6
    k.og = k.os_count = k.os_backs = k.key_items = 0
    k.y = k.x1
    k.scratch = nc.dram_tensor("sample_rows", [SB, 128, DH], F32, kind="Internal").ap()
    with ExitStack() as att:
        k.Qp = sb("Qp", [128, H, T], where=att)
        k.QS = sb("QS", [128, SB, G, 32], where=att)
        k.gt = sb("gt", [128, NT + 1, 3 * H], where=att)
        k.cmask = sb("cmask", [128, NT, 32], where=att)
        k.identb = sb("identb", [128, 128], BF16, where=att)
        k.causb = sb("causb", [128, 128], BF16, where=att)
        k.newb = sb("newb", [128, SB * S + 4], BF16, where=att)
        with ExitStack() as c:
            k.mtmp = sb("mtmp", [128, 132 + SB * S], where=c)
            stage_query(nc, k, c)
        k.z = sb("z", [128, NT + 1, ATT], where=att)
        with ExitStack() as c:
            stage_cmp_branch(nc, k, c)
        for br in (1, 2):
            with ExitStack() as c:
                stage_key_branch(nc, k, c, br)
    with ExitStack() as c:
        stage_out(nc, k, c)


def build(nc, a, outs):
    k = Ctx()
    with ExitStack() as ctx:
        def sb(name, shape, dt=F32, where=ctx):
            return where.enter_context(nc.sbuf_tensor(name, shape, dt))

        def sem(name):
            return ctx.enter_context(nc.semaphore(name))
        k.x_prompt, k.x_sample, k.cache_kv, k.page_table, k.cache_win = (a[n] for n in (
            'x_prompt', 'x_sample', 'cache_kv', 'page_table', 'cache_win'))
        k.state_C, k.state_n, k.state_m, k.state_conv = (a[n][0] for n in ('state_C', 'state_n', 'state_m', 'state_conv'))
        k.a_norm_pre, k.w_up, k.conv_b, k.w_q, k.w_k, k.w_v, k.w_if, k.b_if, k.mh_w, k.skip, k.w_down, k.a_norm_post = (
            a[n][0] for n in ('a_norm_pre', 'a_w_up', 'a_conv_b', 'a_w_q', 'a_w_k', 'a_w_v', 'a_w_if', 'a_b_if',
                              'a_mh_w', 'a_skip', 'a_w_down', 'a_norm_post'))
        k.conv_w = a['a_conv_w'][0].rearrange("j c -> (j c)")
        k.kv_norm, k.w_kv, k.cmp_pos, k.cmp_w1, k.cmp_w2, k.cmp_b2 = (
            a[n] for n in ('kv_norm', 'w_kv', 'cmp_pos', 'cmp_w1', 'cmp_w2', 'cmp_b2'))
        k.cmp_b1 = a['cmp_b1'].rearrange("s n -> (s n)")
        k.b_norm_pre, k.w_in, k.w_out, k.b_norm_post = (a[n][0] for n in ('b_norm_pre', 'b_w_in', 'b_w_out', 'b_norm_post'))
        (k.o_yp, k.o_ys, k.o_kvp, k.o_kvs, k.o_wp, k.o_ws, k.o_cp, k.o_cs, k.o_np, k.o_ns, k.o_mp, k.o_ms,
         k.o_conv_p, k.o_conv_s) = outs
        k.o_conv_p, k.o_conv_s = k.o_conv_p[0, 0], k.o_conv_s[0]
        k.chunks = weight_chunks(k)
        k.ps = ctx.enter_context(nc.psum_tensor("ps", [128, 8, 512], F32))
        k.bank_full = [sem(f"bank_full{b}") for b in range(NRING)]
        k.bank_free = [sem(f"bank_free{b}") for b in range(NRING)]
        k.turns, k.bank_turns, k.bank_of, k.steps, k.chunk_last = 0, [0] * NRING, {}, {}, {}
        k.chunk_here = [sem(f"chunk_here{n}") for n in range(NW)]
        k.c_here = [sem(f"c_here{n}") for n in range(NCS)]
        k.c_stored = [sem(f"c_stored{n}") for n in range(NCS)]
        k.raw_here = [sem(f"raw_here{n}") for n in range(2)]
        k.raw_slot = [sem(f"raw_slot{n}") for n in range(2)]
        k.cst_stored = [sem(f"cst_stored{n}") for n in range(2)]
        k.x_here = sem("x_here")
        k.vec_here = sem("vec_here")
        k.ssq_clear = sem("ssq_clear")
        k.ssq_ready = sem("ssq_ready")
        k.ms_ready = sem("ms_ready")
        k.std_ready = sem("std_ready")
        k.xn_tok = sem("xn_tok")
        k.ident_ready = sem("ident_ready")
        k.pool_step = sem("pool_step")
        k.dve_step = sem("dve_step")
        k.act_step = sem("act_step")
        k.crow_here = sem("crow_here")
        k.wraw_here = sem("wraw_here")
        k.wif_here = sem("wif_here")
        k.bif_here = sem("bif_here")
        k.m0_here = sem("m0_here")
        k.nraw_here = sem("nraw_here")
        k.bd_ready = sem("bd_ready")
        k.pad_clear = sem("pad_clear")
        k.conv_ready = sem("conv_ready")
        k.xc_ready = sem("xc_ready")
        k.tails_ready = sem("tails_ready")
        k.stored = sem("stored")
        k.rows_ready = sem("rows_ready")
        k.wrow_ready = sem("wrow_ready")
        k.absf_ready = sem("absf_ready")
        k.softplus_ready = sem("softplus_ready")
        k.stored_m = sem("stored_m")
        k.p_ready = sem("p_ready")
        k.qm_ready = sem("qm_ready")
        k.acc_free = sem("acc_free")
        k.acc_full = sem("acc_full")
        k.kwm_ready = sem("kwm_ready")
        k.hn_ready = sem("hn_ready")
        k.num4_ready = sem("num4_ready")
        k.prod_ready = sem("prod_ready")
        k.n_ready = sem("n_ready")
        k.c_updated = sem("c_updated")
        k.nbd_ready = sem("nbd_ready")
        k.qw_ready = sem("qw_ready")
        k.skip_ready = sem("skip_ready")
        k.cst_ready = sem("cst_ready")
        k.stored_n = sem("stored_n")
        k.w_ready = sem("w_ready")
        k.var_ready = sem("var_ready")
        k.sd_ready = sem("sd_ready")
        k.gated = sem("gated")
        k.half_done = sem("half_done")
        k.res_ready = sem("res_ready")
        k.stored_x1 = sem("stored_x1")
        k.kv_here = sem("kv_here")
        k.stored_win = sem("stored_win")
        k.stored_kv = sem("stored_kv")
        k.kvt_free = sem("kvt_free")
        k.cw_here = sem("cw_here")
        k.pair_ready = sem("pair_ready")
        k.pages_here = sem("pages_here")
        k.vbd_clear = sem("vbd_clear")
        k.q_clear = sem("q_clear")
        k.os_stored = sem("os_stored")
        k.os_back = sem("os_back")
        k.cp_ready = sem("cp_ready")
        k.cs_ready = sem("cs_ready")
        k.o_full = sem("o_full")
        k.o_free = sem("o_free")
        k.blended = sem("blended")
        k.pv_done = sem("pv_done")
        k.mx_ready = sem("mx_ready")
        k.ss_used = sem("ss_used")
        k.stored_y = sem("stored_y")
        k.wring = sb("wring", [128, NW, WCH])
        k.ident = sb("ident", [128, 128])
        k.ones = sb("ones", [128, 128])
        k.mask32 = sb("mask32", [128, 32])
        k.maskT = sb("maskT", [128, 128])
        k.maskS = sb("maskS", [S, S])
        k.bmask = sb("bmask", [128, SB, S])
        k.tmask = sb("tmask", [S, SB])
        k.fold = sb("fold", [128, S])
        k.vecs1 = sb("vecs1", [128, 112])
        k.vecs2 = sb("vecs2", [128, 28])
        k.xnT = sb("xnT", [128, KD, TA])
        k.arena = sb("arena", [128, (NT + 1) * D + KD * TA])
        k.x1 = k.arena[:, 0:(NT + 1) * D].rearrange("p (i d) -> p i d", d=D)
        k.kvT = k.arena[:, (NT + 1) * D:].rearrange("p (a t) -> p a t", t=TA)
        k.halves, k.nring = 0, NRING
        with ExitStack() as mlstm:
            k.scan_add = sb("scan_add", [AH, TA], where=mlstm)
            k.scan_mul = sb("scan_mul", [AH, TA], where=mlstm)
            k.headsel = sb("headsel", [AH, AH, 128], where=mlstm)
            with ExitStack() as c:
                stage_norm_in(nc, k, c)
            k.xcT = sb("xcT", [128, FT, TA], where=mlstm)
            with ExitStack() as cell:
                k.xrow = k.arena[:, 0:FT * XPW].rearrange("p (f x) -> p f x", x=XPW)
                k.xp = k.xrow[:, :, 0:XPS]
                k.xs = k.xrow[:, :, XPS:XPW].rearrange("p f (b j) -> p f b j", b=SB)
                k.xms = sb("xms", [128, FT, S], where=cell)
                k.wraw = sb("wraw", [128, 3, FT, 4], where=cell)
                k.bd = sb("bd", [128, 3, 4, 128], where=cell)
                k.bif = sb("bif", [36, 1], where=cell)
                k.m0 = sb("m0", [AH, SB], where=cell)
                k.nT = sb("nT", [128, 128], where=cell)
                k.gates = sb("gates", [AH, 2, TA], where=cell)
                with ExitStack() as c:
                    stage_up(nc, k, c)
                k.brow = sb("brow", [AH, TA + S + SB], where=cell)
                k.cols = sb("cols", [128, NT + 1, 96], where=cell)
                with ExitStack() as c:
                    stage_gates(nc, k, c)
                with ExitStack() as c:
                    stage_cell(nc, k, c)
            with ExitStack() as c:
                stage_gate(nc, k, c)
            with ExitStack() as c:
                stage_down(nc, k, c)
        k.V = sb("V", [128, 2, NT + 1, SLOT])
        k.KT = sb("KT", [128, 2, 2, TA])
        k.kcT = sb("kcT", [128, SB + 1, 2, NCMP])
        k.vcS = sb("vcS", [128, 2, SLOT])
        k.VBD = sb("VBD", [128, G, HPG * DH])
        with ExitStack() as c:
            stage_kv(nc, k, c)
        with ExitStack() as c:
            stage_compress(nc, k, c)
        stage_attention(nc, k, sb, ctx)


_INS = ['x_prompt', 'x_sample', 'cache_kv', 'page_table', 'cache_win', 'state_C', 'state_n', 'state_m', 'state_conv',
        'a_norm_pre', 'a_w_up', 'a_conv_w', 'a_conv_b', 'a_w_q', 'a_w_k', 'a_w_v', 'a_w_if', 'a_b_if', 'a_mh_w',
        'a_skip', 'a_w_down', 'a_norm_post', 'kv_norm', 'w_kv', 'cmp_pos', 'cmp_w1', 'cmp_b1', 'cmp_w2', 'cmp_b2',
        'b_norm_pre', 'b_w_in', 'b_w_out', 'b_norm_post']
_OUTS = [(1, 512, 1024), (8, 4, 1024), (1, 512, 4, 4, 64), (8, 4, 4, 4, 64), (1, 512, 2, 4, 64), (8, 512, 2, 4, 64),
         (1, 1, 4, 512, 512), (1, 8, 4, 512, 512), (1, 1, 4, 512), (1, 8, 4, 512), (1, 1, 4), (1, 8, 4),
         (1, 1, 3, 2048), (1, 8, 3, 2048)]


def kernel(**inputs):
    import numpy as _np
    import concourse.bacc as _bacc
    from concourse import mybir as _mybir
    from concourse.bass_utils import run_bass_kernel_spmd as _run

    nc = _bacc.Bacc("TRN2", target_bir_lowering=False, num_devices=1)
    arrays, ins, outs = {}, {}, []
    for name in _INS:
        a = _np.ascontiguousarray(inputs[name])
        arrays[f"in_{name}_dram"] = a
        ins[name] = nc.dram_tensor(f"in_{name}_dram", a.shape, _mybir.dt.from_np(a.dtype), kind="ExternalInput").ap()
    for i, shape in enumerate(_OUTS):
        outs.append(nc.dram_tensor(f"out_{i}_dram", shape, _mybir.dt.float32, kind="ExternalOutput").ap())
    build(nc, ins, outs)
    r = _run(nc, [arrays], core_ids=[0])
    return tuple(r.results[0][f"out_{i}_dram"] for i in range(len(_OUTS)))
```

```python
import concourse.bass as bass
from concourse import mybir
from contextlib import ExitStack

F32 = mybir.dt.float32
BF16 = mybir.dt.bfloat16
I32 = mybir.dt.int32
ALU = mybir.AluOpType
ACT = mybir.ActivationFunctionType
AX = mybir.AxisListType

D = 1024
KD = D // 128
T = 512
NT = T // 128
SB, SI = 8, 4
S = SB * SI
TA = T + S
HALF = [(0, 256), (256, TA)]
INNER = 2048
FT = INNER // 128
AH, AD = 4, 512
HF = AD // 128
CONV = 4
XPW = CONV - 1 + T + SB * (CONV - 1 + SI)
XPS = CONV - 1 + T
H, DH, G = 16, 64, 4
HPG = H // G
ATT = H * DH
PAST = 512
SLOT = G * DH
NCMP = (T - 32) // 16 + 1
NEG = -1.0e30
EPS = 1e-6
NRING = 7
NW = 2
WCH = 8 * 512


class Ctx:
    pass


def weight_chunks(k):
    def cols(w, c0, n):
        return w[:, c0:c0 + n].rearrange("(kt p) n -> p kt n", p=128)
    out = [cols(k.w_up, 512 * c, 512) for c in range(8)]
    for n in range(2):
        for half in range(2):
            out.append(cols(k.w_down[1024 * half:1024 * half + 1024, :], 512 * n, 512))
    out += [cols(k.w_kv, 512 * c, 512) for c in range(3)]
    out += [k.cmp_w1[s].rearrange("(j p) n -> p j n", p=128) for s in range(2)]
    out += [cols(k.w_in, 0, 512), cols(k.w_in, 512, 512), cols(k.w_in, 4096, 48)]
    out += [cols(k.w_in, 512 * c, 512) for c in range(2, 8)]
    out += [cols(k.w_out, 512 * c, 512) for c in range(2)]
    return out


CH_UP, CH_DOWN, CH_KV, CH_CMP, CH_IN, CH_OUT, CH_END = 0, 8, 12, 15, 17, 26, 28


def load_chunks(sp, k, lo, hi):
    for c in range(lo, min(hi, CH_END)):
        src = k.chunks[c]
        n = src.shape[1] * src.shape[2]
        dst = k.wring[:, c % NW, 0:n].rearrange("p (a b) -> p a b", b=src.shape[2])
        if c >= NW:
            bank, n_full = k.chunk_last[c - NW]
            sp.wait_ge(k.half_done if bank == "half" else k.bank_full[bank], n_full)
        sp.dma_start(dst, src).then_inc(k.chunk_here[c % NW], 16)


def chunk(pe, k, c):
    src = k.chunks[c]
    pe.wait_ge(k.chunk_here[c % NW], 16 * (c // NW + 1))
    n = src.shape[1] * src.shape[2]
    return k.wring[:, c % NW, 0:n].rearrange("p (a b) -> p a b", b=src.shape[2])


def open_bank(pe, k, key):
    bank = k.turns % k.nring
    k.turns += 1
    n = k.bank_turns[bank]
    if n:
        pe.wait_ge(k.bank_free[bank], n)
    k.bank_turns[bank] = n + 1
    k.bank_of[key] = (bank, n + 1)
    return k.ps[:, bank], k.bank_full[bank]


def full_bank(eng, k, key):
    bank, n = k.bank_of[key]
    eng.wait_ge(k.bank_full[bank], n)
    return k.ps[:, bank], k.bank_free[bank]


def drained(eng, k, key):
    bank, n = k.bank_of[key]
    eng.wait_ge(k.bank_free[bank], n)


class Steps:

    def __init__(self, eng, sem, k, name):
        self.eng, self.sem, self.k, self.name = eng, sem, k, name

    def then(self, ins):
        self.k.steps[self.name] = n = self.k.steps.get(self.name, 0) + 1
        ins.then_inc(self.sem, 1)
        self.eng.wait_ge(self.sem, n)


def head_blocks(pool, k, r):
    for m3 in range(3):
        pool.tensor_tensor(k.bd[:, m3, :, :].rearrange("p f (n d) -> p f n d", d=4),
                           k.wraw[:, m3, 4 * r:4 * r + 4, :].unsqueeze(2).to_broadcast([128, 4, 32, 4]),
                           k.mask32[:, :].unsqueeze(1).unsqueeze(3).to_broadcast([128, 4, 32, 4]),
                           ALU.mult).then_inc(k.bd_ready, 1)


def stage_norm_in(nc, k, ctx):
    def sb(name, shape, dt=F32):
        return ctx.enter_context(nc.sbuf_tensor(name, shape, dt))
    xt = sb("xt", [128, NT + 1, D])
    sq = sb("sq_junk", [128, D])
    ssq = sb("ssq", [128, NT + 1])
    rstd = sb("rstd", [128, NT + 1])
    v1raw = sb("v1raw", [112, 128])
    v2raw = sb("v2raw", [28, 128])
    block = ctx.enter_context(nc.Block())

    @block.tensor
    def _(pe):
        pe.wait_ge(k.ident_ready, 1)
        pe.wait_ge(k.vec_here, 8 * 16)
        for key, src, n in (("v1", v1raw, 112), ("v2", v2raw, 28)):
            b, full = open_bank(pe, k, key)
            pe.transpose(b[:, 0:n], src[:, :], k.ident[0:n, 0:n]).then_inc(full, 1)
        pe.wait_ge(k.xn_tok, NT + 1)
        for kt in range(KD):
            b, full = open_bank(pe, k, ("xT", kt))
            for i in range(NT):
                m = pe.transpose(b[:, 128 * i:128 * i + 128], xt[:, i, 128 * kt:128 * kt + 128], k.ident[:, :])
            m.then_inc(full, 1)
        b, full = open_bank(pe, k, "xTs")
        for kt in range(KD):
            m = pe.transpose(b[:, S * kt:S * kt + S], xt[0:S, NT, 128 * kt:128 * kt + 128], k.ident[0:S, 0:S])
        m.then_inc(full, 1)

    @block.sync
    def _(sp):
        sp.dma_start(xt[:, 0:NT, :], k.x_prompt[0].rearrange("(i p) d -> p i d", p=128)).then_inc(k.x_here, 16)
        sp.dma_start(xt[0:S, NT, :], k.x_sample.rearrange("b i d -> (b i) d")).then_inc(k.x_here, 16)
        for j, (src, n) in enumerate([(k.conv_w, 4 * FT), (k.conv_b, FT), (k.mh_w, FT), (k.skip, FT)]):
            row = [0, 64, 80, 96][j]
            sp.dma_start(v1raw[row:row + n, :], src.rearrange("(a p) -> a p", p=128)).then_inc(k.vec_here, 16)
        for j, (src, n) in enumerate([(k.a_norm_pre, 8), (k.kv_norm, 8), (k.b_norm_pre, 8), (k.cmp_b1, 4)]):
            row = 8 * j
            sp.dma_start(v2raw[row:row + n, :], src.rearrange("(a p) -> a p", p=128)).then_inc(k.vec_here, 16)
        load_chunks(sp, k, 0, NW)

    @block.gpsimd
    def _(pool):
        st = Steps(pool, k.pool_step, k, "pool")

        def make(t, fill, *selects):
            st.then(pool.memset(t, fill))
            for value, op, base, pattern, cm in selects:
                st.then(pool.affine_select(out=t, in_=t, compare_op=op, fill=value, base=base,
                                           pattern=pattern, channel_multiplier=cm))
        make(k.ident[:, :], 0.0, (1.0, ALU.not_equal, 0, [[-1, 128]], 1))
        pool.memset(k.ones[:, :], 1.0).then_inc(k.ident_ready, 1)
        make(k.mask32[:, :], 1.0, (0.0, ALU.is_ge, 0, [[-4, 32]], 1), (0.0, ALU.is_ge, 3, [[4, 32]], -1))
        make(k.maskT[:, :], 0.0, (NEG, ALU.is_ge, 0, [[1, 128]], -1))
        make(k.maskS[:, :], 0.0, (NEG, ALU.is_ge, 0, [[4, SB], [1, SI]], -1), (NEG, ALU.is_ge, 0, [[-4, SB], [0, SI]], 1))
        make(k.bmask[:, :, :], 0.0, (1.0, ALU.not_equal, 0, [[1, SB], [-1, SB], [0, SI]], 0))
        make(k.tmask[0:S, :], 1.0, (0.0, ALU.is_ge, 0, [[-4, SB]], 1), (0.0, ALU.is_ge, 3, [[4, SB]], -1))
        for block32 in range(1, 4):
            st.then(pool.tensor_copy(k.tmask[32 * block32:32 * block32 + 32, :], k.tmask[0:S, :]))
        make(k.fold[:, :], 0.0, *[(1.0, ALU.not_equal, -32 * g, [[-1, S]], 1) for g in range(4)])
        make(k.headsel[:, :, :], 0.0, (1.0, ALU.not_equal, 0, [[-1, AH], [0, 128]], 1))
        st.then(pool.memset(k.scan_mul[:, :], 1.0))
        st.then(pool.memset(k.scan_mul[:, T:TA].rearrange("p (b i) -> p b i", i=SI)[:, :, 0:1], 0.0))
        st.then(pool.memset(k.scan_add[:, :], 0.0))
        st.then(pool.memset(k.scan_add[:, T:TA].rearrange("p (b i) -> p b i", i=SI)[:, :, 0:1], -1.0e38))

    @block.scalar
    def _(act):
        act.wait_ge(k.x_here, 32)
        act.wait_ge(k.ssq_clear, 1)
        for i in range(NT + 1):
            r = 128 if i < NT else S
            act.activation(sq[0:r, :], xt[0:r, i, :], ACT.Square, accum_out=ssq[0:r, i:i + 1]).then_inc(k.ssq_ready, 1)
            act.wait_ge(k.ssq_ready, i + 1)
        act.wait_ge(k.ms_ready, 1)
        act.activation(rstd[:, :], ssq[:, :], ACT.Sqrt).then_inc(k.std_ready, 1)
        for kt in range(KD):
            b, free = full_bank(act, k, ("xT", kt))
            act.activation(k.xnT[:, kt, 0:T], b[:, 0:T], ACT.Copy, scale=k.vecs2[:, kt:kt + 1]).then_inc(free, 1)

    @block.vector
    def _(dve):
        st = Steps(dve, k.dve_step, k, "dve")
        dve.memset(ssq[:, :], 1.0).then_inc(k.ssq_clear, 1)
        for key, dst, n in (("v1", k.vecs1, 112), ("v2", k.vecs2, 28)):
            b, free = full_bank(dve, k, key)
            dve.tensor_copy(dst[:, :], b[:, 0:n]).then_inc(free, 1)
        dve.wait_ge(k.ssq_ready, NT + 1)
        dve.tensor_scalar(ssq[:, :], ssq[:, :], 1.0 / D, EPS, ALU.mult, ALU.add).then_inc(k.ms_ready, 1)
        dve.wait_ge(k.std_ready, 1)
        st.then(dve.reciprocal(rstd[:, :], rstd[:, :]))
        for i in range(NT + 1):
            r = 128 if i < NT else S
            dve.tensor_scalar(xt[0:r, i, :], xt[0:r, i, :], rstd[0:r, i:i + 1], None, ALU.mult).then_inc(k.xn_tok, 1)
        b, free = full_bank(dve, k, "xTs")
        dve.tensor_tensor(k.xnT[:, :, T:TA], b[:, 0:KD * S].rearrange("p (a b) -> p a b", b=S),
                          k.vecs2[:, 0:KD].unsqueeze(2).to_broadcast([128, KD, S]), ALU.mult).then_inc(free, 1)


def stage_up(nc, k, ctx):
    def sb(name, shape, dt=F32):
        return ctx.enter_context(nc.sbuf_tensor(name, shape, dt))
    wif = sb("wif", [128, 3 * FT, 8])
    crow = sb("crow", [27, INNER])
    convt = sb("convt", [128, 2, XPW])
    bdt = sb("bdt", [128, 3, FT // 4, 128])
    nraw = sb("nraw", [128, 128])
    wc = sb("wc", [128, 2 * FT, 36])
    tails = sb("tails", [128, FT, 27])
    tail_rows = crow
    block = ctx.enter_context(nc.Block())
    RUN = XPW - 3
    q4 = FT // 4

    @block.tensor
    def _(pe):
        pe.wait_ge(k.crow_here, 16)
        b, full = open_bank(pe, k, "cs")
        for f in range(FT):
            m = pe.transpose(b[:, 24 * f:24 * f + 24], crow[0:24, 128 * f:128 * f + 128], k.ident[0:24, 0:24])
        m.then_inc(full, 1)
        pe.wait_ge(k.nraw_here, 16)
        b, full = open_bank(pe, k, "nT")
        pe.transpose(b[:, 0:128], nraw[:, :], k.ident[:, :]).then_inc(full, 1)
        drained(pe, k, ("xT", KD - 1))
        drained(pe, k, "xTs")
        for c in range(4):
            w = chunk(pe, k, CH_UP + c)
            for m4 in range(4):
                f = 4 * c + m4
                for hf, (t0, t1) in enumerate(HALF):
                    b, full = open_bank(pe, k, ("up", f, hf))
                    for kt in range(KD):
                        m = pe.matmul(b[:, 0:t1 - t0], w[:, kt, 128 * m4:128 * m4 + 128], k.xnT[:, kt, t0:t1],
                                      start=kt == 0, stop=kt == KD - 1)
                    m.then_inc(full, 1)
            k.chunk_last[CH_UP + c] = k.bank_of[("up", f, 1)]
            if c == 3:
                pe.wait_ge(k.wif_here, 16)
                for r in range(4):
                    pe.wait_ge(k.bd_ready, 3 * r + 3)
                    for m3 in range(3):
                        b, full = open_bank(pe, k, ("bdt", r, m3))
                        for g in range(q4):
                            m = pe.transpose(b[:, 128 * g:128 * g + 128], k.bd[:, m3, g, :], k.ident[:, :])
                        m.then_inc(full, 1)
                    b, full = open_bank(pe, k, ("wc", r))
                    drained(pe, k, ("bdt", r, 2))
                    for g in range(q4):
                        f = q4 * r + g
                        pe.matmul(b[:, 8 * g:8 * g + 8], bdt[:, 0, g, :], wif[:, f, :], start=True, stop=False)
                        pe.matmul(b[:, 8 * g:8 * g + 8], bdt[:, 1, g, :], wif[:, FT + f, :], start=False, stop=True)
                        m = pe.matmul(b[:, 32 + 8 * g:40 + 8 * g], bdt[:, 2, g, :], wif[:, 2 * FT + f, :],
                                      start=True, stop=True)
                    m.then_inc(full, 1)
        for r in range(4):
            drained(pe, k, ("wc", r))
        pe.wait_ge(k.xc_ready, FT)
        for hf, (t0, t1) in enumerate(HALF):
            b, full = open_bank(pe, k, ("gate", hf))
            for f in range(FT):
                pe.matmul(b[0:36, 0:t1 - t0], wc[:, f, :], k.xcT[:, f, t0:t1], start=f == 0, stop=False)
            for f in range(FT):
                if hf == 0:
                    m = pe.matmul(b[0:36, 0:256], wc[:, FT + f, :], k.xp[:, f, 3:259], start=False, stop=f == FT - 1)
                else:
                    pe.matmul(b[0:36, 0:256], wc[:, FT + f, :], k.xp[:, f, 259:515], start=False, stop=False)
                    m = pe.matmul(b[0:36, 256:288].rearrange("p (b i) -> p b i", i=SI), wc[:, FT + f, :],
                                  k.xs[:, f, :, 3:7], start=False, stop=f == FT - 1)
            m.then_inc(full, 1)
        pe.wait_ge(k.tails_ready, 2)
        for r in range(4):
            b, full = open_bank(pe, k, ("tail", r))
            for g in range(4):
                m = pe.transpose(b[0:27, 128 * g:128 * g + 128], tails[:, 4 * r + g, :], k.ident[:, :])
            m.then_inc(full, 1)

    @block.sync
    def _(sp):
        load_chunks(sp, k, NW, CH_UP + 4)

    @block.gpsimd
    def _(pool):
        pool.dma_start(crow[0:24, :], k.state_conv.rearrange("b j c -> (b j) c")).then_inc(k.crow_here, 16)
        for m3, w in enumerate((k.w_q, k.w_k, k.w_v)):
            pool.dma_start(k.wraw[:, m3, :, :], w.rearrange("(f n) c d -> (n c) f d", f=FT)).then_inc(k.wraw_here, 16)
        pool.dma_start(wif[:, :, :], k.w_if.rearrange("(a p) j -> p a j", p=128)).then_inc(k.wif_here, 16)
        pool.dma_start(k.bif[0:4, :], k.b_if[0:4].unsqueeze(1)).then_inc(k.bif_here, 16)
        pool.dma_start(k.bif[32:36, :], k.b_if[4:8].unsqueeze(1)).then_inc(k.bif_here, 16)
        pool.dma_start(k.m0[:, :], k.state_m.rearrange("b h -> h b"), allow_slow_non_contiguous=True).then_inc(k.m0_here, 16)
        pool.dma_start(nraw[:, :], k.state_n.rearrange("b h (f p) -> (b h f) p", p=128)).then_inc(k.nraw_here, 16)
        pool.wait_ge(k.wraw_here, 48)
        for r in range(4):
            if r:
                drained(pool, k, ("bdt", r - 1, 2))
            head_blocks(pool, k, r)
        drained(pool, k, ("tail", 3))
        pool.dma_start(k.o_conv_p, tail_rows[0:3, :]).then_inc(k.stored, 16)
        pool.dma_start(k.o_conv_s.rearrange("b j c -> (b j) c"), tail_rows[3:27, :]).then_inc(k.stored, 16)
        pool.wait_ge(k.stored, 32)

    @block.scalar
    def _(act):
        act.wait_ge(k.pad_clear, 2)
        for f in range(FT + 1):
            if f < FT:
                for hf in range(2):
                    b, free = full_bank(act, k, ("up", f, hf))
                    m = act.activation(k.xp[:, f, 3 + 256 * hf:259 + 256 * hf], b[:, 0:256], ACT.Copy)
                    if hf == 1:
                        m = act.activation(k.xs[:, f, :, 3:7], b[:, 256:288].rearrange("p (b i) -> p b i", i=SI), ACT.Copy)
                    m.then_inc(free, 1)
            if f:
                act.wait_ge(k.conv_ready, f)
                act.activation(k.xcT[:, f - 1, 0:T], convt[:, (f - 1) % 2, 0:T], ACT.Silu)
                act.activation(k.xcT[:, f - 1, T:TA].rearrange("p (b i) -> p b i", i=SI),
                               convt[:, (f - 1) % 2, 515:515 + 7 * SB].rearrange("p (b j) -> p b j", j=7)[:, :, 0:SI],
                               ACT.Silu).then_inc(k.xc_ready, 1)

    @block.vector
    def _(dve):
        st = Steps(dve, k.dve_step, k, "dve")
        dve.memset(k.xp[:, :, 0:3], 0.0).then_inc(k.pad_clear, 1)
        dve.memset(wc[:, :, :], 0.0).then_inc(k.pad_clear, 1)
        b, free = full_bank(dve, k, "cs")
        dve.tensor_copy(k.xs[:, :, :, 0:3], b[:, 0:24 * FT].rearrange("p (f b j) -> p f b j", b=SB, j=3)).then_inc(free, 1)
        dve.wait_ge(k.pad_clear, 2)
        drained(dve, k, "cs")
        b, free = full_bank(dve, k, "nT")
        dve.tensor_copy(k.nT[:, :], b[:, 0:128]).then_inc(free, 1)

        def conv(f):
            drained(dve, k, ("up", f, 1))
            if f >= 2:
                dve.wait_ge(k.xc_ready, f - 1)
            row = k.xrow[:, f, :]
            out = convt[:, f % 2, 0:RUN]
            st.then(dve.tensor_scalar(out, row[:, 0:RUN], k.vecs1[:, f:f + 1], k.vecs1[:, 64 + f:65 + f], ALU.mult, ALU.add))
            for j in range(1, 4):
                m = dve.scalar_tensor_tensor(out=out, in0=row[:, j:j + RUN], scalar=k.vecs1[:, 16 * j + f:16 * j + f + 1],
                                             in1=out, op0=ALU.mult, op1=ALU.add)
                if j < 3:
                    st.then(m)
                else:
                    m.then_inc(k.conv_ready, 1)

        def gate_weights(r):
            for m3 in range(3):
                b, free = full_bank(dve, k, ("bdt", r, m3))
                dve.tensor_copy(bdt[:, m3, :, :], b.rearrange("p (g c) -> p g c", c=128)).then_inc(free, 1)
            b, free = full_bank(dve, k, ("wc", r))
            for part in range(2):
                src = b[:, 32 * part:32 * part + 32].rearrange("p (g j) -> p g j", j=8)
                rows = wc[:, FT * part + q4 * r:FT * part + q4 * r + q4, :]
                dve.tensor_copy(rows[:, :, 0:4], src[:, :, 0:4])
                m = dve.tensor_copy(rows[:, :, 32:36], src[:, :, 4:8])
            m.then_inc(free, 1)
        for f in range(FT):
            conv(f)
        for r in range(4):
            gate_weights(r)
        dve.wait_ge(k.bif_here, 32)
        for hf, (t0, t1) in enumerate(HALF):
            b, free = full_bank(dve, k, ("gate", hf))
            dve.tensor_scalar(k.gates[:, 0, t0:t1], b[0:4, 0:t1 - t0], k.bif[0:4, :], None, ALU.add)
            dve.tensor_scalar(k.gates[:, 1, t0:t1], b[32:36, 0:t1 - t0], k.bif[32:36, :], None, ALU.add).then_inc(free, 1)
        dve.tensor_copy(k.xms[:, :, :].rearrange("p f (b i) -> p f b i", i=SI), k.xs[:, :, :, 3:7])
        dve.tensor_copy(tails[:, :, 0:3], k.xp[:, :, T:T + 3]).then_inc(k.tails_ready, 1)
        dve.tensor_copy(tails[:, :, 3:27].rearrange("p f (b j) -> p f b j", j=3), k.xs[:, :, :, 4:7]).then_inc(k.tails_ready, 1)
        for r in range(4):
            b, free = full_bank(dve, k, ("tail", r))
            dve.tensor_copy(tail_rows[:, 512 * r:512 * r + 512], b[0:27, :]).then_inc(free, 1)


def stage_gates(nc, k, ctx):
    def sb(name, shape, dt=F32):
        return ctx.enter_context(nc.sbuf_tensor(name, shape, dt))
    e = sb("e", [AH, TA])
    b_sum = sb("b_sum", [AH, TA])
    a_max = sb("a_max", [AH, TA])
    m_tok = sb("m_tok", [AH, TA])
    rows = sb("rows", [96, TA])
    dif = sb("dif", [AH, TA])
    block = ctx.enter_context(nc.Block())
    ig, fg = k.gates[:, 0, :], k.gates[:, 1, :]

    def per_seq(t):
        return t.rearrange("p (b i) -> p b i", i=SI)

    @block.tensor
    def _(pe):
        pe.wait_ge(k.rows_ready, 1)
        pe.wait_ge(k.wrow_ready, 3)
        b, full = open_bank(pe, k, "cols")
        for i in range(NT + 1):
            n = 128 if i < NT else S
            m = pe.transpose(b[0:n, 96 * i:96 * i + 96], rows[:, 128 * i:128 * i + n], k.ident[0:96, 0:96])
        m.then_inc(full, 1)

    @block.vector
    def _(dve):
        st = Steps(dve, k.dve_step, k, "dve")
        st.then(dve.memset(rows[:, :], 0.0))
        dve.scalar_tensor_tensor(out=e[:, :], in0=fg, scalar=-1.0, in1=fg, op0=ALU.mult, op1=ALU.max).then_inc(k.absf_ready, 1)
        dve.wait_ge(k.softplus_ready, 2)
        st.then(dve.scalar_tensor_tensor(out=fg, in0=fg, scalar=0.0, in1=e[:, :], op0=ALU.min, op1=ALU.subtract))
        st.then(dve.tensor_tensor_scan(b_sum[:, :], k.scan_mul[:, :], fg, 0.0, ALU.mult, ALU.add))
        st.then(dve.tensor_tensor(ig, ig, b_sum[:, :], ALU.subtract))
        dve.tensor_copy(rows[0:AH, :], ig)
        st.then(dve.tensor_copy(e[:, :], ig))
        starts = per_seq(e[:, T:TA])[:, :, 0]
        dve.wait_ge(k.m0_here, 16)
        st.then(dve.tensor_tensor(starts, starts, k.m0[:, :], ALU.max))
        st.then(dve.tensor_tensor_scan(a_max[:, :], k.scan_add[:, :], e[:, :], NEG, ALU.add, ALU.max))
        dve.tensor_scalar(k.brow[:, 0:TA], a_max[:, :], -1.0, None, ALU.mult)
        last = per_seq(a_max[:, T:TA])[:, :, SI - 1]
        dve.tensor_tensor(per_seq(k.brow[:, TA:TA + S]), k.m0[:, :].unsqueeze(2).to_broadcast([AH, SB, SI]),
                          per_seq(a_max[:, T:TA]), ALU.subtract)
        dve.tensor_tensor(k.brow[:, TA + S:TA + S + SB], k.m0[:, :], last, ALU.subtract)
        dve.tensor_scalar(dif[:, 0:T], ig[:, 0:T], a_max[:, T - 1:T], None, ALU.subtract)
        dve.tensor_tensor(per_seq(dif[:, T:TA]), per_seq(ig[:, T:TA]), last.unsqueeze(2).to_broadcast([AH, SB, SI]), ALU.subtract)
        dve.tensor_tensor(m_tok[:, :], b_sum[:, :], a_max[:, :], ALU.add).then_inc(k.rows_ready, 1)
        b, free = full_bank(dve, k, "cols")
        dve.tensor_copy(k.cols[:, 0:NT, :], b[:, 0:96 * NT].rearrange("p (i c) -> p i c", c=96))
        dve.tensor_copy(k.cols[0:S, NT, :], b[0:S, 96 * NT:96 * NT + 96]).then_inc(free, 1)

    @block.scalar
    def _(act):
        act.wait_ge(k.absf_ready, 1)
        act.activation(e[:, :], e[:, :], ACT.Exp, scale=-1.0).then_inc(k.softplus_ready, 1)
        act.wait_ge(k.softplus_ready, 1)
        act.activation(e[:, :], e[:, :], ACT.Ln, bias=1.0).then_inc(k.softplus_ready, 1)
        act.wait_ge(k.rows_ready, 1)
        act.activation(k.brow[:, TA:TA + S + SB], k.brow[:, TA:TA + S + SB], ACT.Exp).then_inc(k.wrow_ready, 1)
        act.activation(rows[32:36, :], m_tok[:, :], ACT.Exp, scale=-1.0).then_inc(k.wrow_ready, 1)
        act.activation(rows[64:68, :], dif[:, :], ACT.Exp).then_inc(k.wrow_ready, 1)

    @block.sync
    def _(sp):
        sp.wait_ge(k.rows_ready, 1)
        sp.dma_start(k.o_mp[0, 0].unsqueeze(1), m_tok[:, T - 1:T]).then_inc(k.stored_m, 16)
        sp.dma_start(k.o_ms[0].rearrange("b h -> h b"), per_seq(m_tok[:, T:TA])[:, :, SI - 1],
                     allow_slow_non_contiguous=True).then_inc(k.stored_m, 16)
        sp.wait_ge(k.stored_m, 32)


COL_A, COL_EM, COL_W = 0, 32, 64
NCS = 3
K_BLOCKS = [[(0, 0), (0, 3), (1, 1)], [(1, 0), (0, 1), (1, 3)], [(0, 2), (1, 2)]]
V_BLOCKS = [[(0, 0), (0, 1), (0, 2)], [(1, 0), (0, 3), (1, 2)], [(1, 1), (1, 3)]]


def stage_cell(nc, k, ctx):
    def sb(name, shape, dt=F32):
        return ctx.enter_context(nc.sbuf_tensor(name, shape, dt))
    qT = sb("qT", [128, HF, TA])
    kT = sb("kT", [128, HF, TA])
    kw = sb("kw", [128, NT + 1, AD])
    vt = sb("vt", [128, NT + 1, AD])
    nb = sb("nb", [128, T])
    nbw = sb("nbw", [128, 2 * S + SB])
    nbd = sb("nbd", [128, NT, 128])
    nbds = sb("nbds", [S, S])
    num4 = sb("num4", [128, AD])
    qw = sb("qw", [128, HF, S])
    qm = sb("qm", [128, HF, SB, S])
    prod = sb("prod", [128, HF, S])
    pS = sb("pS", [S, S])
    kS = sb("kS", [128, 2, AD], BF16)
    vS = sb("vS", [128, 2, AD], BF16)
    kM = sb("kM", [128, 2, 2, AD], BF16)
    left = sb("left", [S, AD])
    cst = sb("cst", [128, 2, AD])
    nP = sb("nP", [128, AH * HF])
    stat = sb("stat", [128, NT, 6])
    mv = sb("mv", [128, NT, 2])
    rr = sb("rr", [128, 4, NT])
    ntmp = sb("ntmp", [128, HF, SB])
    nrows = sb("nrows", [128, 128])
    sden = sb("sden", [S, 1])
    nprow = sb("nprow", [AH * HF, 128])
    flat = k.wring[:, :, :].rearrange("p a b -> p (a b)")
    cs = flat[:, 0:NCS * HF * AD].rearrange("p (s f e) -> p s f e", s=NCS, f=HF)
    P = flat[:, NCS * HF * AD:(NCS + 1) * HF * AD].rearrange("p (j t) -> p j t", j=NT)
    acc = k.ps[:, NRING]
    block = ctx.enter_context(nc.Block())
    KSCALE = float(AD) ** -0.5

    def hn_of(h):
        return k.xrow[:, HF * h:HF * h + HF, :].rearrange("p f x -> p (f x)")[:, 0:NT * AD].rearrange("p (i e) -> p i e", i=NT)

    def nT_of(t, h):
        return t[:, :].rearrange("p (b h f) -> p h f b", b=SB, h=AH)[:, h]

    def tok(t, f, i):
        return t[:, f, 128 * i:128 * i + 128] if i < NT else t[:, f, T:TA]

    def sample_state(pe, h, s0, s1):
        if s0 == 0:
            pe.wait_ge(k.qm_ready, HF * (h + 1))
            if h:
                pe.wait_ge(k.acc_free, h)
        for s in range(s0, s1):
            u = SB * h + s
            pe.wait_ge(k.c_here[u % NCS], 16 * (u // NCS + 1))
            for ft in range(HF):
                m = pe.matmul(acc[32 * ft:32 * ft + 32, :], qm[:, ft, s, :], cs[:, u % NCS, ft, :],
                              start=s == 0, stop=s == SB - 1)
            if s == SB - 1:
                m.then_inc(k.acc_full, 1)
            pe.wait_ge(k.km_ready, u + 1)
            for ft in range(HF):
                b, full = open_bank(pe, k, ("up", h, s, ft))
                for c in range(2):
                    m = pe.matmul(b[:, :], kM[:, s % 2, c, 128 * ft:128 * ft + 128], vS[:, c, :], start=c == 0, stop=c == 1)
                m.then_inc(full, 1)

    def turn_samples(pe, h):
        pe.wait_ge(k.hn_ready, (NT + 1) * (h + 1))
        b, full = open_bank(pe, k, ("tr", h, NT))
        for ft in range(HF):
            m = pe.transpose(b[:, S * ft:S * ft + S], hn_of(h)[0:S, 0, 128 * ft:128 * ft + 128], k.ident[0:S, 0:S])
        m.then_inc(full, 1)

    def split(eng, st, src, dst, rest, blocks):
        for part in range(3):
            (c, b0), *more = blocks[part]
            first = dst[32 * b0:32 * b0 + 32, c, :]
            st.then(eng.tensor_copy(first, src))
            for c2, b2 in more:
                st.then(eng.tensor_copy(dst[32 * b2:32 * b2 + 32, c2, :], first))
            if part < 2:
                st.then(eng.tensor_tensor(rest, src, first, ALU.subtract))
                src = rest

    @block.tensor
    def _(pe):
        for h in range(AH):
            b, full = open_bank(pe, k, ("nm", h))
            pe.matmul(b[:, 0:T], k.headsel[:, h, :], k.brow[:, 0:T], start=True, stop=True).then_inc(full, 1)
            b, full = open_bank(pe, k, ("nw", h))
            pe.matmul(b[:, 0:2 * S + SB], k.headsel[:, h, :], k.brow[:, T:TA + S + SB], start=True, stop=True).then_inc(full, 1)
            pe.wait_ge(k.bd_ready, 12 + 3 * h + 3)
            for m3 in range(2):
                for ft in range(HF):
                    for hf, (t0, t1) in enumerate(HALF):
                        b, full = open_bank(pe, k, ("qk", h, m3, ft, hf))
                        pe.matmul(b[:, 0:t1 - t0], k.bd[:, m3, ft, :], k.xcT[:, HF * h + ft, t0:t1],
                                  start=True, stop=True).then_inc(full, 1)
            for i in range(NT + 1):
                n = 128 if i < NT else S
                b, full = open_bank(pe, k, ("ktok", h, i))
                for ft in range(HF):
                    m = pe.matmul(b[0:n, 128 * ft:128 * ft + 128], tok(k.xcT, HF * h + ft, i), k.bd[:, 1, ft, :],
                                  start=True, stop=True)
                m.then_inc(full, 1)
            for i in range(NT + 1):
                n = 128 if i < NT else S
                b, full = open_bank(pe, k, ("vtok", h, i))
                for ft in range(HF):
                    f = HF * h + ft
                    x = k.xp[:, f, 3 + 128 * i:131 + 128 * i] if i < NT else k.xms[:, f, :]
                    m = pe.matmul(b[0:n, 128 * ft:128 * ft + 128], x, k.bd[:, 2, ft, :], start=True, stop=True)
                m.then_inc(full, 1)
            drained(pe, k, ("qk", h, 1, HF - 1, 1))
            for j in range(NT):
                b, full = open_bank(pe, k, ("S", h, j))
                for ft in range(HF):
                    m = pe.matmul(b[:, 128 * j:T], kT[:, ft, 128 * j:128 * j + 128], qT[:, ft, 128 * j:T],
                                  start=ft == 0, stop=ft == HF - 1)
                m.then_inc(full, 1)
            b, full = open_bank(pe, k, ("Ss", h))
            for ft in range(HF):
                m = pe.matmul(b[0:S, 0:S], kT[:, ft, T:TA], qT[:, ft, T:TA], start=ft == 0, stop=ft == HF - 1)
            m.then_inc(full, 1)
            drained(pe, k, ("ktok", h, NT))
            drained(pe, k, ("vtok", h, NT))
            for ft in range(HF):
                if ft == 2:
                    sample_state(pe, h, 0, 1)
                b, full = open_bank(pe, k, ("Cp", h, ft))
                for j in range(NT):
                    m = pe.matmul(b[:, :], kw[:, j, 128 * ft:128 * ft + 128], vt[:, j, :], start=j == 0, stop=j == NT - 1)
                m.then_inc(full, 1)
            b, full = open_bank(pe, k, ("nn", h))
            for ft in range(HF):
                for j in range(NT):
                    pe.matmul(b[:, 9 * ft:9 * ft + 1], kw[:, j, 128 * ft:128 * ft + 128], k.ones[:, 0:1],
                              start=j == 0, stop=j == NT - 1)
                m = pe.matmul(b[:, 9 * ft + 1:9 * ft + 9], kw[0:S, NT, 128 * ft:128 * ft + 128], k.tmask[0:S, :],
                              start=True, stop=True)
            m.then_inc(full, 1)
            sample_state(pe, h, 1, 2)
            if h:
                turn_samples(pe, h - 1)
            sample_state(pe, h, 2, 4)
            pe.wait_ge(k.p_ready, 5 * h + 4)
            b, full = open_bank(pe, k, ("den", h))
            for i in range(NT):
                for j in range(i + 1):
                    m = pe.matmul(b[:, i:i + 1], P[:, j, 128 * i:128 * i + 128], k.ones[:, 0:1], start=j == 0, stop=j == i)
            m.then_inc(full, 1)
            for i in range(NT):
                b, full = open_bank(pe, k, ("num", h, i))
                for j in range(i + 1):
                    m = pe.matmul(b[:, :], P[:, j, 128 * i:128 * i + 128], vt[:, j, :], start=j == 0, stop=j == i)
                m.then_inc(full, 1)
            for i in range(NT):
                sample_state(pe, h, 4 + i, 5 + i)
                pe.wait_ge(k.hn_ready, (NT + 1) * h + i + 1)
                b, full = open_bank(pe, k, ("tr", h, i))
                for ft in range(HF):
                    m = pe.transpose(b[:, 128 * ft:128 * ft + 128], hn_of(h)[:, i, 128 * ft:128 * ft + 128], k.ident[:, :])
                m.then_inc(full, 1)
            pe.wait_ge(k.num4_ready, h + 1)
            b, full = open_bank(pe, k, ("nums", h))
            pe.matmul(b[0:S, :], k.fold[:, :], num4[:, :], start=True, stop=False)
            pe.wait_ge(k.p_ready, 5 * h + 5)
            pe.matmul(b[0:S, :], pS[:, :], vt[0:S, NT, :], start=False, stop=True).then_inc(full, 1)
            pe.wait_ge(k.prod_ready, h + 1)
            b, full = open_bank(pe, k, ("dens", h))
            for ft in range(HF):
                pe.matmul(b[0:S, 0:1], prod[:, ft, :], k.ones[:, 0:1], start=ft == 0, stop=False)
            pe.matmul(b[0:S, 0:1], pS[:, :], k.ones[0:S, 0:1], start=False, stop=True).then_inc(full, 1)
        turn_samples(pe, AH - 1)
        pe.wait_ge(k.n_ready, AH)
        b, full = open_bank(pe, k, "nrows")
        pe.transpose(b[:, 0:128], k.nT[:, :], k.ident[:, :])
        pe.transpose(b[0:16, 128:256], nP[:, :], k.ident[:, :]).then_inc(full, 1)

    @block.sync
    def _(sp):
        for u in range(AH * SB):
            h, s = u // SB, u % SB
            if u >= NCS:
                sp.wait_ge(k.c_stored[u % NCS], 16 * (u // NCS))
            sp.dma_start(cs[:, u % NCS, :, :], k.state_C[s, h].rearrange("(f p) e -> p f e", p=128)).then_inc(k.c_here[u % NCS], 16)

    @block.gpsimd
    def _(pool):
        ps = Steps(pool, k.pool_step, k, "pool")

        def store_state(u):
            for ft in range(HF):
                drained(pool, k, ("up", u // SB, u % SB, ft))
            pool.dma_start(k.o_cs[0, u % SB, u // SB].rearrange("(f p) e -> p f e", p=128),
                           cs[:, u % NCS, :, :]).then_inc(k.c_stored[u % NCS], 16)
        head_blocks(pool, k, 0)
        for h in range(AH):
            drained(pool, k, ("nw", h))
            pool.tensor_tensor(nbd[:, :, :], nb[:, :].rearrange("p (j t) -> p j t", j=NT),
                               k.maskT[:, :].unsqueeze(1).to_broadcast([128, NT, 128]), ALU.add).then_inc(k.nbd_ready, 1)
            pool.tensor_tensor(nbds[:, :], nbw[0:S, 0:S], k.maskS[:, :], ALU.add).then_inc(k.nbd_ready, 1)
            pool.wait_ge(k.qw_ready, h + 1)
            for ft in range(HF):
                pool.tensor_tensor(qm[:, ft, :, :], qw[:, ft, :].unsqueeze(1).to_broadcast([128, SB, S]),
                                   k.bmask[:, :, :], ALU.mult).then_inc(k.qm_ready, 1)
            drained(pool, k, ("vtok", h, NT))
            if h:
                bank, n = k.bank_of[("up", h - 1, SB - 1, HF - 1)]
                pool.wait_ge(k.bank_full[bank], n)
            split(pool, ps, vt[0:S, NT, :], vS, left[:, :], V_BLOCKS)
            pool.sem_inc(k.vs_ready, 1)
            if h + 1 < AH:
                bank, n = k.bank_of[("vtok", h, NT)]
                pool.wait_ge(k.bank_full[bank], n)
                head_blocks(pool, k, h + 1)
            drained(pool, k, ("ktok", h, NT))
            for ft in range(HF):
                f = HF * h + ft
                pool.tensor_scalar(k.xcT[:, f, :], k.xcT[:, f, :], k.vecs1[:, 96 + f:97 + f], None, ALU.mult).then_inc(k.skip_ready, 1)
            for ft in range(HF):
                pool.wait_ge(k.cst_ready, HF * h + ft + 1)
                pool.dma_start(k.o_cp[0, 0, h, 128 * ft:128 * ft + 128, :], cst[:, ft % 2, :]).then_inc(k.cst_stored[ft % 2], 16)
                if ft == 1:
                    store_state(SB * h)
            for s in range(1, SB):
                store_state(SB * h + s)
        drained(pool, k, "nrows")
        pool.dma_start(k.o_ns[0].rearrange("b h (f p) -> (b h f) p", p=128), nrows[:, :]).then_inc(k.stored_n, 16)
        pool.dma_start(k.o_np[0, 0].rearrange("h (f p) -> (h f) p", p=128), nprow[:, :]).then_inc(k.stored_n, 16)
        pool.wait_ge(k.stored_n, 32)
        for c in range(NCS):
            pool.wait_ge(k.c_stored[c], 16 * ((AH * SB - c + NCS - 1) // NCS))
        for c in range(2):
            pool.wait_ge(k.cst_stored[c], 16 * 2 * AH)

    @block.scalar
    def _(act):
        def mask(h, s):
            u = SB * h + s
            if u >= 2:
                bank, n = k.bank_of[("up", (u - 2) // SB, (u - 2) % SB, HF - 1)]
                act.wait_ge(k.bank_full[bank], n)
            act.activation(kM[:, s % 2, :, :], kS[:, :, :], ACT.Copy, scale=k.tmask[:, s:s + 1]).then_inc(k.km_ready, 1)

        def sample_deviation(h):
            act.wait_ge(k.var_ready, 2 * h + 2)
            act.activation(rr[0:S, 2, 0:1], rr[0:S, 1, 0:1], ACT.Sqrt).then_inc(k.sd_ready, 1)

        for h in range(AH):
            for m3, dst in ((0, qT), (1, kT)):
                for ft in range(HF):
                    for hf, (t0, t1) in enumerate(HALF):
                        b, free = full_bank(act, k, ("qk", h, m3, ft, hf))
                        act.activation(dst[:, ft, t0:t1], b[:, 0:t1 - t0], ACT.Copy, scale=1.0 if m3 == 0 else KSCALE).then_inc(free, 1)
            for i in range(NT + 1):
                n = 128 if i < NT else S
                b, free = full_bank(act, k, ("vtok", h, i))
                act.activation(vt[0:n, i, :], b[0:n, :], ACT.Copy).then_inc(free, 1)
            act.wait_ge(k.nbd_ready, 2 * h + 2)
            for j in range(NT):
                a = k.cols[:, j, COL_A + h:COL_A + h + 1]
                m = act.activation(P[:, j, 128 * j:128 * j + 128], nbd[:, j, :], ACT.Exp, bias=a)
                if j < NT - 1:
                    m = act.activation(P[:, j, 128 * j + 128:T], nb[:, 128 * j + 128:T], ACT.Exp, bias=a)
                m.then_inc(k.w_ready, 1)
            act.activation(pS[:, :], nbds[:, :], ACT.Exp, bias=k.cols[0:S, NT, COL_A + h:COL_A + h + 1]).then_inc(k.w_ready, 1)
            if h:
                sample_deviation(h - 1)
            act.wait_ge(k.ks_ready, h + 1)
            act.wait_ge(k.vs_ready, h + 1)
            mask(h, 0)
            mask(h, 1)
            for ft in range(HF):
                b, free = full_bank(act, k, ("Cp", h, ft))
                c = 2 * h + ft // 2
                if c:
                    act.wait_ge(k.cst_stored[ft % 2], 16 * c)
                act.activation(cst[:, ft % 2, :], b[:, :], ACT.Copy).then_inc(free, 1)
                drained(act, k, ("Cp", h, ft))
                act.sem_inc(k.cst_ready, 1)
            mask(h, 2)
            mask(h, 3)
            act.wait_ge(k.var_ready, 2 * h + 1)
            act.activation(rr[:, 2, :], rr[:, 1, :], ACT.Sqrt).then_inc(k.sd_ready, 1)
            for s in range(4, SB):
                mask(h, s)
            act.wait_ge(k.acc_full, h + 1)
            act.activation(num4[:, :], acc[:, :], ACT.Copy).then_inc(k.acc_free, 1)
            act.wait_ge(k.acc_free, h + 1)
            act.sem_inc(k.num4_ready, 1)
        sample_deviation(AH - 1)

    @block.vector
    def _(dve):
        st = Steps(dve, k.dve_step, k, "dve")
        def new_states(h, s0, s1):
            for s in range(s0, s1):
                u = SB * h + s
                for ft in range(HF):
                    b, free = full_bank(dve, k, ("up", h, s, ft))
                    c = cs[:, u % NCS, ft, :]
                    dve.scalar_tensor_tensor(out=c, in0=c, scalar=nbw[:, 2 * S + s:2 * S + s + 1], in1=b[:, :],
                                             op0=ALU.mult, op1=ALU.add).then_inc(free, 1)

        def mix(h, i):
            n = 128 if i < NT else S
            b, free = full_bank(dve, k, ("tr", h, i))
            for ft in range(HF):
                f = HF * h + ft
                m = dve.scalar_tensor_tensor(out=tok(k.xcT, f, i), in0=b[:, n * ft:n * ft + n], scalar=k.vecs1[:, 80 + f:81 + f],
                                             in1=tok(k.xcT, f, i), op0=ALU.mult, op1=ALU.add)
            m.then_inc(free, 1)

        def sample_variance(h):
            st.then(dve.bn_stats(stat[0:S, 0, :], hn_of(h)[0:S, 0, :]))
            st.then(dve.bn_aggr(mv[0:S, 0, :], stat[0:S, 0, :]))
            st.then(dve.tensor_scalar(rr[0:S, 0, 0:1], sden[:, :], -1.0, k.cols[0:S, NT, COL_EM + h:COL_EM + h + 1], ALU.mult, ALU.max))
            st.then(dve.tensor_tensor(rr[0:S, 0, 0:1], rr[0:S, 0, 0:1], sden[:, :], ALU.max))
            st.then(dve.reciprocal(rr[0:S, 0, 0:1], rr[0:S, 0, 0:1]))
            st.then(dve.tensor_tensor(rr[0:S, 1, 0:1], mv[0:S, 0, 1:2], rr[0:S, 0, 0:1], ALU.mult))
            st.then(dve.tensor_tensor(rr[0:S, 1, 0:1], rr[0:S, 1, 0:1], rr[0:S, 0, 0:1], ALU.mult))
            dve.tensor_scalar(rr[0:S, 1, 0:1], rr[0:S, 1, 0:1], EPS, None, ALU.add).then_inc(k.var_ready, 1)

        def sample_norm(h):
            dve.wait_ge(k.sd_ready, 2 * h + 2)
            st.then(dve.reciprocal(rr[0:S, 2, 0:1], rr[0:S, 2, 0:1]))
            st.then(dve.tensor_tensor(rr[0:S, 3, 0:1], rr[0:S, 2, 0:1], rr[0:S, 0, 0:1], ALU.mult))
            rows = hn_of(h)[0:S, 0, :]
            dve.tensor_scalar(rows, rows, mv[0:S, 0, 0:1], rr[0:S, 3, 0:1], ALU.subtract, ALU.mult).then_inc(k.hn_ready, 1)

        for h in range(AH):
            b, free = full_bank(dve, k, ("nm", h))
            dve.tensor_copy(nb[:, :], b[:, :]).then_inc(free, 1)
            b, free = full_bank(dve, k, ("nw", h))
            dve.tensor_copy(nbw[:, :], b[:, 0:2 * S + SB]).then_inc(free, 1)
            drained(dve, k, ("nw", h))
            drained(dve, k, ("qk", h, 0, HF - 1, 1))
            st.then(dve.tensor_tensor(qw[:, :, :], qT[:, :, T:TA], nbw[:, S:2 * S].unsqueeze(1).to_broadcast([128, HF, S]), ALU.mult))
            dve.sem_inc(k.qw_ready, 1)
            dve.tensor_tensor(prod[:, :, :].rearrange("p f (b i) -> p f b i", i=SI),
                              qw[:, :, :].rearrange("p f (b i) -> p f b i", i=SI),
                              nT_of(k.nT, h).unsqueeze(3).to_broadcast([128, HF, SB, SI]), ALU.mult).then_inc(k.prod_ready, 1)
            for i in range(NT + 1):
                n = 128 if i < NT else S
                b, free = full_bank(dve, k, ("ktok", h, i))
                dve.tensor_scalar(kw[0:n, i, :], b[0:n, :], KSCALE, k.cols[0:n, i, COL_W + h:COL_W + h + 1],
                                  ALU.mult, ALU.mult).then_inc(free, 1)
            drained(dve, k, ("ktok", h, NT))
            if h:
                dve.wait_ge(k.km_ready, SB * h)
            split(dve, st, kw[0:S, NT, :], kS, num4[0:S, :], K_BLOCKS)
            dve.wait_ge(k.dve_step, k.steps["dve"])
            dve.sem_inc(k.ks_ready, 1)
            if h:
                sample_variance(h - 1)
            for j in range(NT):
                dve.wait_ge(k.w_ready, 5 * h + j + 1)
                b, free = full_bank(dve, k, ("S", h, j))
                st.then(dve.tensor_tensor(P[:, j, 128 * j:T], P[:, j, 128 * j:T], b[:, 128 * j:T], ALU.mult))
                dve.sem_inc(free, 1)
                dve.sem_inc(k.p_ready, 1)
            dve.wait_ge(k.w_ready, 5 * h + 5)
            b, free = full_bank(dve, k, ("Ss", h))
            st.then(dve.tensor_tensor(pS[:, :], pS[:, :], b[0:S, 0:S], ALU.mult))
            dve.sem_inc(free, 1)
            dve.sem_inc(k.p_ready, 1)
            if h:
                sample_norm(h - 1)
            new_states(h, 0, 1)
            b, free = full_bank(dve, k, ("nn", h))
            nn = b[:, 0:9 * HF].rearrange("p (f c) -> p f c", c=9)
            dve.tensor_copy(nP[:, HF * h:HF * h + HF], nn[:, :, 0])
            dve.wait_ge(k.prod_ready, h + 1)
            st.then(dve.tensor_tensor(ntmp[:, :, :], nT_of(k.nT, h), nbw[:, 2 * S:2 * S + SB].unsqueeze(1).to_broadcast([128, HF, SB]), ALU.mult))
            st.then(dve.tensor_tensor(nT_of(k.nT, h), ntmp[:, :, :], nn[:, :, 1:9], ALU.add))
            dve.sem_inc(free, 1)
            dve.sem_inc(k.n_ready, 1)
            new_states(h, 1, 2)
            if h:
                mix(h - 1, NT)
            new_states(h, 2, 4)
            em = k.cols[:, 0:NT, COL_EM + h]
            b, free = full_bank(dve, k, ("den", h))
            st.then(dve.tensor_scalar(rr[:, 0, :], b[:, 0:NT], -1.0, None, ALU.mult))
            st.then(dve.tensor_tensor(rr[:, 0, :], rr[:, 0, :], b[:, 0:NT], ALU.max))
            dve.sem_inc(free, 1)
            st.then(dve.tensor_tensor(rr[:, 0, :], rr[:, 0, :], em, ALU.max))
            st.then(dve.reciprocal(rr[:, 0, :], rr[:, 0, :]))
            for i in range(NT):
                b, free = full_bank(dve, k, ("num", h, i))
                st.then(dve.bn_stats(stat[:, i, :], b[:, :]))
                st.then(dve.bn_aggr(mv[:, i, :], stat[:, i, :]))
            st.then(dve.tensor_tensor(rr[:, 1, :], mv[:, :, 1], rr[:, 0, :], ALU.mult))
            st.then(dve.tensor_tensor(rr[:, 1, :], rr[:, 1, :], rr[:, 0, :], ALU.mult))
            dve.tensor_scalar(rr[:, 1, :], rr[:, 1, :], EPS, None, ALU.add).then_inc(k.var_ready, 1)
            dve.wait_ge(k.sd_ready, 2 * h + 1)
            st.then(dve.reciprocal(rr[:, 2, :], rr[:, 2, :]))
            st.then(dve.tensor_tensor(rr[:, 3, :], rr[:, 2, :], rr[:, 0, :], ALU.mult))
            for i in range(NT):
                b, free = full_bank(dve, k, ("num", h, i))
                st.then(dve.tensor_scalar(hn_of(h)[:, i, :], b[:, :], mv[:, i, 0:1], rr[:, 3, i:i + 1], ALU.subtract, ALU.mult))
                dve.sem_inc(free, 1)
                dve.sem_inc(k.hn_ready, 1)
            dve.wait_ge(k.skip_ready, HF * (h + 1))
            for i in range(NT):
                new_states(h, 4 + i, 5 + i)
                mix(h, i)
            b, free = full_bank(dve, k, ("nums", h))
            dve.tensor_copy(hn_of(h)[0:S, 0, :], b[0:S, :]).then_inc(free, 1)
            b, free = full_bank(dve, k, ("dens", h))
            dve.tensor_copy(sden[:, :], b[0:S, 0:1]).then_inc(free, 1)
            drained(dve, k, ("nums", h))
            drained(dve, k, ("dens", h))
        sample_variance(AH - 1)
        sample_norm(AH - 1)
        mix(AH - 1, NT)
        b, free = full_bank(dve, k, "nrows")
        dve.tensor_copy(nrows[:, :], b[:, 0:128])
        dve.tensor_copy(nprow[:, :], b[0:16, 128:256]).then_inc(free, 1)


def stage_gate(nc, k, ctx):
    zt = ctx.enter_context(nc.sbuf_tensor("zt", [128, 4, 288], F32))
    block = ctx.enter_context(nc.Block())

    @block.tensor
    def _(pe):
        for c in range(4, 8):
            w = chunk(pe, k, CH_UP + c)
            for m4 in range(4):
                f = 4 * (c - 4) + m4
                for hf, (t0, t1) in enumerate(HALF):
                    b, full = open_bank(pe, k, ("z", f, hf))
                    for kt in range(KD):
                        m = pe.matmul(b[:, 0:t1 - t0], w[:, kt, 128 * m4:128 * m4 + 128], k.xnT[:, kt, t0:t1],
                                      start=kt == 0, stop=kt == KD - 1)
                    m.then_inc(full, 1)
            k.chunk_last[CH_UP + c] = k.bank_of[("z", f, 1)]

    @block.sync
    def _(sp):
        load_chunks(sp, k, CH_UP + 4, CH_DOWN + NW)

    @block.scalar
    def _(act):
        for u in range(2 * FT):
            f, hf = u // 2, u % 2
            n = HALF[hf][1] - HALF[hf][0]
            b, free = full_bank(act, k, ("z", f, hf))
            if u >= 4:
                act.wait_ge(k.gated, u - 3)
            act.activation(zt[:, u % 4, 0:n], b[:, 0:n], ACT.Silu).then_inc(free, 1)

    @block.vector
    def _(dve):
        for u in range(2 * FT):
            f, hf = u // 2, u % 2
            t0, t1 = HALF[hf]
            drained(dve, k, ("z", f, hf))
            dve.tensor_tensor(k.xcT[:, f, t0:t1], k.xcT[:, f, t0:t1], zt[:, u % 4, 0:t1 - t0], ALU.mult).then_inc(k.gated, 1)


def project_rows(pe, k, key, xT, c0, halves):
    banks = []
    for i in range(NT + 1):
        banks.append(open_bank(pe, k, (key, i)))
    for half in range(halves):
        w = chunk(pe, k, c0 + half)
        for i in range(NT + 1):
            n = 128 if i < NT else S
            b, full = banks[i]
            for kt in range(8):
                if i == NT and w.shape[2] == 512:
                    p0 = 32 * (kt % 4)
                    m = pe.matmul(b[p0:p0 + S, :], xT[:, 8 * half + kt, T:TA], w[:, kt, :],
                                  start=half == 0 and kt < 4, stop=half == halves - 1 and kt >= 4)
                    continue
                m = pe.matmul(b[0:n, 0:w.shape[2]], xT[:, 8 * half + kt, 128 * i:128 * i + n], w[:, kt, :],
                              start=half == 0 and kt == 0, stop=half == halves - 1 and kt == 7)
            if half == halves - 1:
                m.then_inc(full, 1)
        if half < halves - 1:
            m.then_inc(k.half_done, 1)
            k.halves += 1
            k.chunk_last[c0 + half] = ("half", k.halves)
        else:
            k.chunk_last[c0 + half] = k.bank_of[(key, NT)]


def fold(dve, k, st, key, out):
    b, free = full_bank(dve, k, (key, NT))
    st.then(dve.tensor_copy(out, b[0:S, :]))
    for j in range(1, 4):
        m = dve.tensor_tensor(out, out, b[32 * j:32 * j + S, :], ALU.add)
        if j < 3:
            st.then(m)
    m.then_inc(free, 1)


def norm_residual(k, dve, st, y, xr, npost, rstd_i, i):
    r = 128 if i < NT else S
    st.then(dve.scalar_tensor_tensor(out=y[0:r, i, :], in0=y[0:r, i, :], scalar=rstd_i, in1=npost[0:r, :],
                                     op0=ALU.mult, op1=ALU.mult))
    st.then(dve.tensor_tensor(xr[0:r, i, :], xr[0:r, i, :], y[0:r, i, :], ALU.add))
    dve.sem_inc(k.res_ready, 1)


class RowNorms:

    def __init__(self, k, keys, ssq, rstd, before):
        self.k, self.ssq, self.rstd, self.before = k, ssq, rstd, before
        self.no = {key: n + 1 for n, key in enumerate(keys)}

    def col(self, t, key):
        r = 128 if key[1] < NT else S
        n = self.no[key] - 1
        return t[0:r, n:n + 1]

    def square(self, act, key, src, junk):
        act.activation(junk, src, ACT.Square, accum_out=self.col(self.ssq, key)).then_inc(self.k.ssq_ready, 1)
        act.wait_ge(self.k.ssq_ready, self.before[0] + self.no[key])

    def mean(self, dve, key):
        dve.wait_ge(self.k.ssq_ready, self.before[0] + self.no[key])
        c = self.col(self.ssq, key)
        dve.tensor_scalar(c, c, 1.0 / D, EPS, ALU.mult, ALU.add).then_inc(self.k.ms_ready, 1)

    def root(self, act, key):
        act.wait_ge(self.k.ms_ready, self.before[1] + self.no[key])
        act.activation(self.col(self.rstd, key), self.col(self.ssq, key), ACT.Sqrt).then_inc(self.k.std_ready, 1)

    def invert(self, dve, st, key):
        dve.wait_ge(self.k.std_ready, self.before[1] + self.no[key])
        c = self.col(self.rstd, key)
        st.then(dve.reciprocal(c, c))
        return c


def stage_down(nc, k, ctx):
    def sb(name, shape, dt=F32):
        return ctx.enter_context(nc.sbuf_tensor(name, shape, dt))
    y = sb("y_down", [128, NT + 1, D])
    npost = sb("npost", [128, D])
    sq = sb("sq2", [128, D])
    ssq = sb("ssq2", [128, 2 * (NT + 1)])
    rstd = sb("rstd2", [128, 2 * (NT + 1)])
    x1 = k.x1
    block = ctx.enter_context(nc.Block())
    DK = D // 512
    norms = RowNorms(k, [("y", 0)] + [key for i in range(NT) for key in (("y", i + 1), ("x1", i))] + [("x1", NT)],
                     ssq, rstd, (NT + 1, 1))

    @block.tensor
    def _(pe):
        for n in range(DK):
            project_rows(pe, k, ("down", n), k.xcT, CH_DOWN + 2 * n, 2)
        pe.wait_ge(k.xn_tok, 2 * (NT + 1))
        for kt in range(KD):
            b, full = open_bank(pe, k, ("x1T", kt))
            for i in range(NT):
                m = pe.transpose(b[:, 128 * i:128 * i + 128], y[:, i, 128 * kt:128 * kt + 128], k.ident[:, :])
            m.then_inc(full, 1)
        b, full = open_bank(pe, k, "x1Ts")
        for kt in range(KD):
            m = pe.transpose(b[:, S * kt:S * kt + S], y[0:S, NT, 128 * kt:128 * kt + 128], k.ident[0:S, 0:S])
        m.then_inc(full, 1)

    @block.sync
    def _(sp):
        sp.dma_start(x1[:, 0:NT, :], k.x_prompt[0].rearrange("(i p) d -> p i d", p=128)).then_inc(k.x_here, 16)
        sp.dma_start(x1[0:S, NT, :], k.x_sample.rearrange("b i d -> (b i) d")).then_inc(k.x_here, 16)
        sp.dma_start(npost[:, :], k.a_norm_post.partition_broadcast(128)).then_inc(k.x_here, 16)
        load_chunks(sp, k, CH_DOWN + NW, CH_KV + NW)
        sp.wait_ge(k.res_ready, NT + 1)
        sp.dma_start(k.o_yp[0].rearrange("(i p) d -> p i d", p=128), x1[:, 0:NT, :]).then_inc(k.stored_x1, 16)
        sp.dma_start(k.o_ys.rearrange("b i d -> (b i) d"), x1[0:S, NT, :]).then_inc(k.stored_x1, 16)
        sp.wait_ge(k.stored_x1, 32)

    @block.scalar
    def _(act):
        def rows(t, i):
            return t[0:128 if i < NT else S, i, :]

        def tile(i):
            if i <= NT:
                norms.square(act, ("y", i), rows(y, i), sq[0:128 if i < NT else S, :])
            if i:
                act.wait_ge(k.res_ready, i)
                norms.square(act, ("x1", i - 1), rows(x1, i - 1), sq[0:128 if i - 1 < NT else S, :])
            if i <= NT:
                norms.root(act, ("y", i))
            if i:
                norms.root(act, ("x1", i - 1))

        for n in range(DK):
            for i in range(NT):
                b, free = full_bank(act, k, (("down", n), i))
                act.activation(y[:, i, 512 * n:512 * n + 512], b, ACT.Copy).then_inc(free, 1)
                if n == DK - 1:
                    drained(act, k, (("down", n), i))
                    tile(i)
        drained(act, k, (("down", 0), NT))
        drained(act, k, (("down", 1), NT))
        tile(NT)
        tile(NT + 1)
        for kt in range(1, KD, 2):
            b, free = full_bank(act, k, ("x1T", kt))
            act.activation(k.kvT[:, kt, 0:T], b[:, 0:T], ACT.Copy, scale=k.vecs2[:, 8 + kt:9 + kt])
            act.activation(k.xnT[:, kt, 0:T], b[:, 0:T], ACT.Copy, scale=k.vecs2[:, 16 + kt:17 + kt]).then_inc(free, 1)

    @block.vector
    def _(dve):
        st = Steps(dve, k.dve_step, k, "dve")
        fold(dve, k, st, ("down", 0), y[0:S, NT, 0:512])
        dve.wait_ge(k.x_here, 32 + 48)
        for i in range(NT + 2):
            if i == NT:
                fold(dve, k, st, ("down", 1), y[0:S, NT, 512:1024])
            if i <= NT:
                norms.mean(dve, ("y", i))
            if i:
                norms.mean(dve, ("x1", i - 1))
            if i <= NT:
                norm_residual(k, dve, st, y, x1, npost, norms.invert(dve, st, ("y", i)), i)
            if i:
                j = i - 1
                r = 128 if j < NT else S
                dve.tensor_scalar(y[0:r, j, :], x1[0:r, j, :], norms.invert(dve, st, ("x1", j)), None, ALU.mult).then_inc(k.xn_tok, 1)
        for kt in range(0, KD, 2):
            b, free = full_bank(dve, k, ("x1T", kt))
            dve.tensor_scalar(k.kvT[:, kt, 0:T], b[:, 0:T], k.vecs2[:, 8 + kt:9 + kt], None, ALU.mult)
            dve.tensor_scalar(k.xnT[:, kt, 0:T], b[:, 0:T], k.vecs2[:, 16 + kt:17 + kt], None, ALU.mult).then_inc(free, 1)
        b, free = full_bank(dve, k, "x1Ts")
        src = b[:, 0:KD * S].rearrange("p (a b) -> p a b", b=S)
        dve.tensor_tensor(k.kvT[:, :, T:TA], src, k.vecs2[:, 8:16].unsqueeze(2).to_broadcast([128, KD, S]), ALU.mult)
        dve.tensor_tensor(k.xnT[:, :, T:TA], src, k.vecs2[:, 16:24].unsqueeze(2).to_broadcast([128, KD, S]), ALU.mult).then_inc(free, 1)


def stage_kv(nc, k, ctx):
    kvt = ctx.enter_context(nc.sbuf_tensor("kvt", [128, 2, NT + 1, 2 * SLOT], F32))
    block = ctx.enter_context(nc.Block())

    @block.tensor
    def _(pe):
        for c in range(3):
            project_rows(pe, k, ("kv", c), k.kvT, CH_KV + c, 1)
            if c:
                for gp in range(2):
                    b, full = open_bank(pe, k, ("KT", c, gp))
                    for i in range(NT):
                        pe.wait_ge(k.kv_here, (NT + 1) * c + i + 1)
                        m = pe.transpose(b[:, 128 * i:128 * i + 128], kvt[:, c % 2, i, 128 * gp:128 * gp + 128], k.ident[:, :])
                    m.then_inc(full, 1)
                b, full = open_bank(pe, k, ("KTs", c))
                pe.wait_ge(k.kv_here, (NT + 1) * (c + 1))
                for gp in range(2):
                    m = pe.transpose(b[:, S * gp:S * gp + S], kvt[0:S, c % 2, NT, 128 * gp:128 * gp + 128], k.ident[0:S, 0:S])
                m.then_inc(full, 1)

    @block.sync
    def _(sp):
        load_chunks(sp, k, CH_KV + NW, CH_CMP + NW)

    @block.gpsimd
    def _(pool):
        for s in range(SB):
            pool.dma_start(k.o_ws[s, 0:512 - SI].rearrange("t a g d -> t (a g d)"),
                           k.cache_win[s, SI:512].rearrange("t a g d -> t (a g d)")).then_inc(k.stored_win, 16)
        for c in range(3):
            pool.wait_ge(k.kv_here, (NT + 1) * (c + 1))
            if c < 2:
                pool.dma_start(k.o_kvp[0].rearrange("(i p) s g d -> p i (s g d)", p=128)[:, :, 512 * c:512 * c + 512],
                               kvt[:, c % 2, 0:NT, :]).then_inc(k.stored_kv, 16)
                pool.dma_start(k.o_kvs.rearrange("b i s g d -> (b i) (s g d)")[:, 512 * c:512 * c + 512],
                               kvt[0:S, c % 2, NT, :]).then_inc(k.stored_kv, 16)
            else:
                pool.dma_start(k.o_wp[0].rearrange("(i p) s g d -> p i (s g d)", p=128), kvt[:, c % 2, 0:NT, :]).then_inc(k.stored_kv, 16)
                for s in range(SB):
                    pool.dma_start(k.o_ws[s, 512 - SI:512].rearrange("t a g d -> t (a g d)"),
                                   kvt[SI * s:SI * s + SI, c % 2, NT, :]).then_inc(k.stored_kv, 16)
            if c == 0:
                pool.wait_ge(k.stored_kv, 32)
                pool.sem_inc(k.kvt_free, 1)
        pool.wait_ge(k.stored_kv, 16 * (5 + SB))
        pool.wait_ge(k.stored_win, 16 * SB)

    @block.scalar
    def _(act):
        for c in range(3):
            if c == 2:
                act.wait_ge(k.kvt_free, 1)
            for i in range(NT + 1):
                if i < NT:
                    b, free = full_bank(act, k, (("kv", c), i))
                    act.activation(kvt[:, c % 2, i, :], b, ACT.Copy).then_inc(free, 1)
                drained(act, k, (("kv", c), i))
                act.sem_inc(k.kv_here, 1)

    @block.vector
    def _(dve):
        st = Steps(dve, k.dve_step, k, "dve")
        for c in range(3):
            if c == 2:
                dve.wait_ge(k.kvt_free, 1)
            fold(dve, k, st, ("kv", c), kvt[0:S, c % 2, NT, :])
            if c == 0:
                continue
            for gp in range(2):
                b, free = full_bank(dve, k, ("KT", c, gp))
                dve.tensor_copy(k.KT[:, c - 1, gp, 0:T], b[:, 0:T]).then_inc(free, 1)
            b, free = full_bank(dve, k, ("KTs", c))
            dve.tensor_copy(k.KT[:, c - 1, :, T:TA], b[:, 0:2 * S].rearrange("p (a b) -> p a b", b=S)).then_inc(free, 1)
            for i in range(NT + 1):
                r = 128 if i < NT else S
                dve.wait_ge(k.kv_here, (NT + 1) * c + i + 1)
                dve.tensor_copy(k.V[0:r, c - 1, i, :], kvt[0:r, c % 2, i, SLOT:2 * SLOT])


def stage_compress(nc, k, ctx):
    def sb(name, shape, dt=F32):
        return ctx.enter_context(nc.sbuf_tensor(name, shape, dt))
    NS = SB + 1
    pages = sb("pages", [1, SB * 4], I32)
    raw = sb("craw", [128, 2, 2, 2, 512])
    pair = sb("cpair", [128, 2, 2, G, 2, DH])
    R = sb("cR", [128, 2, 2, G, 256])
    
    hid = sb("chid", [128, 2, 2, 2, G * NCMP])
    w2 = sb("cw2", [128, 2, 2, DH])
    b2k = sb("cb2k", [128, 1])
    b2v = sb("cb2v", [NCMP, DH])
    posr = sb("posr", [32, 128])
    posT = sb("posT", [128, 32])
    pb = sb("cpb", [128, 4])
    block = ctx.enter_context(nc.Block())

    @block.tensor
    def _(pe):
        w1 = [chunk(pe, k, CH_CMP + s) for s in range(2)]
        pe.wait_ge(k.cw_here, 16 * 6)
        b, full = open_bank(pe, k, "posT")
        pe.transpose(b[:, 0:32], posr[:, :], k.ident[0:32, 0:32]).then_inc(full, 1)
        drained(pe, k, "posT")
        b, full = open_bank(pe, k, "pb")
        for s in range(2):
            for hh in range(2):
                for j in range(16):
                    m = pe.matmul(b[:, 2 * s + hh:2 * s + hh + 1], w1[s][:, j, 128 * hh:128 * hh + 128],
                                  posT[:, 16 * s + j:16 * s + j + 1], start=j == 0, stop=j == 15)
        m.then_inc(full, 1)
        def turn_pairs(q):
            pe.wait_ge(k.pair_ready, 2 * (q + 1))
            for s in range(2):
                for gp in range(2):
                    b, full = open_bank(pe, k, ("R", q, s, gp))
                    for g in range(2):
                        for j in range(2):
                            m = pe.transpose(b[:, 256 * g + 128 * j:256 * g + 128 * j + 128],
                                             pair[:, j, s, 2 * gp + g, :, :].rearrange("p a d -> p (a d)"), k.ident[:, :])
                    m.then_inc(full, 1)

        def hidden(q):
            for s in range(2):
                drained(pe, k, ("R", q, s, 0))
                drained(pe, k, ("R", q, s, 1))
                b, full = open_bank(pe, k, ("hid", q, s))
                for hh in range(2):
                    for j in range(16):
                        m = pe.matmul(b[:, G * NCMP * hh:G * NCMP * (hh + 1)].rearrange("p (g n) -> p g n", g=G),
                                      w1[s][:, j, 128 * hh:128 * hh + 128],
                                      R[:, q % 2, s, :, j:j + 8 * (NCMP - 1) + 1:8], start=j == 0, stop=j == 15)
                m.then_inc(full, 1)
            k.chunk_last[CH_CMP], k.chunk_last[CH_CMP + 1] = k.bank_of[("hid", q, 0)], k.bank_of[("hid", q, 1)]

        def output(q):
            drained(pe, k, ("hid", q, 1))
            drained(pe, k, ("hid", q, 0))
            b, full = open_bank(pe, k, ("kc", q))
            for g in range(G):
                p0 = 64 * (g % 2)
                for hh in range(2):
                    m = pe.matmul(b[p0:p0 + DH, NCMP * (g // 2):NCMP * (g // 2) + NCMP], w2[:, 0, hh, :],
                                  hid[:, q % 2, 0, hh, NCMP * g:NCMP * g + NCMP], start=hh == 0, stop=hh == 1)
            m.then_inc(full, 1)
            b, full = open_bank(pe, k, ("vc", q))
            for g in range(G):
                for hh in range(2):
                    m = pe.matmul(b[0:NCMP, DH * g:DH * g + DH], hid[:, q % 2, 1, hh, NCMP * g:NCMP * g + NCMP], w2[:, 1, hh, :],
                                  start=hh == 0, stop=hh == 1)
            m.then_inc(full, 1)

        turn_pairs(0)
        for q in range(NS):
            if q + 1 < NS:
                turn_pairs(q + 1)
            hidden(q)
            if q:
                output(q - 1)
        output(NS - 1)

    @block.sync
    def _(sp):
        sp.dma_start(pages[:, :], k.page_table.rearrange("b p -> (b p)").unsqueeze(0)).then_inc(k.pages_here, 16)
        sp.wait_ge(k.pages_here, 16)
        for q in range(NS):
            if q >= 2:
                sp.wait_ge(k.pair_ready, 2 * (q - 1))
            if q < SB:
                for pg in range(4):
                    page = sp.value_load(pages[0:1, 4 * q + pg:4 * q + pg + 1], min_val=0, max_val=k.cache_kv.shape[0] - 1)
                    src = k.cache_kv[bass.ds(page, 1)].rearrange("o (t a) s g d -> (o t) a (s g d)", a=2)[:, :, 0:512]
                    sp.dma_start(raw[64 * (pg % 2):64 * (pg % 2) + 64, q % 2, pg // 2, :, :], src).then_inc(k.raw_here[q % 2], 16)
            else:
                for j in range(2):
                    src = k.o_kvp[0, 256 * j:256 * j + 256].rearrange("(t a) s g d -> t a (s g d)", a=2)[:, :, 0:512]
                    sp.dma_start(raw[:, q % 2, j, :, :], src).then_inc(k.raw_here[q % 2], 32)
        load_chunks(sp, k, CH_CMP + NW, CH_IN + NW)

    @block.scalar
    def _(act):
        act.dma_start(posr[:, :], k.cmp_pos.rearrange("s (j a) d -> (s j) (a d)", a=2)).then_inc(k.cw_here, 16)
        act.dma_start(w2[:, 0, :, :], k.cmp_w2[0].rearrange("(h p) d -> p h d", p=128)).then_inc(k.cw_here, 16)
        act.dma_start(w2[:, 1, :, :], k.cmp_w2[1].rearrange("(h p) d -> p h d", p=128)).then_inc(k.cw_here, 16)
        act.dma_start(b2k[0:64, :], k.cmp_b2[0].unsqueeze(1)).then_inc(k.cw_here, 16)
        act.dma_start(b2k[64:128, :], k.cmp_b2[0].unsqueeze(1)).then_inc(k.cw_here, 16)
        act.dma_start(b2v[:, :], k.cmp_b2[1].partition_broadcast(NCMP)).then_inc(k.cw_here, 16)
        drained(act, k, "pb")
        for q in range(NS):
            for s in range(2):
                if q >= 2:
                    bank, n = k.bank_of[("vc" if s else "kc", q - 2)]
                    act.wait_ge(k.bank_full[bank], n)
                b, free = full_bank(act, k, ("hid", q, s))
                for hh in range(2):
                    m = act.activation(hid[:, q % 2, s, hh, :], b[:, G * NCMP * hh:G * NCMP * (hh + 1)], ACT.Silu,
                                       bias=pb[:, 2 * s + hh:2 * s + hh + 1])
                m.then_inc(free, 1)

    @block.vector
    def _(dve):
        dve.wait_ge(k.cw_here, 16 * 6)
        b, free = full_bank(dve, k, "posT")
        dve.tensor_copy(posT[:, :], b[:, 0:32]).then_inc(free, 1)
        b, free = full_bank(dve, k, "pb")
        dve.tensor_tensor(pb[:, :], b[:, 0:4], k.vecs2[:, 24:28], ALU.add).then_inc(free, 1)
        dve.memset(k.VBD[:, :, :], 0.0).then_inc(k.vbd_clear, 1)
        dve.wait_ge(k.vbd_clear, 1)

        def pairs(q):
            dve.wait_ge(k.raw_here[q % 2], 64 * (q // 2 + 1))
            if q:
                bank, n = k.bank_of[("R", q - 1, 1, 1)]
                dve.wait_ge(k.bank_full[bank], n)
            for s in range(2):
                src = raw[:, q % 2, :, :, 256 * s:256 * s + 256]
                for a in range(2):
                    m = dve.tensor_copy(pair[:, :, s, :, a, :], src[:, :, a, :].rearrange("p j (g d) -> p j g d", g=G))
                m.then_inc(k.pair_ready, 1)

        def keep_pairs(q):
            for s in range(2):
                if q >= 2:
                    bank, n = k.bank_of[("hid", q - 2, s)]
                    dve.wait_ge(k.bank_full[bank], n)
                for gp in range(2):
                    b, free = full_bank(dve, k, ("R", q, s, gp))
                    dve.tensor_copy(R[:, q % 2, s, 2 * gp:2 * gp + 2, :], b.rearrange("p (g t) -> p g t", g=2)).then_inc(free, 1)

        def keep_output(q):
            b, free = full_bank(dve, k, ("kc", q))
            dve.tensor_scalar(k.kcT[:, q, :, :], b[:, 0:2 * NCMP].rearrange("p (a n) -> p a n", a=2), b2k[:, :], None, ALU.add).then_inc(free, 1)
            b, free = full_bank(dve, k, ("vc", q))
            bias = b2v[:, :].unsqueeze(1).to_broadcast([NCMP, G, DH])
            src = b[0:NCMP, 0:SLOT].rearrange("p (g d) -> p g d", g=G)
            if q < SB:
                p0 = 32 * (q % 4)
                dve.tensor_tensor(k.vcS[p0:p0 + NCMP, q // 4, :].rearrange("p (g d) -> p g d", g=G), src, bias, ALU.add).then_inc(free, 1)
            else:
                for hh in range(HPG):
                    m = dve.tensor_tensor(k.VBD[32 * hh:32 * hh + NCMP, :, DH * hh:DH * hh + DH], src, bias, ALU.add)
                m.then_inc(free, 1)

        pairs(0)
        keep_pairs(0)
        pairs(1)
        for q in range(NS):
            if q + 1 < NS:
                keep_pairs(q + 1)
            if q + 2 < NS:
                pairs(q + 2)
            if q:
                keep_output(q - 1)
        keep_output(NS - 1)




def stage_query(nc, k, ctx):
    block = ctx.enter_context(nc.Block())
    SCALE = float(DH) ** -0.5

    @block.tensor
    def _(pe):
        for c in range(2):
            w = chunk(pe, k, CH_IN + c)
            for m4 in range(4):
                for hf, (t0, t1) in enumerate(HALF):
                    b, full = open_bank(pe, k, ("q", 4 * c + m4, hf))
                    for kt in range(KD):
                        m = pe.matmul(b[:, 0:t1 - t0], w[:, kt, 128 * m4:128 * m4 + 128], k.xnT[:, kt, t0:t1],
                                      start=kt == 0, stop=kt == KD - 1)
                    m.then_inc(full, 1)
            k.chunk_last[CH_IN + c] = k.bank_of[("q", 4 * c + 3, 1)]
        project_rows(pe, k, "bg", k.xnT, CH_IN + 2, 1)

    @block.sync
    def _(sp):
        load_chunks(sp, k, CH_IN + NW, CH_IN + 3 + NW)

    @block.gpsimd
    def _(pool):
        st = Steps(pool, k.pool_step, k, "pool")
        st.then(pool.memset(k.cmask[:, :, :], 0.0))
        st.then(pool.affine_select(out=k.cmask[:, :, :], in_=k.cmask[:, :, :], compare_op=ALU.is_ge, fill=NEG, base=-31,
                                   pattern=[[128, NT], [-16, 32]], channel_multiplier=1))
        st.then(pool.memset(k.mtmp[:, :], 0.0))
        st.then(pool.affine_select(out=k.mtmp[:, 0:128], in_=k.mtmp[:, 0:128], compare_op=ALU.is_ge, fill=NEG, base=0,
                                   pattern=[[-1, 128]], channel_multiplier=1))
        new = k.mtmp[0:32, 128:128 + SB * S].rearrange("p (b t) -> p b t", b=SB)
        st.then(pool.affine_select(out=new, in_=new, compare_op=ALU.is_ge, fill=NEG, base=0,
                                   pattern=[[-4, SB], [1, S]], channel_multiplier=0))
        st.then(pool.affine_select(out=new, in_=new, compare_op=ALU.is_ge, fill=NEG, base=0,
                                   pattern=[[16, SB], [-4, S]], channel_multiplier=1))
        old = k.mtmp[0:32, 128 + SB * S:132 + SB * S]
        st.then(pool.affine_select(out=old, in_=old, compare_op=ALU.is_ge, fill=NEG, base=-1,
                                   pattern=[[4, 4]], channel_multiplier=-1))
        pool.tensor_copy(k.identb[:, :], k.ident[:, :])
        pool.tensor_copy(k.causb[:, :], k.mtmp[:, 0:128])
        for g in range(G):
            st.then(pool.tensor_copy(k.newb[32 * g:32 * g + 32, :], k.mtmp[0:32, 128:132 + SB * S]))

    @block.scalar
    def _(act):
        act.wait_ge(k.q_clear, 3)
        for m in range(8):
            g = m // 2
            d0 = 64 * (g % 2)
            for hf in range(2):
                b, free = full_bank(act, k, ("q", m, hf))
                for a in range(2):
                    x = act.activation(k.Qp[d0:d0 + 64, 2 * m + a, 256 * hf:256 * hf + 256], b[64 * a:64 * a + 64, 0:256],
                                       ACT.Copy, scale=SCALE)
                    if hf:
                        hh = (2 * m + a) % HPG
                        x = act.activation(k.QS[d0:d0 + 64, :, g, hh:16:HPG],
                                           b[64 * a:64 * a + 64, 256:288].rearrange("p (b i) -> p b i", i=SI), ACT.Copy, scale=SCALE)
                x.then_inc(free, 1)
        for i in range(NT + 1):
            r = 128 if i < NT else S
            b, free = full_bank(act, k, ("bg", i))
            act.activation(k.gt[0:r, i, :], b[0:r, 0:3 * H], ACT.Sigmoid).then_inc(free, 1)

    @block.vector
    def _(dve):
        q = k.Qp[:, :, :].rearrange("p (a g h) t -> p a g (h t)", a=2, g=2)
        dve.memset(q[64:128, :, 0, :], 0.0).then_inc(k.q_clear, 1)
        dve.memset(q[0:64, :, 1, :], 0.0).then_inc(k.q_clear, 1)
        dve.memset(k.QS[:, :, :, :], 0.0).then_inc(k.q_clear, 1)


def z_rows(pe, k, br):
    for c in range(2):
        project_rows(pe, k, ("zb", br, c), k.xnT, CH_IN + 3 + 2 * br + c, 1)


def z_silu(act, k, br):
    for c in range(2):
        for i in range(NT):
            b, free = full_bank(act, k, (("zb", br, c), i))
            act.activation(k.z[:, i, 512 * c:512 * c + 512], b, ACT.Silu).then_inc(free, 1)
        drained(act, k, (("zb", br, c), NT))
        zs = k.z[0:S, NT + (br + 1) % 2, 512 * c:512 * c + 512]
        act.activation(zs, zs, ACT.Silu).then_inc(k.zs_ready, 1)


def z_fold(dve, k, st, br):
    for c in range(2):
        fold(dve, k, st, ("zb", br, c), k.z[0:S, NT + (br + 1) % 2, 512 * c:512 * c + 512])


def z_all(eng, k, br):
    for c in range(2):
        for i in range(NT):
            drained(eng, k, (("zb", br, c), i))


def blend(pool, k, st, br, tmp, z, y):
    if br == 0:
        st.then(pool.tensor_tensor(y, tmp, z, ALU.mult))
    else:
        st.then(pool.tensor_tensor(tmp, tmp, z, ALU.mult))
        st.then(pool.tensor_tensor(y, y, tmp, ALU.add))


def finish_samples(pool, k, st, br):
    pool.wait_ge(k.os_stored, 16 * SB * (br + 1))
    osall = k.osall
    for s in range(SB):
        pool.dma_start(osall[SI * s:SI * s + SI, :].rearrange("i (g x) -> i g x", g=G),
                       k.scratch[s].rearrange("(g i x) d -> i g (x d)", g=G, i=8)[0:SI]).then_inc(k.os_back, 16)
    pool.wait_ge(k.os_back, 16 * SB * (br + 1))
    st.then(pool.tensor_tensor(osall[:, :].rearrange("p (h d) -> p h d", h=H), osall[:, :].rearrange("p (h d) -> p h d", h=H),
                               k.gt[0:S, NT, H * br:H * br + H].unsqueeze(2).to_broadcast([S, H, DH]), ALU.mult))
    pool.wait_ge(k.zs_ready, 2 * (br + 1))
    blend(pool, k, st, br, osall[:, :], k.z[0:S, NT + (br + 1) % 2, :], k.y[0:S, NT, :])


def stage_cmp_branch(nc, k, ctx):
    def sb(name, shape, dt=F32):
        return ctx.enter_context(nc.sbuf_tensor(name, shape, dt))
    Sc = sb("Sc", [128, 2, H, 32])
    Pc = sb("Pc", [128, 2, H, 32])
    PcT = sb("PcT", [128, 2, 4, 128])
    mx = sb("cmx", [128, 2, H])
    sm = sb("csm", [128, 2, H])
    tmp = sb("ctmp", [128, 2, HPG * DH])
    osb = k.osb
    block = ctx.enter_context(nc.Block())
    k.og0 = k.og

    @block.tensor
    def _(pe):
        z_rows(pe, k, 0)
        for i in range(NT + 1):
            b, full = open_bank(pe, k, ("cS", i))
            if i < NT:
                for h in range(H):
                    m = pe.matmul(b[:, 32 * h:32 * h + NCMP], k.Qp[:, h, 128 * i:128 * i + 128], k.kcT[:, SB, h // 8, :],
                                  start=True, stop=True)
            else:
                for s in range(SB):
                    for g in range(G):
                        m = pe.matmul(b[32 * g:32 * g + 32, 32 * s:32 * s + NCMP], k.QS[:, s, g, :], k.kcT[:, s, g // 2, :],
                                      start=True, stop=True)
            m.then_inc(full, 1)
        for i in range(NT):
            pe.wait_ge(k.cp_ready, i + 1)
            b, full = open_bank(pe, k, ("cT", i))
            for g in range(G):
                m = pe.transpose(b[:, 128 * g:128 * g + 128], Pc[:, i % 2, 4 * g:4 * g + 4, :].rearrange("p h n -> p (h n)"), k.ident[:, :])
            m.then_inc(full, 1)
            drained(pe, k, ("cT", i))
            for g in range(G):
                o = G * i + g
                if k.og0 + o >= 2:
                    pe.wait_ge(k.o_free, k.og0 + o - 1)
                pe.matmul(k.ps[:, 6 + o % 2, 0:256], PcT[:, i % 2, g, :], k.VBD[:, g, :],
                          start=True, stop=True).then_inc(k.o_full, 1)
        pe.wait_ge(k.cp_ready, NT + 1)
        b, full = open_bank(pe, k, ("cT", NT))
        for a in range(2):
            m = pe.transpose(b[:, 128 * a:128 * a + 128], Pc[:, 0, 4 * a:4 * a + 4, :].rearrange("p h n -> p (h n)"), k.ident[:, :])
        m.then_inc(full, 1)
        drained(pe, k, ("cT", NT))
        for r in range(4):
            b, full = open_bank(pe, k, ("cO", r))
            for a in range(2):
                for g in range(G):
                    m = pe.matmul(b[32 * g:32 * g + 32, DH * a:DH * a + DH], PcT[32 * r:32 * r + NCMP, 0, a, 32 * g:32 * g + 32],
                                  k.vcS[32 * r:32 * r + NCMP, a, DH * g:DH * g + DH], start=True, stop=True)
            m.then_inc(full, 1)

    @block.sync
    def _(sp):
        load_chunks(sp, k, CH_IN + 3 + NW, CH_IN + 5 + NW)

    @block.scalar
    def _(act):
        z_silu(act, k, 0)
        for i in range(NT + 1):
            act.wait_ge(k.cs_ready, i + 1)
            if i < NT:
                src, dst = Sc[:, i % 2, :, :], Pc[:, i % 2, :, :]
            else:
                src, dst = Sc[:, 0, 0:SB, :], Pc[:, 0, 0:SB, :]
            act.activation(dst, src, ACT.Exp).then_inc(k.cp_ready, 1)

    @block.vector
    def _(dve):
        st = Steps(dve, k.dve_step, k, "dve")
        st.then(dve.memset(Sc[:, :, :, :], NEG))
        z_fold(dve, k, st, 0)

        def scores(i):
            b, free = full_bank(dve, k, ("cS", i))
            if i < NT:
                n, s_, m_ = H, Sc[:, i % 2, :, :], mx[:, i % 2, :]
                src = b.rearrange("p (h n) -> p h n", n=32)[:, :, 0:NCMP]
                st.then(dve.tensor_tensor(s_[:, :, 0:NCMP], src, k.cmask[:, i, 0:NCMP].unsqueeze(1).to_broadcast([128, H, NCMP]), ALU.add))
            else:
                n, s_, m_ = SB, Sc[:, 0, 0:SB, :], mx[:, 0, 0:SB]
                src = b[:, 0:32 * SB].rearrange("p (h n) -> p h n", n=32)[:, :, 0:NCMP]
                st.then(dve.tensor_copy(s_[:, :, 0:NCMP], src))
            dve.sem_inc(free, 1)
            st.then(dve.tensor_reduce(out=m_, in_=s_, axis=AX.X, op=ALU.max))
            st.then(dve.tensor_scalar(m_, m_, NEG / 10, None, ALU.max))
            dve.tensor_tensor(s_, s_, m_.unsqueeze(2).to_broadcast([128, n, 32]), ALU.subtract).then_inc(k.cs_ready, 1)

        def sums(i):
            dve.wait_ge(k.cp_ready, i + 1)
            if i < NT:
                p_, m_ = Pc[:, i % 2, :, :], sm[:, i % 2, :]
            else:
                p_, m_ = Pc[:, 0, 0:SB, :], sm[:, 0, 0:SB]
            st.then(dve.tensor_reduce(out=m_, in_=p_, axis=AX.X, op=ALU.add))
            st.then(dve.tensor_scalar(m_, m_, 1.0e-30, None, ALU.max))
            st.then(dve.reciprocal(m_, m_))
            if i < NT:
                st.then(dve.tensor_tensor(m_, m_, k.gt[:, i, 0:H], ALU.mult))
        scores(0)
        for i in range(NT):
            if i + 1 < NT:
                if i:
                    dve.wait_ge(k.cp_ready, i)
                scores(i + 1)
            sums(i)
            b, free = full_bank(dve, k, ("cT", i))
            if i >= 2:
                dve.wait_ge(k.o_full, k.og0 + G * (i - 1))
            dve.tensor_copy(PcT[:, i % 2, :, :], b.rearrange("p (g t) -> p g t", g=G)).then_inc(free, 1)
            for g in range(G):
                o = G * i + g
                dve.wait_ge(k.o_full, k.og0 + o + 1)
                if o >= 2:
                    dve.wait_ge(k.blended, k.og0 + o - 1)
                dve.tensor_tensor(tmp[:, o % 2, :].rearrange("p (h d) -> p h d", h=HPG),
                                  k.ps[:, 6 + o % 2, 0:256].rearrange("p (h d) -> p h d", h=HPG),
                                  sm[:, i % 2, 4 * g:4 * g + 4].unsqueeze(2).to_broadcast([128, HPG, DH]), ALU.mult).then_inc(k.o_free, 1)
        dve.wait_ge(k.cp_ready, NT)
        scores(NT)
        sums(NT)
        b, free = full_bank(dve, k, ("cT", NT))
        dve.wait_ge(k.o_full, k.og0 + G * (NT - 1))
        dve.tensor_copy(PcT[:, 0, 0:2, :], b[:, 0:256].rearrange("p (g t) -> p g t", g=2)).then_inc(free, 1)
        for r in range(4):
            b, free = full_bank(dve, k, ("cO", r))
            dve.tensor_tensor(osb[:, r:SB:4, :], b[:, 0:2 * DH].rearrange("p (a d) -> p a d", d=DH),
                              sm[:, 0, r:SB:4].unsqueeze(2).to_broadcast([128, 2, DH]), ALU.mult).then_inc(free, 1)

    @block.gpsimd
    def _(pool):
        st = Steps(pool, k.pool_step, k, "pool")
        z_all(pool, k, 0)
        for i in range(NT):
            for g in range(G):
                o = G * i + g
                pool.wait_ge(k.o_free, k.og0 + o + 1)
                blend(pool, k, st, 0, tmp[:, o % 2, :], k.z[:, i, 256 * g:256 * g + 256], k.y[:, i, 256 * g:256 * g + 256])
                pool.sem_inc(k.blended, 1)
        for r in range(4):
            drained(pool, k, ("cO", r))
        for s in range(SB):
            pool.dma_start(k.scratch[s], osb[:, s, :]).then_inc(k.os_stored, 16)
    k.og += G * NT


def stage_key_branch(nc, k, ctx, br):
    def sb(name, shape, dt=F32):
        return ctx.enter_context(nc.sbuf_tensor(f"{name}_{br}", shape, dt))
    TURN, MUL = 2, 4
    P = sb("P", [128, 3, T])
    PT = sb("PT", [128, 3, T])
    nmx = sb("nmx", [128, 4])
    sm = sb("sm", [128, NT, H])
    rc = sb("rc", [128, 2, HPG])
    tmp = sb("tmp", [128, 2, HPG * DH])
    sP = sb("sP", [128, TA])
    sPT = sb("sPT", [128, T + 128])
    snmx = sb("snmx", [128, 3])
    ss = sb("ss", [128, 3])
    KTs = sb("KTs", [128, 2, T])
    pages = sb("pages", [1, SB * 4], I32)
    raw = k.arena[:, (NT + 1) * D:(NT + 1) * D + 4096].rearrange("p (s r x) -> p s r x", s=2, r=4)
    block = ctx.enter_context(nc.Block())
    og0 = k.og
    items = [(i, h) for i in range(NT) for h in range(H)]
    NI = len(items)
    EVERY = NI // SB
    KEYS, SCORES, TURNS, VALUES = 0, 2, 4, 6
    v = br - 1

    def sequence(n, stage):
        return n // EVERY if n < NI and n % EVERY == stage else None
    max_no = {}
    for n in range(NI):
        max_no["A", n] = k.maxima + len(max_no) + 1
        if sequence(n, SCORES) is not None:
            max_no["sA", sequence(n, SCORES)] = k.maxima + len(max_no) + 1

    @block.tensor
    def _(pe):
        z_rows(pe, k, br)
        for n in range(NI + MUL):
            if n < NI:
                i, h = items[n]
                w = 128 * (i + 1)
                b, full = open_bank(pe, k, ("A", br, n))
                pe.matmul(b[:, 0:w], k.Qp[:, h, 128 * i:128 * i + 128], k.KT[:, v, h // 8, 0:w], start=True, stop=True)
                pe.matmul(b[:, w - 128:w], k.identb[:, :], k.causb[:, :], start=False, stop=True,
                          skip_group_check=True).then_inc(full, 1)
            s = sequence(n, KEYS)
            if s is not None:
                pe.wait_ge(k.raw_slot[s % 2], 16 * k.raw_need(br, s))
                for gp in range(2):
                    b, full = open_bank(pe, k, ("sK", br, s, gp))
                    for r in range(4):
                        m = pe.transpose(b[:, 128 * r:128 * r + 128], raw[:, s % 2, r, 128 * gp:128 * gp + 128], k.ident[:, :])
                    m.then_inc(full, 1)
            s = sequence(n, SCORES)
            if s is not None:
                drained(pe, k, ("sK", br, s, 0))
                drained(pe, k, ("sK", br, s, 1))
                b, full = open_bank(pe, k, ("sA", br, s))
                for g in range(G):
                    m = pe.matmul(b[32 * g:32 * g + 32, :], k.QS[:, s, g, :], KTs[:, g // 2, :], start=True, stop=True)
                if br == 2:
                    m = pe.matmul(b[:, 0:T:128], k.identb[:, :], k.newb[:, SB * S:SB * S + 4], start=False, stop=True,
                                  skip_group_check=True)
                m.then_inc(full, 1)
                b, full = open_bank(pe, k, ("sN", br, s))
                for g in range(G):
                    pe.matmul(b[32 * g:32 * g + 32, 0:S], k.QS[:, s, g, :], k.KT[:, v, g // 2, T:TA], start=True, stop=True)
                pe.matmul(b[:, 0:S], k.identb[:, :], k.newb[:, S * s:S * s + S], start=False, stop=True,
                          skip_group_check=True).then_inc(full, 1)
            s = sequence(n, TURNS)
            if s is not None:
                drained(pe, k, ("sA", br, s))
                drained(pe, k, ("sN", br, s))
                b, full = open_bank(pe, k, ("sT", br, s))
                for r in range(4):
                    m = pe.transpose(b[:, 128 * r:128 * r + 128], sP[:, 128 * r:128 * r + 128], k.ident[:, :])
                m.then_inc(full, 1)
                b, full = open_bank(pe, k, ("sTn", br, s))
                pe.transpose(b[0:S, 0:128], sP[:, T:TA], k.ident[:, :]).then_inc(full, 1)
            s = sequence(n, VALUES)
            if s is not None:
                drained(pe, k, ("sT", br, s))
                drained(pe, k, ("sTn", br, s))
                b, full = open_bank(pe, k, ("sO", br, s))
                for g in range(G):
                    for r in range(4):
                        pe.matmul(b[32 * g:32 * g + 32, 0:DH], sPT[:, 128 * r + 32 * g:128 * r + 32 * g + 32],
                                  raw[:, s % 2, r, SLOT + DH * g:SLOT + DH * g + DH], start=r == 0, stop=False)
                    m = pe.matmul(b[32 * g:32 * g + 32, 0:DH], sPT[0:S, T + 32 * g:T + 32 * g + 32],
                                  k.V[0:S, v, NT, DH * g:DH * g + DH], start=False, stop=True)
                m.then_inc(full, 1)
            if TURN <= n < NI + TURN:
                i, h = items[n - TURN]
                drained(pe, k, ("A", br, n - TURN))
                b, full = open_bank(pe, k, ("T", br, n - TURN))
                for j in range(i + 1):
                    m = pe.transpose(b[:, 128 * j:128 * j + 128], P[:, (n - TURN) % 3, 128 * j:128 * j + 128], k.ident[:, :])
                m.then_inc(full, 1)
            if n >= MUL:
                i, h = items[n - MUL]
                drained(pe, k, ("T", br, n - MUL))
                o, hh = (n - MUL) // HPG, (n - MUL) % HPG
                if hh == 0 and og0 + o >= 2:
                    pe.wait_ge(k.o_free, og0 + o - 1)
                g = h // HPG
                for j in range(i + 1):
                    m = pe.matmul(k.ps[:, 6 + o % 2, DH * hh:DH * hh + DH], PT[:, (n - MUL) % 3, 128 * j:128 * j + 128],
                                  k.V[:, v, j, DH * g:DH * g + DH], start=j == 0, stop=j == i)
                m.then_inc(k.pv_done, 1)

    @block.sync
    def _(sp):
        if br == 1:
            sp.dma_start(pages[:, :], k.page_table.rearrange("b p -> (b p)").unsqueeze(0)).then_inc(k.pages_here, 16)
            sp.wait_ge(k.pages_here, 32)
        for s in range(SB):
            if s == 2:
                load_chunks(sp, k, CH_IN + 3 + 2 * br + NW, CH_IN + 5 + 2 * br + NW)
            if s >= 2:
                bank, n = k.bank_of[("sO", br, s - 2)]
                sp.wait_ge(k.bank_full[bank], n)
            if br == 1:
                for pg in range(4):
                    page = sp.value_load(pages[0:1, 4 * s + pg:4 * s + pg + 1], min_val=0, max_val=k.cache_kv.shape[0] - 1)
                    src = k.cache_kv[bass.ds(page, 1)].rearrange("o (t r) s g d -> (o t) r (s g d)", r=4)[:, :, 2 * SLOT:4 * SLOT]
                    sp.dma_start(raw[32 * pg:32 * pg + 32, s % 2, :, :], src).then_inc(k.raw_slot[s % 2], 16)
            else:
                sp.dma_start(raw[:, s % 2, :, :], k.cache_win[s].rearrange("(t r) a g d -> t r (a g d)", r=4)).then_inc(k.raw_slot[s % 2], 16)

    @block.scalar
    def _(act):
        z_silu(act, k, br)
        for n in range(NI):
            i, h = items[n]
            w = 128 * (i + 1)
            act.wait_ge(k.mx_ready, max_no["A", n])
            b, free = full_bank(act, k, ("A", br, n))
            if n >= 3:
                bank, c = k.bank_of[("T", br, n - 3)]
                act.wait_ge(k.bank_full[bank], c)
            act.activation(P[:, n % 3, 0:w], b[:, 0:w], ACT.Exp, bias=nmx[:, n % 4:n % 4 + 1], accum_out=sm[:, i, h:h + 1]).then_inc(free, 1)
            s = sequence(n, SCORES)
            if s is not None:
                act.wait_ge(k.mx_ready, max_no["sA", s])
                if s:
                    bank, c = k.bank_of[("sTn", br, s - 1)]
                    act.wait_ge(k.bank_full[bank], c)
                if SB * v + s:
                    act.wait_ge(k.ss_used, SB * v + s)
                b, free = full_bank(act, k, ("sA", br, s))
                act.activation(sP[:, 0:T], b[:, :], ACT.Exp, bias=snmx[:, 2:3], accum_out=ss[:, 0:1]).then_inc(free, 1)
                b, free = full_bank(act, k, ("sN", br, s))
                act.activation(sP[:, T:TA], b[:, 0:S], ACT.Exp, bias=snmx[:, 2:3], accum_out=ss[:, 1:2]).then_inc(free, 1)

    @block.vector
    def _(dve):
        st = Steps(dve, k.dve_step, k, "dve")
        z_fold(dve, k, st, br)

        def maximum(n):
            i, h = items[n]
            b, _ = full_bank(dve, k, ("A", br, n))
            if n >= 4:
                drained(dve, k, ("A", br, n - 4))
            dve.tensor_reduce(out=nmx[:, n % 4:n % 4 + 1], in_=b[:, 0:128 * (i + 1)], axis=AX.X, op=ALU.max, negate=True).then_inc(k.mx_ready, 1)

        def keep(n):
            i, h = items[n]
            if n >= 3:
                dve.wait_ge(k.pv_done, NI * v + n - 2)
            b, free = full_bank(dve, k, ("T", br, n))
            dve.tensor_copy(PT[:, n % 3, 0:128 * (i + 1)], b[:, 0:128 * (i + 1)]).then_inc(free, 1)

        def out(o):
            i, g = o // G, o % G
            drained(dve, k, ("A", br, HPG * o + HPG - 1))
            st.then(dve.reciprocal(rc[:, o % 2, :], sm[:, i, HPG * g:HPG * g + HPG]))
            st.then(dve.tensor_tensor(rc[:, o % 2, :], rc[:, o % 2, :], k.gt[:, i, H * br + HPG * g:H * br + HPG * g + HPG], ALU.mult))
            dve.wait_ge(k.pv_done, NI * v + HPG * (o + 1))
            if o >= 2:
                dve.wait_ge(k.blended, og0 + o - 1)
            dve.tensor_tensor(tmp[:, o % 2, :].rearrange("p (h d) -> p h d", h=HPG),
                              k.ps[:, 6 + o % 2, 0:256].rearrange("p (h d) -> p h d", h=HPG),
                              rc[:, o % 2, :].unsqueeze(2).to_broadcast([128, HPG, DH]), ALU.mult).then_inc(k.o_free, 1)

        for n in range(NI + MUL + 1):
            if n < NI:
                maximum(n)
            s = sequence(n, KEYS)
            if s is not None:
                for gp in range(2):
                    b, free = full_bank(dve, k, ("sK", br, s, gp))
                    if s:
                        bank, c = k.bank_of[("sA", br, s - 1)]
                        dve.wait_ge(k.bank_full[bank], c)
                    dve.tensor_copy(KTs[:, gp, :], b[:, :]).then_inc(free, 1)
            s = sequence(n, SCORES)
            if s is not None:
                if s:
                    drained(dve, k, ("sN", br, s - 1))
                b, _ = full_bank(dve, k, ("sA", br, s))
                dve.tensor_reduce(out=snmx[:, 0:1], in_=b[:, :], axis=AX.X, op=ALU.max)
                b, _ = full_bank(dve, k, ("sN", br, s))
                st.then(dve.tensor_reduce(out=snmx[:, 1:2], in_=b[:, 0:S], axis=AX.X, op=ALU.max))
                dve.tensor_reduce(out=snmx[:, 2:3], in_=snmx[:, 0:2], axis=AX.X, op=ALU.max, negate=True).then_inc(k.mx_ready, 1)
            s = sequence(n, TURNS)
            if s is not None:
                if s:
                    bank, c = k.bank_of[("sO", br, s - 1)]
                    dve.wait_ge(k.bank_full[bank], c)
                b, free = full_bank(dve, k, ("sT", br, s))
                dve.tensor_copy(sPT[:, 0:T], b[:, :]).then_inc(free, 1)
                b, free = full_bank(dve, k, ("sTn", br, s))
                dve.tensor_copy(sPT[0:S, T:T + 128], b[0:S, 0:128]).then_inc(free, 1)
            s = sequence(n, VALUES)
            if s is not None:
                drained(dve, k, ("sN", br, s))
                st.then(dve.tensor_tensor(ss[:, 2:3], ss[:, 0:1], ss[:, 1:2], ALU.add))
                st.then(dve.reciprocal(ss[:, 2:3], ss[:, 2:3]))
                b, free = full_bank(dve, k, ("sO", br, s))
                st.then(dve.tensor_scalar(k.osb[:, s, :], b[:, 0:DH], ss[:, 2:3], None, ALU.mult))
                dve.sem_inc(free, 1)
                dve.sem_inc(k.ss_used, 1)
            if TURN <= n < NI + TURN:
                keep(n - TURN)
            if n > MUL and (n - MUL) % HPG == 0:
                out((n - MUL) // HPG - 1)

    @block.gpsimd
    def _(pool):
        st = Steps(pool, k.pool_step, k, "pool")
        finish_samples(pool, k, st, br - 1)
        z_all(pool, k, br)
        for o in range(NI // HPG):
            i, g = o // G, o % G
            pool.wait_ge(k.o_free, og0 + o + 1)
            blend(pool, k, st, br, tmp[:, o % 2, :], k.z[:, i, 256 * g:256 * g + 256], k.y[:, i, 256 * g:256 * g + 256])
            pool.sem_inc(k.blended, 1)
            if o % 2:
                s = o // 2
                drained(pool, k, ("sO", br, s))
                pool.dma_start(k.scratch[s], k.osb[:, s, :]).then_inc(k.os_stored, 16)
    k.og += NI // HPG
    k.maxima += NI + SB


def stage_out(nc, k, ctx):
    def sb(name, shape, dt=F32):
        return ctx.enter_context(nc.sbuf_tensor(name, shape, dt))
    yT = sb("yT", [128, KD, TA])
    yo = sb("yo", [128, NT + 1, D])
    xr = k.z[:, 0:NT + 1, :]
    npost = sb("npost2", [128, D])
    sq = sb("sq3", [128, D])
    ssq = sb("ssq3", [128, NT + 1])
    rstd = sb("rstd3", [128, NT + 1])
    norms = RowNorms(k, [("o", i) for i in range(NT + 1)], ssq, rstd, (3 * (NT + 1), 1 + 2 * (NT + 1)))
    block = ctx.enter_context(nc.Block())

    @block.tensor
    def _(pe):
        for kt in range(KD):
            b, full = open_bank(pe, k, ("yT", kt))
            for i in range(NT):
                m = pe.transpose(b[:, 128 * i:128 * i + 128], k.y[:, i, 128 * kt:128 * kt + 128], k.ident[:, :])
            m.then_inc(full, 1)
        pe.wait_ge(k.y_ready, 1)
        b, full = open_bank(pe, k, "yTs")
        for kt in range(KD):
            m = pe.transpose(b[:, S * kt:S * kt + S], k.y[0:S, NT, 128 * kt:128 * kt + 128], k.ident[0:S, 0:S])
        m.then_inc(full, 1)
        for kt in range(KD):
            drained(pe, k, ("yT", kt))
        drained(pe, k, "yTs")
        for n in range(D // 512):
            project_rows(pe, k, ("o", n), yT, CH_OUT + n, 1)

    @block.sync
    def _(sp):
        sp.dma_start(xr[:, 0:NT, :], k.o_yp[0].rearrange("(i p) d -> p i d", p=128)).then_inc(k.x_here, 16)
        sp.dma_start(xr[0:S, NT, :], k.o_ys.rearrange("b i d -> (b i) d")).then_inc(k.x_here, 16)
        sp.dma_start(npost[:, :], k.b_norm_post.partition_broadcast(128)).then_inc(k.x_here, 16)
        for i in range(NT + 1):
            sp.wait_ge(k.res_ready, NT + 1 + i + 1)
            if i < NT:
                sp.dma_start(k.o_yp[0, 128 * i:128 * i + 128, :], xr[:, i, :]).then_inc(k.stored_y, 16)
            else:
                sp.dma_start(k.o_ys.rearrange("b i d -> (b i) d"), xr[0:S, NT, :]).then_inc(k.stored_y, 16)
        sp.wait_ge(k.stored_y, 16 * (NT + 1))

    @block.scalar
    def _(act):
        for n in range(D // 512):
            for i in range(NT):
                b, free = full_bank(act, k, (("o", n), i))
                act.activation(yo[:, i, 512 * n:512 * n + 512], b, ACT.Copy).then_inc(free, 1)
                if n:
                    drained(act, k, (("o", n), i))
                    norms.square(act, ("o", i), yo[:, i, :], sq[:, :])
                    norms.root(act, ("o", i))
        drained(act, k, (("o", 0), NT))
        drained(act, k, (("o", 1), NT))
        norms.square(act, ("o", NT), yo[0:S, NT, :], sq[0:S, :])
        norms.root(act, ("o", NT))

    @block.gpsimd
    def _(pool):
        st = Steps(pool, k.pool_step, k, "pool")
        finish_samples(pool, k, st, 2)
        pool.sem_inc(k.y_ready, 1)

    @block.vector
    def _(dve):
        st = Steps(dve, k.dve_step, k, "dve")
        for kt in range(KD):
            b, free = full_bank(dve, k, ("yT", kt))
            dve.tensor_copy(yT[:, kt, 0:T], b[:, 0:T]).then_inc(free, 1)
        b, free = full_bank(dve, k, "yTs")
        dve.tensor_copy(yT[:, :, T:TA], b[:, 0:KD * S].rearrange("p (a b) -> p a b", b=S)).then_inc(free, 1)
        fold(dve, k, st, ("o", 0), yo[0:S, NT, 0:512])
        dve.wait_ge(k.x_here, 16 * 8)
        for i in range(NT + 1):
            if i == NT:
                fold(dve, k, st, ("o", 1), yo[0:S, NT, 512:1024])
            norms.mean(dve, ("o", i))
            norm_residual(k, dve, st, yo, xr, npost, norms.invert(dve, st, ("o", i)), i)


def stage_attention(nc, k, sb, ctx):
    k.raw_need = lambda br, s: (4 if br == 1 else 1) * (s // 2 + 1) + (0 if br == 1 else 16)
    k.nring = 6
    k.og = k.maxima = 0
    k.y = k.x1
    k.scratch = nc.dram_tensor("sample_rows", [SB, 128, DH], F32, kind="Internal").ap()
    k.gt = sb("gt", [128, NT + 1, 3 * H])
    k.z = sb("z", [128, NT + 2, ATT])
    k.osb = sb("osb", [128, SB, DH])
    k.osall = sb("osall", [S, ATT])
    with ExitStack() as att:
        k.Qp = sb("Qp", [128, H, T], where=att)
        k.QS = sb("QS", [128, SB, G, 32], where=att)
        k.cmask = sb("cmask", [128, NT, 32], where=att)
        k.identb = sb("identb", [128, 128], BF16, where=att)
        k.causb = sb("causb", [128, 128], BF16, where=att)
        k.newb = sb("newb", [128, SB * S + 4], BF16, where=att)
        with ExitStack() as c:
            k.mtmp = sb("mtmp", [128, 132 + SB * S], where=c)
            stage_query(nc, k, c)
        with ExitStack() as c:
            stage_cmp_branch(nc, k, c)
        for br in (1, 2):
            with ExitStack() as c:
                stage_key_branch(nc, k, c, br)
    with ExitStack() as c:
        stage_out(nc, k, c)


def build(nc, a, outs):
    k = Ctx()
    with ExitStack() as ctx:
        def sb(name, shape, dt=F32, where=ctx):
            return where.enter_context(nc.sbuf_tensor(name, shape, dt))

        def sem(name):
            return ctx.enter_context(nc.semaphore(name))
        k.x_prompt, k.x_sample, k.cache_kv, k.page_table, k.cache_win = (a[n] for n in (
            'x_prompt', 'x_sample', 'cache_kv', 'page_table', 'cache_win'))
        k.state_C, k.state_n, k.state_m, k.state_conv = (a[n][0] for n in ('state_C', 'state_n', 'state_m', 'state_conv'))
        k.a_norm_pre, k.w_up, k.conv_b, k.w_q, k.w_k, k.w_v, k.w_if, k.b_if, k.mh_w, k.skip, k.w_down, k.a_norm_post = (
            a[n][0] for n in ('a_norm_pre', 'a_w_up', 'a_conv_b', 'a_w_q', 'a_w_k', 'a_w_v', 'a_w_if', 'a_b_if',
                              'a_mh_w', 'a_skip', 'a_w_down', 'a_norm_post'))
        k.conv_w = a['a_conv_w'][0].rearrange("j c -> (j c)")
        k.kv_norm, k.w_kv, k.cmp_pos, k.cmp_w1, k.cmp_w2, k.cmp_b2 = (
            a[n] for n in ('kv_norm', 'w_kv', 'cmp_pos', 'cmp_w1', 'cmp_w2', 'cmp_b2'))
        k.cmp_b1 = a['cmp_b1'].rearrange("s n -> (s n)")
        k.b_norm_pre, k.w_in, k.w_out, k.b_norm_post = (a[n][0] for n in ('b_norm_pre', 'b_w_in', 'b_w_out', 'b_norm_post'))
        (k.o_yp, k.o_ys, k.o_kvp, k.o_kvs, k.o_wp, k.o_ws, k.o_cp, k.o_cs, k.o_np, k.o_ns, k.o_mp, k.o_ms,
         k.o_conv_p, k.o_conv_s) = outs
        k.o_conv_p, k.o_conv_s = k.o_conv_p[0, 0], k.o_conv_s[0]
        k.chunks = weight_chunks(k)
        k.ps = ctx.enter_context(nc.psum_tensor("ps", [128, 8, 512], F32))
        k.bank_full = [sem(f"bank_full{b}") for b in range(NRING)]
        k.bank_free = [sem(f"bank_free{b}") for b in range(NRING)]
        k.turns, k.bank_turns, k.bank_of, k.steps, k.chunk_last = 0, [0] * NRING, {}, {}, {}
        k.chunk_here = [sem(f"chunk_here{n}") for n in range(NW)]
        k.c_here = [sem(f"c_here{n}") for n in range(NCS)]
        k.c_stored = [sem(f"c_stored{n}") for n in range(NCS)]
        k.raw_here = [sem(f"raw_here{n}") for n in range(2)]
        k.raw_slot = [sem(f"raw_slot{n}") for n in range(2)]
        k.cst_stored = [sem(f"cst_stored{n}") for n in range(2)]
        k.x_here = sem("x_here")
        k.vec_here = sem("vec_here")
        k.ssq_clear = sem("ssq_clear")
        k.ssq_ready = sem("ssq_ready")
        k.ms_ready = sem("ms_ready")
        k.std_ready = sem("std_ready")
        k.xn_tok = sem("xn_tok")
        k.ident_ready = sem("ident_ready")
        k.pool_step = sem("pool_step")
        k.dve_step = sem("dve_step")
        k.act_step = sem("act_step")
        k.crow_here = sem("crow_here")
        k.wraw_here = sem("wraw_here")
        k.wif_here = sem("wif_here")
        k.bif_here = sem("bif_here")
        k.m0_here = sem("m0_here")
        k.nraw_here = sem("nraw_here")
        k.bd_ready = sem("bd_ready")
        k.pad_clear = sem("pad_clear")
        k.conv_ready = sem("conv_ready")
        k.xc_ready = sem("xc_ready")
        k.tails_ready = sem("tails_ready")
        k.stored = sem("stored")
        k.rows_ready = sem("rows_ready")
        k.wrow_ready = sem("wrow_ready")
        k.absf_ready = sem("absf_ready")
        k.softplus_ready = sem("softplus_ready")
        k.stored_m = sem("stored_m")
        k.p_ready = sem("p_ready")
        k.qm_ready = sem("qm_ready")
        k.acc_free = sem("acc_free")
        k.acc_full = sem("acc_full")
        k.km_ready = sem("km_ready")
        k.ks_ready = sem("ks_ready")
        k.vs_ready = sem("vs_ready")
        k.hn_ready = sem("hn_ready")
        k.num4_ready = sem("num4_ready")
        k.prod_ready = sem("prod_ready")
        k.n_ready = sem("n_ready")
        k.nbd_ready = sem("nbd_ready")
        k.qw_ready = sem("qw_ready")
        k.skip_ready = sem("skip_ready")
        k.cst_ready = sem("cst_ready")
        k.stored_n = sem("stored_n")
        k.w_ready = sem("w_ready")
        k.var_ready = sem("var_ready")
        k.sd_ready = sem("sd_ready")
        k.gated = sem("gated")
        k.half_done = sem("half_done")
        k.res_ready = sem("res_ready")
        k.stored_x1 = sem("stored_x1")
        k.kv_here = sem("kv_here")
        k.stored_win = sem("stored_win")
        k.stored_kv = sem("stored_kv")
        k.kvt_free = sem("kvt_free")
        k.cw_here = sem("cw_here")
        k.pair_ready = sem("pair_ready")
        k.pages_here = sem("pages_here")
        k.vbd_clear = sem("vbd_clear")
        k.q_clear = sem("q_clear")
        k.os_stored = sem("os_stored")
        k.os_back = sem("os_back")
        k.cp_ready = sem("cp_ready")
        k.cs_ready = sem("cs_ready")
        k.o_full = sem("o_full")
        k.o_free = sem("o_free")
        k.blended = sem("blended")
        k.pv_done = sem("pv_done")
        k.mx_ready = sem("mx_ready")
        k.ss_used = sem("ss_used")
        k.zs_ready = sem("zs_ready")
        k.y_ready = sem("y_ready")
        k.stored_y = sem("stored_y")
        k.wring = sb("wring", [128, NW, WCH])
        k.ident = sb("ident", [128, 128])
        k.ones = sb("ones", [128, 128])
        k.mask32 = sb("mask32", [128, 32])
        k.maskT = sb("maskT", [128, 128])
        k.maskS = sb("maskS", [S, S])
        k.bmask = sb("bmask", [128, SB, S])
        k.tmask = sb("tmask", [128, SB])
        k.fold = sb("fold", [128, S])
        k.vecs1 = sb("vecs1", [128, 112])
        k.vecs2 = sb("vecs2", [128, 28])
        k.xnT = sb("xnT", [128, KD, TA])
        k.arena = sb("arena", [128, (NT + 1) * D + KD * TA])
        k.x1 = k.arena[:, 0:(NT + 1) * D].rearrange("p (i d) -> p i d", d=D)
        k.kvT = k.arena[:, (NT + 1) * D:].rearrange("p (a t) -> p a t", t=TA)
        k.halves, k.nring = 0, NRING
        with ExitStack() as mlstm:
            k.scan_add = sb("scan_add", [AH, TA], where=mlstm)
            k.scan_mul = sb("scan_mul", [AH, TA], where=mlstm)
            k.headsel = sb("headsel", [AH, AH, 128], where=mlstm)
            with ExitStack() as c:
                stage_norm_in(nc, k, c)
            k.xcT = sb("xcT", [128, FT, TA], where=mlstm)
            with ExitStack() as cell:
                k.xrow = k.arena[:, 0:FT * XPW].rearrange("p (f x) -> p f x", x=XPW)
                k.xp = k.xrow[:, :, 0:XPS]
                k.xs = k.xrow[:, :, XPS:XPW].rearrange("p f (b j) -> p f b j", b=SB)
                k.xms = sb("xms", [128, FT, S], where=cell)
                k.wraw = sb("wraw", [128, 3, FT, 4], where=cell)
                k.bd = sb("bd", [128, 3, 4, 128], where=cell)
                k.bif = sb("bif", [36, 1], where=cell)
                k.m0 = sb("m0", [AH, SB], where=cell)
                k.nT = sb("nT", [128, 128], where=cell)
                k.gates = k.wring[0:AH, 0, 0:2 * TA].rearrange("p (a t) -> p a t", t=TA)
                with ExitStack() as c:
                    stage_up(nc, k, c)
                k.brow = sb("brow", [AH, TA + S + SB], where=cell)
                k.cols = sb("cols", [128, NT + 1, 96], where=cell)
                with ExitStack() as c:
                    stage_gates(nc, k, c)
                with ExitStack() as c:
                    stage_cell(nc, k, c)
            with ExitStack() as c:
                stage_gate(nc, k, c)
            with ExitStack() as c:
                stage_down(nc, k, c)
        k.V = sb("V", [128, 2, NT + 1, SLOT])
        k.KT = sb("KT", [128, 2, 2, TA])
        k.kcT = sb("kcT", [128, SB + 1, 2, NCMP])
        k.vcS = sb("vcS", [128, 2, SLOT])
        k.VBD = sb("VBD", [128, G, HPG * DH])
        with ExitStack() as c:
            stage_kv(nc, k, c)
        with ExitStack() as c:
            stage_compress(nc, k, c)
        stage_attention(nc, k, sb, ctx)


_INS = ['x_prompt', 'x_sample', 'cache_kv', 'page_table', 'cache_win', 'state_C', 'state_n', 'state_m', 'state_conv',
        'a_norm_pre', 'a_w_up', 'a_conv_w', 'a_conv_b', 'a_w_q', 'a_w_k', 'a_w_v', 'a_w_if', 'a_b_if', 'a_mh_w',
        'a_skip', 'a_w_down', 'a_norm_post', 'kv_norm', 'w_kv', 'cmp_pos', 'cmp_w1', 'cmp_b1', 'cmp_w2', 'cmp_b2',
        'b_norm_pre', 'b_w_in', 'b_w_out', 'b_norm_post']
_OUTS = [(1, 512, 1024), (8, 4, 1024), (1, 512, 4, 4, 64), (8, 4, 4, 4, 64), (1, 512, 2, 4, 64), (8, 512, 2, 4, 64),
         (1, 1, 4, 512, 512), (1, 8, 4, 512, 512), (1, 1, 4, 512), (1, 8, 4, 512), (1, 1, 4), (1, 8, 4),
         (1, 1, 3, 2048), (1, 8, 3, 2048)]


def kernel(**inputs):
    import numpy as _np
    import concourse.bacc as _bacc
    from concourse import mybir as _mybir
    from concourse.bass_utils import run_bass_kernel_spmd as _run

    nc = _bacc.Bacc("TRN2", target_bir_lowering=False, num_devices=1)
    arrays, ins, outs = {}, {}, []
    for name in _INS:
        a = _np.ascontiguousarray(inputs[name])
        arrays[f"in_{name}_dram"] = a
        ins[name] = nc.dram_tensor(f"in_{name}_dram", a.shape, _mybir.dt.from_np(a.dtype), kind="ExternalInput").ap()
    for i, shape in enumerate(_OUTS):
        outs.append(nc.dram_tensor(f"out_{i}_dram", shape, _mybir.dt.float32, kind="ExternalOutput").ap())
    build(nc, ins, outs)
    r = _run(nc, [arrays], core_ids=[0])
    return tuple(r.results[0][f"out_{i}_dram"] for i in range(len(_OUTS)))
```

```python
import concourse.bass as bass
from concourse import mybir
from contextlib import ExitStack

F32 = mybir.dt.float32
BF16 = mybir.dt.bfloat16
F32R = mybir.dt.float32r
I32 = mybir.dt.int32
ALU = mybir.AluOpType
ACT = mybir.ActivationFunctionType
AX = mybir.AxisListType

D = 1024
KD = D // 128
T = 512
NT = T // 128
SB, SI = 8, 4
S = SB * SI
TA = T + S
HALF = [(0, 256), (256, TA)]
INNER = 2048
FT = INNER // 128
AH, AD = 4, 512
HF = AD // 128
CONV = 4
XPW = CONV - 1 + T + SB * (CONV - 1 + SI)
XPS = CONV - 1 + T
H, DH, G = 16, 64, 4
HPG = H // G
ATT = H * DH
PAST = 512
SLOT = G * DH
NCMP = (T - 32) // 16 + 1
TILES = (NT,) + tuple(range(NT))
NEG = -1.0e30
EPS = 1e-6
NRING = 7
NW = 2
WCH = 8 * 512


class Ctx:
    pass


def weight_chunks(k):
    def cols(w, c0, n):
        return w[:, c0:c0 + n].rearrange("(kt p) n -> p kt n", p=128)
    out = [cols(k.w_up, 512 * c, 512) for c in range(8)]
    for n in range(2):
        for half in range(2):
            out.append(cols(k.w_down[1024 * half:1024 * half + 1024, :], 512 * n, 512))
    out += [cols(k.w_kv, 512 * c, 512) for c in range(3)]
    out += [k.cmp_w1[s].rearrange("(j p) n -> p j n", p=128) for s in range(2)]
    out += [cols(k.w_in, 0, 512), cols(k.w_in, 512, 512), cols(k.w_in, 4096, 48)]
    out += [cols(k.w_in, 512 * c, 512) for c in range(2, 8)]
    out += [cols(k.w_out, 512 * c, 512) for c in range(2)]
    return out


CH_UP, CH_DOWN, CH_KV, CH_CMP, CH_IN, CH_OUT, CH_END = 0, 8, 12, 15, 17, 26, 28


def load_chunks(sp, k, lo, hi):
    for c in range(lo, min(hi, CH_END)):
        src = k.chunks[c]
        n = src.shape[1] * src.shape[2]
        dst = k.wring[:, c % NW, 0:n].rearrange("p (a b) -> p a b", b=src.shape[2])
        if c >= NW:
            bank, n_full = k.chunk_last[c - NW]
            sp.wait_ge(k.half_done if bank == "half" else k.w_low if bank == "low" else k.bank_full[bank], n_full)
        sp.dma_start(dst, src).then_inc(k.chunk_here[c % NW], 16)


def chunk(pe, k, c):
    src = k.chunks[c]
    pe.wait_ge(k.chunk_here[c % NW], 16 * (c // NW + 1))
    n = src.shape[1] * src.shape[2]
    return k.wring[:, c % NW, 0:n].rearrange("p (a b) -> p a b", b=src.shape[2])


def open_bank(pe, k, key):
    bank = k.turns % k.nring
    k.turns += 1
    n = k.bank_turns[bank]
    if n:
        pe.wait_ge(k.bank_free[bank], n)
    k.bank_turns[bank] = n + 1
    k.bank_of[key] = (bank, n + 1)
    return k.ps[:, bank], k.bank_full[bank]


def full_bank(eng, k, key):
    bank, n = k.bank_of[key]
    eng.wait_ge(k.bank_full[bank], n)
    return k.ps[:, bank], k.bank_free[bank]


def drained(eng, k, key):
    bank, n = k.bank_of[key]
    eng.wait_ge(k.bank_free[bank], n)


class Steps:

    def __init__(self, eng, sem, k, name):
        self.eng, self.sem, self.k, self.name = eng, sem, k, name

    def then(self, ins):
        self.k.steps[self.name] = n = self.k.steps.get(self.name, 0) + 1
        ins.then_inc(self.sem, 1)
        self.eng.wait_ge(self.sem, n)


def head_blocks(pool, k, r):
    for m3 in range(3):
        pool.tensor_tensor(k.bd[:, m3, :, :].rearrange("p f (n d) -> p f n d", d=4),
                           k.wraw[:, m3, 4 * r:4 * r + 4, :].unsqueeze(2).to_broadcast([128, 4, 32, 4]),
                           k.mask32[:, :].unsqueeze(1).unsqueeze(3).to_broadcast([128, 4, 32, 4]),
                           ALU.mult).then_inc(k.bd_ready, 1)


class RowNorms:

    def __init__(self, k, keys, ssq, rstd, before):
        self.k, self.ssq, self.rstd, self.before = k, ssq, rstd, before
        self.no = {key: n + 1 for n, key in enumerate(keys)}

    def col(self, t, key):
        r = 128 if key[1] < NT else S
        n = self.no[key] - 1
        return t[0:r, n:n + 1]

    def square(self, act, key, src, junk):
        act.activation(junk, src, ACT.Square, accum_out=self.col(self.ssq, key)).then_inc(self.k.ssq_ready, 1)
        act.wait_ge(self.k.ssq_ready, self.before + self.no[key])

    def mean(self, dve, key):
        dve.wait_ge(self.k.ssq_ready, self.before + self.no[key])
        c = self.col(self.ssq, key)
        dve.tensor_scalar(c, c, 1.0 / D, EPS, ALU.mult, ALU.add).then_inc(self.k.ms_ready, 1)

    def root(self, act, key):
        act.wait_ge(self.k.ms_ready, self.before + self.no[key])
        act.activation(self.col(self.rstd, key), self.col(self.ssq, key), ACT.Sqrt).then_inc(self.k.std_ready, 1)

    def invert(self, dve, st, key):
        dve.wait_ge(self.k.std_ready, self.before + self.no[key])
        c = self.col(self.rstd, key)
        st.then(dve.reciprocal(c, c))
        return c


def stage_norm_in(nc, k, ctx):
    def sb(name, shape, dt=F32):
        return ctx.enter_context(nc.sbuf_tensor(name, shape, dt))
    xt = sb("xt", [128, NT + 1, D])
    sq = sb("sq_junk", [128, D])
    ssq = sb("ssq", [128, NT + 1])
    rstd = sb("rstd", [128, NT + 1])
    norms = RowNorms(k, [("x", i) for i in TILES], ssq, rstd, 0)
    v1raw = sb("v1raw", [112, 128])
    v2raw = sb("v2raw", [28, 128])
    block = ctx.enter_context(nc.Block())

    @block.tensor
    def _(pe):
        pe.wait_ge(k.ident_ready, 1)
        pe.wait_ge(k.vec_here, 8 * 16)
        for key, src, n in (("v1", v1raw, 112), ("v2", v2raw, 28)):
            b, full = open_bank(pe, k, key)
            pe.transpose(b[:, 0:n], src[:, :], k.ident[0:n, 0:n]).then_inc(full, 1)
        pe.wait_ge(k.xn_tok, NT + 1)
        for kt in range(KD):
            b, full = open_bank(pe, k, ("xT", kt))
            for i in range(NT):
                m = pe.transpose(b[:, 128 * i:128 * i + 128], xt[:, i, 128 * kt:128 * kt + 128], k.ident[:, :])
            m.then_inc(full, 1)
        b, full = open_bank(pe, k, "xTs")
        for kt in range(KD):
            m = pe.transpose(b[:, S * kt:S * kt + S], xt[0:S, NT, 128 * kt:128 * kt + 128], k.ident[0:S, 0:S])
        m.then_inc(full, 1)

    @block.sync
    def _(sp):
        sp.dma_start(xt[0:S, NT, :], k.x_sample.rearrange("b i d -> (b i) d")).then_inc(k.x_tile[NT], 16)
        for i in range(NT):
            sp.dma_start(xt[:, i, :], k.x_prompt[0, 128 * i:128 * i + 128, :]).then_inc(k.x_tile[i], 16)
        for j, (src, n) in enumerate([(k.conv_w, 4 * FT), (k.conv_b, FT), (k.mh_w, FT), (k.skip, FT)]):
            row = [0, 64, 80, 96][j]
            sp.dma_start(v1raw[row:row + n, :], src.rearrange("(a p) -> a p", p=128)).then_inc(k.vec_here, 16)
        for j, (src, n) in enumerate([(k.a_norm_pre, 8), (k.kv_norm, 8), (k.b_norm_pre, 8), (k.cmp_b1, 4)]):
            row = 8 * j
            sp.dma_start(v2raw[row:row + n, :], src.rearrange("(a p) -> a p", p=128)).then_inc(k.vec_here, 16)
        sp.dma_start(k.pages[:, :], k.page_table.rearrange("b p -> (b p)").unsqueeze(0)).then_inc(k.pages_here, 16)
        load_chunks(sp, k, 0, NW)

    @block.gpsimd
    def _(pool):
        st = Steps(pool, k.pool_step, k, "pool")

        def make(t, fill, *selects):
            st.then(pool.memset(t, fill))
            for value, op, base, pattern, cm in selects:
                st.then(pool.affine_select(out=t, in_=t, compare_op=op, fill=value, base=base,
                                           pattern=pattern, channel_multiplier=cm))
        make(k.ident[:, :], 0.0, (1.0, ALU.not_equal, 0, [[-1, 128]], 1))
        pool.memset(k.ones[:, :], 1.0).then_inc(k.ident_ready, 1)
        make(k.mask32[:, :], 1.0, (0.0, ALU.is_ge, 0, [[-4, 32]], 1), (0.0, ALU.is_ge, 3, [[4, 32]], -1))
        make(k.maskT[:, :], 0.0, (NEG, ALU.is_ge, 0, [[1, 128]], -1))
        make(k.maskS[:, :], 0.0, (NEG, ALU.is_ge, 0, [[4, SB], [1, SI]], -1), (NEG, ALU.is_ge, 0, [[-4, SB], [0, SI]], 1))
        make(k.bmask[:, :, :], 0.0, (1.0, ALU.not_equal, 0, [[1, SB], [-1, SB], [0, SI]], 0))
        make(k.tmask[0:S, :], 1.0, (0.0, ALU.is_ge, 0, [[-4, SB]], 1), (0.0, ALU.is_ge, 3, [[4, SB]], -1))
        for block32 in range(1, 4):
            st.then(pool.tensor_copy(k.tmask[32 * block32:32 * block32 + 32, :], k.tmask[0:S, :]))
        make(k.fold[:, :], 0.0, *[(1.0, ALU.not_equal, -32 * g, [[-1, S]], 1) for g in range(4)])
        make(k.headsel[:, :, :], 0.0, (1.0, ALU.not_equal, 0, [[-1, AH], [0, 128]], 1))
        st.then(pool.memset(k.scan_mul[:, :], 1.0))
        st.then(pool.memset(k.scan_mul[:, T:TA].rearrange("p (b i) -> p b i", i=SI)[:, :, 0:1], 0.0))
        st.then(pool.memset(k.scan_add[:, :], 0.0))
        st.then(pool.memset(k.scan_add[:, T:TA].rearrange("p (b i) -> p b i", i=SI)[:, :, 0:1], -1.0e38))

    @block.scalar
    def _(act):
        for n, i in enumerate(TILES):
            r = 128 if i < NT else S
            act.wait_ge(k.x_tile[i], 16)
            norms.square(act, ("x", i), xt[0:r, i, :], sq[0:r, :])
            if n:
                norms.root(act, ("x", TILES[n - 1]))
        norms.root(act, ("x", TILES[NT]))
        for kt in range(KD):
            b, free = full_bank(act, k, ("xT", kt))
            if kt == 0:
                drained(act, k, "v2")
            act.activation(k.xnT[:, kt, 0:T], b[:, 0:T], ACT.Copy, scale=k.vecs2[:, kt:kt + 1]).then_inc(free, 1)

    @block.vector
    def _(dve):
        st = Steps(dve, k.dve_step, k, "dve")
        for i in TILES:
            r = 128 if i < NT else S
            norms.mean(dve, ("x", i))
            rstd_i = norms.invert(dve, st, ("x", i))
            dve.tensor_scalar(xt[0:r, i, :], xt[0:r, i, :], rstd_i, None, ALU.mult).then_inc(k.xn_tok, 1)
        for key, dst, n in (("v1", k.vecs1, 112), ("v2", k.vecs2, 28)):
            b, free = full_bank(dve, k, key)
            dve.tensor_copy(dst[:, :], b[:, 0:n]).then_inc(free, 1)
        b, free = full_bank(dve, k, "xTs")
        dve.tensor_tensor(k.xnT[:, :, T:TA], b[:, 0:KD * S].rearrange("p (a b) -> p a b", b=S),
                          k.vecs2[:, 0:KD].unsqueeze(2).to_broadcast([128, KD, S]), ALU.mult).then_inc(free, 1)


def stage_up(nc, k, ctx):
    def sb(name, shape, dt=F32):
        return ctx.enter_context(nc.sbuf_tensor(name, shape, dt))
    wif = sb("wif", [128, 3 * FT, 8])
    crow = sb("crow", [27, INNER])
    convt = sb("convt", [128, 2, XPW])
    bdt = sb("bdt", [128, 3, FT // 4, 128])
    nraw = sb("nraw", [128, 128])
    wc = sb("wc", [128, 2 * FT, 36])
    tails = sb("tails", [128, FT, 27])
    tail_rows = crow
    block = ctx.enter_context(nc.Block())
    RUN = XPW - 3
    q4 = FT // 4

    @block.tensor
    def _(pe):
        drained(pe, k, ("xT", KD - 1))
        drained(pe, k, "xTs")

        def turn_blocks(r):
            pe.wait_ge(k.bd_ready, 3 * r + 3)
            for m3 in range(3):
                b, full = open_bank(pe, k, ("bdt", r, m3))
                for g in range(q4):
                    m = pe.transpose(b[:, 128 * g:128 * g + 128], k.bd[:, m3, g, :], k.ident[:, :])
                m.then_inc(full, 1)

        def gate_products(r):
            if r == 0:
                pe.wait_ge(k.wif_here, 16)
            b, full = open_bank(pe, k, ("wc", r))
            drained(pe, k, ("bdt", r, 2))
            for g in range(q4):
                f = q4 * r + g
                pe.matmul(b[:, 8 * g:8 * g + 8], bdt[:, 0, g, :], wif[:, f, :], start=True, stop=False)
                pe.matmul(b[:, 8 * g:8 * g + 8], bdt[:, 1, g, :], wif[:, FT + f, :], start=False, stop=True)
                m = pe.matmul(b[:, 32 + 8 * g:40 + 8 * g], bdt[:, 2, g, :], wif[:, 2 * FT + f, :], start=True, stop=True)
            m.then_inc(full, 1)

        for c in range(4):
            w = chunk(pe, k, CH_UP + c)
            for m4 in range(4):
                f = 4 * c + m4
                if c and m4 == 1:
                    gate_products(c - 1)
                if f == 3:
                    pe.wait_ge(k.crow_here, 16)
                    b, full = open_bank(pe, k, "cs")
                    for f2 in range(FT):
                        m = pe.transpose(b[:, 24 * f2:24 * f2 + 24], crow[0:24, 128 * f2:128 * f2 + 128], k.ident[0:24, 0:24])
                    m.then_inc(full, 1)
                    pe.wait_ge(k.nraw_here, 16)
                    b, full = open_bank(pe, k, "nT")
                    pe.transpose(b[:, 0:128], nraw[:, :], k.ident[:, :]).then_inc(full, 1)
                for hf, (t0, t1) in enumerate(HALF):
                    b, full = open_bank(pe, k, ("up", f, hf))
                    for kt in range(KD):
                        m = pe.matmul(b[:, 0:t1 - t0], w[:, kt, 128 * m4:128 * m4 + 128], k.xnT[:, kt, t0:t1],
                                      start=kt == 0, stop=kt == KD - 1)
                    m.then_inc(full, 1)
            k.chunk_last[CH_UP + c] = k.bank_of[("up", f, 1)]
            turn_blocks(c)
        gate_products(3)
        for r in range(4):
            drained(pe, k, ("wc", r))
        for hf, (t0, t1) in enumerate(HALF):
            b, full = open_bank(pe, k, ("gate", hf))
            pe.wait_ge(k.xc_ready, 1)
            pe.matmul(b[0:36, 0:t1 - t0], wc[:, 0, :], k.xcT[:, 0, t0:t1], start=True, stop=False)
            for f in range(FT):
                if hf == 0:
                    pe.matmul(b[0:36, 0:256], wc[:, FT + f, :], k.xp[:, f, 3:259], start=False, stop=False)
                else:
                    pe.matmul(b[0:36, 0:256], wc[:, FT + f, :], k.xp[:, f, 259:515], start=False, stop=False)
                    pe.matmul(b[0:36, 256:288].rearrange("p (b i) -> p b i", i=SI), wc[:, FT + f, :],
                              k.xs[:, f, :, 3:7], start=False, stop=False)
            for f in range(1, FT):
                if hf == 0:
                    pe.wait_ge(k.xc_ready, f + 1)
                m = pe.matmul(b[0:36, 0:t1 - t0], wc[:, f, :], k.xcT[:, f, t0:t1], start=False, stop=f == FT - 1)
            m.then_inc(full, 1)
        pe.wait_ge(k.tails_ready, 2)
        for r in range(4):
            b, full = open_bank(pe, k, ("tail", r))
            for g in range(4):
                m = pe.transpose(b[0:27, 128 * g:128 * g + 128], tails[:, 4 * r + g, :], k.ident[:, :])
            m.then_inc(full, 1)

    @block.sync
    def _(sp):
        load_chunks(sp, k, NW, CH_UP + 4)

    @block.gpsimd
    def _(pool):
        pool.dma_start(crow[0:24, :], k.state_conv.rearrange("b j c -> (b j) c")).then_inc(k.crow_here, 16)
        for m3, w in enumerate((k.w_q, k.w_k, k.w_v)):
            pool.dma_start(k.wraw[:, m3, :, :], w.rearrange("(f n) c d -> (n c) f d", f=FT)).then_inc(k.wraw_here, 16)
        pool.dma_start(wif[:, :, :], k.w_if.rearrange("(a p) j -> p a j", p=128)).then_inc(k.wif_here, 16)
        pool.dma_start(k.bif[0:4, :], k.b_if[0:4].unsqueeze(1)).then_inc(k.bif_here, 16)
        pool.dma_start(k.bif[32:36, :], k.b_if[4:8].unsqueeze(1)).then_inc(k.bif_here, 16)
        pool.dma_start(k.m0[:, :], k.state_m.rearrange("b h -> h b"), allow_slow_non_contiguous=True).then_inc(k.m0_here, 16)
        pool.dma_start(nraw[:, :], k.state_n.rearrange("b h (f p) -> (b h f) p", p=128)).then_inc(k.nraw_here, 16)
        pool.wait_ge(k.wraw_here, 48)
        for r in range(4):
            if r:
                drained(pool, k, ("bdt", r - 1, 2))
            head_blocks(pool, k, r)
        drained(pool, k, ("tail", 3))
        pool.dma_start(k.o_conv_p, tail_rows[0:3, :]).then_inc(k.stored, 16)
        pool.dma_start(k.o_conv_s.rearrange("b j c -> (b j) c"), tail_rows[3:27, :]).then_inc(k.stored, 16)
        pool.wait_ge(k.stored, 32)

    @block.scalar
    def _(act):
        act.wait_ge(k.pad_clear, 2)
        for f in range(FT + 1):
            if f < FT:
                for hf in range(2):
                    b, free = full_bank(act, k, ("up", f, hf))
                    m = act.activation(k.xp[:, f, 3 + 256 * hf:259 + 256 * hf], b[:, 0:256], ACT.Copy)
                    if hf == 1:
                        m = act.activation(k.xs[:, f, :, 3:7], b[:, 256:288].rearrange("p (b i) -> p b i", i=SI), ACT.Copy)
                    m.then_inc(free, 1)
            if f:
                act.wait_ge(k.conv_ready, f)
                act.activation(k.xcT[:, f - 1, 0:T], convt[:, (f - 1) % 2, 0:T], ACT.Silu)
                act.activation(k.xcT[:, f - 1, T:TA].rearrange("p (b i) -> p b i", i=SI),
                               convt[:, (f - 1) % 2, 515:515 + 7 * SB].rearrange("p (b j) -> p b j", j=7)[:, :, 0:SI],
                               ACT.Silu).then_inc(k.xc_ready, 1)

    @block.vector
    def _(dve):
        st = Steps(dve, k.dve_step, k, "dve")
        dve.memset(k.xp[:, :, 0:3], 0.0).then_inc(k.pad_clear, 1)
        dve.memset(wc[:, :, :], 0.0).then_inc(k.pad_clear, 1)
        b, free = full_bank(dve, k, "cs")
        dve.tensor_copy(k.xs[:, :, :, 0:3], b[:, 0:24 * FT].rearrange("p (f b j) -> p f b j", b=SB, j=3)).then_inc(free, 1)
        dve.wait_ge(k.pad_clear, 2)
        drained(dve, k, "cs")
        b, free = full_bank(dve, k, "nT")
        dve.tensor_copy(k.nT[:, :], b[:, 0:128]).then_inc(free, 1)

        def conv(f):
            drained(dve, k, ("up", f, 1))
            if f >= 2:
                dve.wait_ge(k.xc_ready, f - 1)
            row = k.xrow[:, f, :]
            out = convt[:, f % 2, 0:RUN]
            st.then(dve.tensor_scalar(out, row[:, 0:RUN], k.vecs1[:, f:f + 1], k.vecs1[:, 64 + f:65 + f], ALU.mult, ALU.add))
            for j in range(1, 4):
                m = dve.scalar_tensor_tensor(out=out, in0=row[:, j:j + RUN], scalar=k.vecs1[:, 16 * j + f:16 * j + f + 1],
                                             in1=out, op0=ALU.mult, op1=ALU.add)
                if j < 3:
                    st.then(m)
                else:
                    m.then_inc(k.conv_ready, 1)

        def keep_blocks(r):
            for m3 in range(3):
                if r and m3 == 0:
                    bank, n = k.bank_of[("wc", r - 1)]
                    dve.wait_ge(k.bank_full[bank], n)
                b, free = full_bank(dve, k, ("bdt", r, m3))
                dve.tensor_copy(bdt[:, m3, :, :], b.rearrange("p (g c) -> p g c", c=128)).then_inc(free, 1)

        def keep_gate_weights(r):
            b, free = full_bank(dve, k, ("wc", r))
            for part in range(2):
                src = b[:, 32 * part:32 * part + 32].rearrange("p (g j) -> p g j", j=8)
                rows = wc[:, FT * part + q4 * r:FT * part + q4 * r + q4, :]
                dve.tensor_copy(rows[:, :, 0:4], src[:, :, 0:4])
                m = dve.tensor_copy(rows[:, :, 32:36], src[:, :, 4:8])
            m.then_inc(free, 1)
        for f in range(FT):
            conv(f)
            if f % 4 == 3:
                keep_blocks(f // 4)
            if f % 4 == 0 and f:
                keep_gate_weights(f // 4 - 1)
        keep_gate_weights(3)
        dve.wait_ge(k.bif_here, 32)
        for hf, (t0, t1) in enumerate(HALF):
            b, free = full_bank(dve, k, ("gate", hf))
            dve.tensor_scalar(k.gates[:, 0, t0:t1], b[0:4, 0:t1 - t0], k.bif[0:4, :], None, ALU.add)
            dve.tensor_scalar(k.gates[:, 1, t0:t1], b[32:36, 0:t1 - t0], k.bif[32:36, :], None, ALU.add).then_inc(free, 1)
        dve.tensor_copy(k.xms[:, :, :].rearrange("p f (b i) -> p f b i", i=SI), k.xs[:, :, :, 3:7])
        dve.tensor_copy(tails[:, :, 0:3], k.xp[:, :, T:T + 3]).then_inc(k.tails_ready, 1)
        dve.tensor_copy(tails[:, :, 3:27].rearrange("p f (b j) -> p f b j", j=3), k.xs[:, :, :, 4:7]).then_inc(k.tails_ready, 1)
        for r in range(4):
            b, free = full_bank(dve, k, ("tail", r))
            dve.tensor_copy(tail_rows[:, 512 * r:512 * r + 512], b[0:27, :]).then_inc(free, 1)


def stage_gates(nc, k, ctx):
    def sb(name, shape, dt=F32):
        return ctx.enter_context(nc.sbuf_tensor(name, shape, dt))
    e = sb("e", [AH, TA])
    b_sum = sb("b_sum", [AH, TA])
    a_max = sb("a_max", [AH, TA])
    m_tok = sb("m_tok", [AH, TA])
    rows = sb("rows", [96, TA])
    dif = sb("dif", [AH, TA])
    block = ctx.enter_context(nc.Block())
    ig, fg = k.gates[:, 0, :], k.gates[:, 1, :]

    def per_seq(t):
        return t.rearrange("p (b i) -> p b i", i=SI)

    @block.tensor
    def _(pe):
        pe.wait_ge(k.rows_ready, 1)
        pe.wait_ge(k.wrow_ready, 3)
        b, full = open_bank(pe, k, "cols")
        for i in range(NT + 1):
            n = 128 if i < NT else S
            m = pe.transpose(b[0:n, 96 * i:96 * i + 96], rows[:, 128 * i:128 * i + n], k.ident[0:96, 0:96])
        m.then_inc(full, 1)

    @block.vector
    def _(dve):
        st = Steps(dve, k.dve_step, k, "dve")
        st.then(dve.memset(rows[:, :], 0.0))
        dve.scalar_tensor_tensor(out=e[:, :], in0=fg, scalar=-1.0, in1=fg, op0=ALU.mult, op1=ALU.max).then_inc(k.absf_ready, 1)
        dve.wait_ge(k.softplus_ready, 2)
        st.then(dve.scalar_tensor_tensor(out=fg, in0=fg, scalar=0.0, in1=e[:, :], op0=ALU.min, op1=ALU.subtract))
        st.then(dve.tensor_tensor_scan(b_sum[:, :], k.scan_mul[:, :], fg, 0.0, ALU.mult, ALU.add))
        st.then(dve.tensor_tensor(ig, ig, b_sum[:, :], ALU.subtract))
        dve.tensor_copy(rows[0:AH, :], ig)
        st.then(dve.tensor_copy(e[:, :], ig))
        starts = per_seq(e[:, T:TA])[:, :, 0]
        dve.wait_ge(k.m0_here, 16)
        st.then(dve.tensor_tensor(starts, starts, k.m0[:, :], ALU.max))
        st.then(dve.tensor_tensor_scan(a_max[:, :], k.scan_add[:, :], e[:, :], NEG, ALU.add, ALU.max))
        dve.tensor_scalar(k.brow[:, 0:TA], a_max[:, :], -1.0, None, ALU.mult)
        last = per_seq(a_max[:, T:TA])[:, :, SI - 1]
        dve.tensor_tensor(per_seq(k.brow[:, TA:TA + S]), k.m0[:, :].unsqueeze(2).to_broadcast([AH, SB, SI]),
                          per_seq(a_max[:, T:TA]), ALU.subtract)
        dve.tensor_tensor(k.brow[:, TA + S:TA + S + SB], k.m0[:, :], last, ALU.subtract)
        dve.tensor_scalar(dif[:, 0:T], ig[:, 0:T], a_max[:, T - 1:T], None, ALU.subtract)
        dve.tensor_tensor(per_seq(dif[:, T:TA]), per_seq(ig[:, T:TA]), last.unsqueeze(2).to_broadcast([AH, SB, SI]), ALU.subtract)
        dve.tensor_tensor(m_tok[:, :], b_sum[:, :], a_max[:, :], ALU.add).then_inc(k.rows_ready, 1)
        b, free = full_bank(dve, k, "cols")
        dve.tensor_copy(k.cols[:, 0:NT, :], b[:, 0:96 * NT].rearrange("p (i c) -> p i c", c=96))
        dve.tensor_copy(k.cols[0:S, NT, :], b[0:S, 96 * NT:96 * NT + 96]).then_inc(free, 1)

    @block.scalar
    def _(act):
        act.wait_ge(k.absf_ready, 1)
        act.activation(e[:, :], e[:, :], ACT.Exp, scale=-1.0).then_inc(k.softplus_ready, 1)
        act.wait_ge(k.softplus_ready, 1)
        act.activation(e[:, :], e[:, :], ACT.Ln, bias=1.0).then_inc(k.softplus_ready, 1)
        act.wait_ge(k.rows_ready, 1)
        act.activation(k.brow[:, TA:TA + S + SB], k.brow[:, TA:TA + S + SB], ACT.Exp).then_inc(k.wrow_ready, 1)
        act.activation(rows[32:36, :], m_tok[:, :], ACT.Exp, scale=-1.0).then_inc(k.wrow_ready, 1)
        act.activation(rows[64:68, :], dif[:, :], ACT.Exp).then_inc(k.wrow_ready, 1)

    @block.sync
    def _(sp):
        sp.wait_ge(k.rows_ready, 1)
        sp.dma_start(k.o_mp[0, 0].unsqueeze(1), m_tok[:, T - 1:T]).then_inc(k.stored_m, 16)
        sp.dma_start(k.o_ms[0].rearrange("b h -> h b"), per_seq(m_tok[:, T:TA])[:, :, SI - 1],
                     allow_slow_non_contiguous=True).then_inc(k.stored_m, 16)
        sp.wait_ge(k.stored_m, 32)


COL_A, COL_EM, COL_W = 0, 32, 64
NCS = 3
K_BLOCKS = [[(0, 0), (0, 3), (1, 1)], [(1, 0), (0, 1), (1, 3)], [(0, 2), (1, 2)]]
V_BLOCKS = [[(0, 0), (0, 1), (0, 2)], [(1, 0), (0, 3), (1, 2)], [(1, 1), (1, 3)]]


def stage_cell(nc, k, ctx):
    def sb(name, shape, dt=F32):
        return ctx.enter_context(nc.sbuf_tensor(name, shape, dt))
    qT = sb("qT", [128, HF, TA])
    kT = sb("kT", [128, HF, TA])
    kw = sb("kw", [128, NT + 1, AD])
    vt = sb("vt", [128, NT + 1, AD])
    nb = sb("nb", [128, T])
    nbw = sb("nbw", [128, 2 * S + SB])
    nbd = sb("nbd", [128, NT, 128])
    nbds = sb("nbds", [S, S])
    num4 = sb("num4", [128, AD])
    qw = sb("qw", [128, HF, S])
    qm = sb("qm", [128, HF, SB, S])
    prod = sb("prod", [128, HF, S])
    pS = sb("pS", [S, S])
    kS = sb("kS", [128, 2, AD], BF16)
    vS = sb("vS", [128, 2, AD], BF16)
    kM = sb("kM", [128, 2, 2, AD], BF16)
    left = sb("left", [S, AD])
    cst = sb("cst", [128, 2, AD])
    nP = sb("nP", [128, AH * HF])
    stat = sb("stat", [128, NT, 6])
    mv = sb("mv", [128, NT, 2])
    rr = sb("rr", [128, 4, NT])
    ntmp = sb("ntmp", [128, HF, SB])
    nrows = sb("nrows", [128, 128])
    sden = sb("sden", [S, 1])
    nprow = sb("nprow", [AH * HF, 128])
    flat = k.wring[:, :, :].rearrange("p a b -> p (a b)")
    cs = flat[:, 0:NCS * HF * AD].rearrange("p (s f e) -> p s f e", s=NCS, f=HF)
    P = flat[:, NCS * HF * AD:(NCS + 1) * HF * AD].rearrange("p (j t) -> p j t", j=NT)
    acc = k.ps[:, NRING]
    block = ctx.enter_context(nc.Block())
    KSCALE = float(AD) ** -0.5

    def hn_of(h):
        return k.xrow[:, HF * h:HF * h + HF, :].rearrange("p f x -> p (f x)")[:, 0:NT * AD].rearrange("p (i e) -> p i e", i=NT)

    def nT_of(t, h):
        return t[:, :].rearrange("p (b h f) -> p h f b", b=SB, h=AH)[:, h]

    def tok(t, f, i):
        return t[:, f, 128 * i:128 * i + 128] if i < NT else t[:, f, T:TA]

    def sample_state(pe, h, s0, s1):
        if s0 == 0:
            pe.wait_ge(k.qm_ready, HF * (h + 1))
            if h:
                pe.wait_ge(k.acc_free, h)
        for s in range(s0, s1):
            u = SB * h + s
            pe.wait_ge(k.c_here[u % NCS], 16 * (u // NCS + 1))
            for ft in range(HF):
                m = pe.matmul(acc[32 * ft:32 * ft + 32, :], qm[:, ft, s, :], cs[:, u % NCS, ft, :],
                              start=s == 0, stop=s == SB - 1)
            if s == SB - 1:
                m.then_inc(k.acc_full, 1)
            pe.wait_ge(k.km_ready, u + 1)
            for ft in range(HF):
                b, full = open_bank(pe, k, ("up", h, s, ft))
                for c in range(2):
                    m = pe.matmul(b[:, :], kM[:, s % 2, c, 128 * ft:128 * ft + 128], vS[:, c, :], start=c == 0, stop=c == 1)
                m.then_inc(full, 1)

    def turn_samples(pe, h):
        pe.wait_ge(k.hn_ready, (NT + 1) * (h + 1))
        b, full = open_bank(pe, k, ("tr", h, NT))
        for ft in range(HF):
            m = pe.transpose(b[:, S * ft:S * ft + S], hn_of(h)[0:S, 0, 128 * ft:128 * ft + 128], k.ident[0:S, 0:S])
        m.then_inc(full, 1)

    def split(eng, st, src, dst, rest, blocks):
        for part in range(3):
            (c, b0), *more = blocks[part]
            first = dst[32 * b0:32 * b0 + 32, c, :]
            st.then(eng.tensor_copy(first, src))
            for c2, b2 in more:
                st.then(eng.tensor_copy(dst[32 * b2:32 * b2 + 32, c2, :], first))
            if part < 2:
                st.then(eng.tensor_tensor(rest, src, first, ALU.subtract))
                src = rest

    @block.tensor
    def _(pe):
        for h in range(AH):
            b, full = open_bank(pe, k, ("nm", h))
            pe.matmul(b[:, 0:T], k.headsel[:, h, :], k.brow[:, 0:T], start=True, stop=True).then_inc(full, 1)
            b, full = open_bank(pe, k, ("nw", h))
            pe.matmul(b[:, 0:2 * S + SB], k.headsel[:, h, :], k.brow[:, T:TA + S + SB], start=True, stop=True).then_inc(full, 1)
            pe.wait_ge(k.bd_ready, 12 + 3 * h + 3)
            for i in range(NT + 1):
                n = 128 if i < NT else S
                b, full = open_bank(pe, k, ("ktok", h, i))
                for ft in range(HF):
                    m = pe.matmul(b[0:n, 128 * ft:128 * ft + 128], tok(k.xcT, HF * h + ft, i), k.bd[:, 1, ft, :],
                                  start=True, stop=True)
                m.then_inc(full, 1)
            for i in range(NT + 1):
                n = 128 if i < NT else S
                b, full = open_bank(pe, k, ("vtok", h, i))
                for ft in range(HF):
                    f = HF * h + ft
                    x = k.xp[:, f, 3 + 128 * i:131 + 128 * i] if i < NT else k.xms[:, f, :]
                    m = pe.matmul(b[0:n, 128 * ft:128 * ft + 128], x, k.bd[:, 2, ft, :], start=True, stop=True)
                m.then_inc(full, 1)
            for m3 in range(2):
                for ft in range(HF):
                    for hf, (t0, t1) in enumerate(HALF):
                        b, full = open_bank(pe, k, ("qk", h, m3, ft, hf))
                        pe.matmul(b[:, 0:t1 - t0], k.bd[:, m3, ft, :], k.xcT[:, HF * h + ft, t0:t1],
                                  start=True, stop=True).then_inc(full, 1)
            drained(pe, k, ("qk", h, 1, HF - 1, 1))
            for j in range(NT):
                b, full = open_bank(pe, k, ("S", h, j))
                for ft in range(HF):
                    m = pe.matmul(b[:, 128 * j:T], kT[:, ft, 128 * j:128 * j + 128], qT[:, ft, 128 * j:T],
                                  start=ft == 0, stop=ft == HF - 1)
                m.then_inc(full, 1)
            b, full = open_bank(pe, k, ("Ss", h))
            for ft in range(HF):
                m = pe.matmul(b[0:S, 0:S], kT[:, ft, T:TA], qT[:, ft, T:TA], start=ft == 0, stop=ft == HF - 1)
            m.then_inc(full, 1)
            drained(pe, k, ("ktok", h, NT))
            drained(pe, k, ("vtok", h, NT))
            for ft in range(HF):
                if ft % 2:
                    sample_state(pe, h, ft // 2, ft // 2 + 1)
                b, full = open_bank(pe, k, ("Cp", h, ft))
                for j in range(NT):
                    m = pe.matmul(b[:, :], kw[:, j, 128 * ft:128 * ft + 128], vt[:, j, :], start=j == 0, stop=j == NT - 1)
                m.then_inc(full, 1)
            b, full = open_bank(pe, k, ("nn", h))
            for ft in range(HF):
                for j in range(NT):
                    pe.matmul(b[:, 9 * ft:9 * ft + 1], kw[:, j, 128 * ft:128 * ft + 128], k.ones[:, 0:1],
                              start=j == 0, stop=j == NT - 1)
                m = pe.matmul(b[:, 9 * ft + 1:9 * ft + 9], kw[0:S, NT, 128 * ft:128 * ft + 128], k.tmask[0:S, :],
                              start=True, stop=True)
            m.then_inc(full, 1)
            if h:
                turn_samples(pe, h - 1)
            sample_state(pe, h, 2, 3)
            pe.wait_ge(k.p_ready, 5 * h + 4)
            b, full = open_bank(pe, k, ("den", h))
            for i in range(NT):
                for j in range(i + 1):
                    m = pe.matmul(b[:, i:i + 1], P[:, j, 128 * i:128 * i + 128], k.ones[:, 0:1], start=j == 0, stop=j == i)
            m.then_inc(full, 1)
            sample_state(pe, h, 3, 5)
            for i in range(NT):
                b, full = open_bank(pe, k, ("num", h, i))
                for j in range(i + 1):
                    m = pe.matmul(b[:, :], P[:, j, 128 * i:128 * i + 128], vt[:, j, :], start=j == 0, stop=j == i)
                m.then_inc(full, 1)
            for i in range(NT):
                if i < SB - 5:
                    sample_state(pe, h, 5 + i, 6 + i)
                pe.wait_ge(k.hn_ready, (NT + 1) * h + i + 1)
                b, full = open_bank(pe, k, ("tr", h, i))
                for ft in range(HF):
                    m = pe.transpose(b[:, 128 * ft:128 * ft + 128], hn_of(h)[:, i, 128 * ft:128 * ft + 128], k.ident[:, :])
                m.then_inc(full, 1)
            if h == AH - 1:
                pe.wait_ge(k.n_ready, AH)
                b, full = open_bank(pe, k, "nrows")
                pe.transpose(b[:, 0:128], k.nT[:, :], k.ident[:, :])
                pe.transpose(b[0:16, 128:256], nP[:, :], k.ident[:, :]).then_inc(full, 1)
            pe.wait_ge(k.num4_ready, h + 1)
            b, full = open_bank(pe, k, ("nums", h))
            pe.matmul(b[0:S, :], k.fold[:, :], num4[:, :], start=True, stop=False)
            pe.wait_ge(k.p_ready, 5 * h + 5)
            pe.matmul(b[0:S, :], pS[:, :], vt[0:S, NT, :], start=False, stop=True).then_inc(full, 1)
            pe.wait_ge(k.prod_ready, h + 1)
            b, full = open_bank(pe, k, ("dens", h))
            for ft in range(HF):
                pe.matmul(b[0:S, 0:1], prod[:, ft, :], k.ones[:, 0:1], start=ft == 0, stop=False)
            pe.matmul(b[0:S, 0:1], pS[:, :], k.ones[0:S, 0:1], start=False, stop=True).then_inc(full, 1)
        turn_samples(pe, AH - 1)

    @block.sync
    def _(sp):
        for u in range(AH * SB):
            h, s = u // SB, u % SB
            if u >= NCS:
                sp.wait_ge(k.c_stored[u % NCS], 16 * (u // NCS))
            sp.dma_start(cs[:, u % NCS, :, :], k.state_C[s, h].rearrange("(f p) e -> p f e", p=128)).then_inc(k.c_here[u % NCS], 16)
        for c in range(NCS):
            sp.wait_ge(k.c_stored[c], 16 * ((AH * SB - c + NCS - 1) // NCS))
        bank, n = k.bank_of[("num", AH - 1, NT - 1)]
        sp.wait_ge(k.bank_full[bank], n)
        load_chunks(sp, k, CH_UP + 4, CH_UP + 4 + NW)

    @block.gpsimd
    def _(pool):
        ps = Steps(pool, k.pool_step, k, "pool")

        def store_state(u):
            for ft in range(HF):
                drained(pool, k, ("up", u // SB, u % SB, ft))
            pool.dma_start(k.o_cs[0, u % SB, u // SB].rearrange("(f p) e -> p f e", p=128),
                           cs[:, u % NCS, :, :]).then_inc(k.c_stored[u % NCS], 16)
        head_blocks(pool, k, 0)
        for h in range(AH):
            drained(pool, k, ("nw", h))
            pool.tensor_tensor(nbd[:, :, :], nb[:, :].rearrange("p (j t) -> p j t", j=NT),
                               k.maskT[:, :].unsqueeze(1).to_broadcast([128, NT, 128]), ALU.add).then_inc(k.nbd_ready, 1)
            pool.tensor_tensor(nbds[:, :], nbw[0:S, 0:S], k.maskS[:, :], ALU.add).then_inc(k.nbd_ready, 1)
            drained(pool, k, ("vtok", h, NT))
            if h:
                bank, n = k.bank_of[("up", h - 1, SB - 1, HF - 1)]
                pool.wait_ge(k.bank_full[bank], n)
            split(pool, ps, vt[0:S, NT, :], vS, left[:, :], V_BLOCKS)
            pool.sem_inc(k.vs_ready, 1)
            pool.wait_ge(k.qw_ready, h + 1)
            for ft in range(HF):
                pool.tensor_tensor(qm[:, ft, :, :], qw[:, ft, :].unsqueeze(1).to_broadcast([128, SB, S]),
                                   k.bmask[:, :, :], ALU.mult).then_inc(k.qm_ready, 1)
            if h + 1 < AH:
                bank, n = k.bank_of[("qk", h, 1, HF - 1, 1)]
                pool.wait_ge(k.bank_full[bank], n)
                head_blocks(pool, k, h + 1)
            drained(pool, k, ("qk", h, 1, HF - 1, 1))
            for ft in range(HF):
                f = HF * h + ft
                pool.tensor_scalar(k.xcT[:, f, :], k.xcT[:, f, :], k.vecs1[:, 96 + f:97 + f], None, ALU.mult).then_inc(k.skip_ready, 1)
            for ft in range(HF):
                pool.wait_ge(k.cst_ready, HF * h + ft + 1)
                pool.dma_start(k.o_cp[0, 0, h, 128 * ft:128 * ft + 128, :], cst[:, ft % 2, :]).then_inc(k.cst_stored[ft % 2], 16)
                if ft % 2 == 0:
                    store_state(SB * h + ft // 2)
            for s in range(2, SB):
                store_state(SB * h + s)
        drained(pool, k, "nrows")
        pool.dma_start(k.o_ns[0].rearrange("b h (f p) -> (b h f) p", p=128), nrows[:, :]).then_inc(k.stored_n, 16)
        pool.dma_start(k.o_np[0, 0].rearrange("h (f p) -> (h f) p", p=128), nprow[:, :]).then_inc(k.stored_n, 16)
        pool.wait_ge(k.stored_n, 32)
        for c in range(NCS):
            pool.wait_ge(k.c_stored[c], 16 * ((AH * SB - c + NCS - 1) // NCS))
        for c in range(2):
            pool.wait_ge(k.cst_stored[c], 16 * 2 * AH)

    @block.scalar
    def _(act):
        def mask(h, s):
            u = SB * h + s
            if u >= 2:
                bank, n = k.bank_of[("up", (u - 2) // SB, (u - 2) % SB, HF - 1)]
                act.wait_ge(k.bank_full[bank], n)
            act.activation(kM[:, s % 2, :, :], kS[:, :, :], ACT.Copy, scale=k.tmask[:, s:s + 1]).then_inc(k.km_ready, 1)

        def sample_deviation(h):
            act.wait_ge(k.var_ready, 2 * h + 2)
            act.activation(rr[0:S, 2, 0:1], rr[0:S, 1, 0:1], ACT.Sqrt).then_inc(k.sd_ready, 1)

        for h in range(AH):
            for i in range(NT + 1):
                n = 128 if i < NT else S
                b, free = full_bank(act, k, ("vtok", h, i))
                act.activation(vt[0:n, i, :], b[0:n, :], ACT.Copy).then_inc(free, 1)
            for m3, dst in ((0, qT), (1, kT)):
                for ft in range(HF):
                    for hf, (t0, t1) in enumerate(HALF):
                        b, free = full_bank(act, k, ("qk", h, m3, ft, hf))
                        act.activation(dst[:, ft, t0:t1], b[:, 0:t1 - t0], ACT.Copy, scale=1.0 if m3 == 0 else KSCALE).then_inc(free, 1)
            act.wait_ge(k.nbd_ready, 2 * h + 2)
            for j in range(NT):
                a = k.cols[:, j, COL_A + h:COL_A + h + 1]
                m = act.activation(P[:, j, 128 * j:128 * j + 128], nbd[:, j, :], ACT.Exp, bias=a)
                if j < NT - 1:
                    m = act.activation(P[:, j, 128 * j + 128:T], nb[:, 128 * j + 128:T], ACT.Exp, bias=a)
                m.then_inc(k.w_ready, 1)
            act.activation(pS[:, :], nbds[:, :], ACT.Exp, bias=k.cols[0:S, NT, COL_A + h:COL_A + h + 1]).then_inc(k.w_ready, 1)
            if h:
                sample_deviation(h - 1)
            act.wait_ge(k.ks_ready, h + 1)
            act.wait_ge(k.vs_ready, h + 1)
            mask(h, 0)
            mask(h, 1)
            for ft in range(HF):
                b, free = full_bank(act, k, ("Cp", h, ft))
                c = 2 * h + ft // 2
                if c:
                    act.wait_ge(k.cst_stored[ft % 2], 16 * c)
                act.activation(cst[:, ft % 2, :], b[:, :], ACT.Copy).then_inc(free, 1)
                drained(act, k, ("Cp", h, ft))
                act.sem_inc(k.cst_ready, 1)
                if ft == 1:
                    mask(h, 2)
            mask(h, 3)
            mask(h, 4)
            act.wait_ge(k.var_ready, 2 * h + 1)
            act.activation(rr[:, 2, :], rr[:, 1, :], ACT.Sqrt).then_inc(k.sd_ready, 1)
            for s in range(5, SB):
                mask(h, s)
            act.wait_ge(k.acc_full, h + 1)
            act.activation(num4[:, :], acc[:, :], ACT.Copy).then_inc(k.acc_free, 1)
            act.wait_ge(k.acc_free, h + 1)
            act.sem_inc(k.num4_ready, 1)
        sample_deviation(AH - 1)

    @block.vector
    def _(dve):
        st = Steps(dve, k.dve_step, k, "dve")
        def new_states(h, s0, s1):
            for s in range(s0, s1):
                u = SB * h + s
                for ft in range(HF):
                    b, free = full_bank(dve, k, ("up", h, s, ft))
                    c = cs[:, u % NCS, ft, :]
                    dve.scalar_tensor_tensor(out=c, in0=c, scalar=nbw[:, 2 * S + s:2 * S + s + 1], in1=b[:, :],
                                             op0=ALU.mult, op1=ALU.add).then_inc(free, 1)

        def mix(h, i):
            n = 128 if i < NT else S
            b, free = full_bank(dve, k, ("tr", h, i))
            for ft in range(HF):
                f = HF * h + ft
                m = dve.scalar_tensor_tensor(out=tok(k.xcT, f, i), in0=b[:, n * ft:n * ft + n], scalar=k.vecs1[:, 80 + f:81 + f],
                                             in1=tok(k.xcT, f, i), op0=ALU.mult, op1=ALU.add)
            m.then_inc(free, 1)

        def sample_variance(h):
            st.then(dve.bn_stats(stat[0:S, 0, :], hn_of(h)[0:S, 0, :]))
            st.then(dve.bn_aggr(mv[0:S, 0, :], stat[0:S, 0, :]))
            st.then(dve.tensor_scalar(rr[0:S, 0, 0:1], sden[:, :], -1.0, k.cols[0:S, NT, COL_EM + h:COL_EM + h + 1], ALU.mult, ALU.max))
            st.then(dve.tensor_tensor(rr[0:S, 0, 0:1], rr[0:S, 0, 0:1], sden[:, :], ALU.max))
            st.then(dve.reciprocal(rr[0:S, 0, 0:1], rr[0:S, 0, 0:1]))
            st.then(dve.tensor_tensor(rr[0:S, 1, 0:1], mv[0:S, 0, 1:2], rr[0:S, 0, 0:1], ALU.mult))
            st.then(dve.tensor_tensor(rr[0:S, 1, 0:1], rr[0:S, 1, 0:1], rr[0:S, 0, 0:1], ALU.mult))
            dve.tensor_scalar(rr[0:S, 1, 0:1], rr[0:S, 1, 0:1], EPS, None, ALU.add).then_inc(k.var_ready, 1)

        def sample_norm(h):
            dve.wait_ge(k.sd_ready, 2 * h + 2)
            st.then(dve.reciprocal(rr[0:S, 2, 0:1], rr[0:S, 2, 0:1]))
            st.then(dve.tensor_tensor(rr[0:S, 3, 0:1], rr[0:S, 2, 0:1], rr[0:S, 0, 0:1], ALU.mult))
            rows = hn_of(h)[0:S, 0, :]
            dve.tensor_scalar(rows, rows, mv[0:S, 0, 0:1], rr[0:S, 3, 0:1], ALU.subtract, ALU.mult).then_inc(k.hn_ready, 1)

        for h in range(AH):
            b, free = full_bank(dve, k, ("nm", h))
            dve.tensor_copy(nb[:, :], b[:, :]).then_inc(free, 1)
            b, free = full_bank(dve, k, ("nw", h))
            dve.tensor_copy(nbw[:, :], b[:, 0:2 * S + SB]).then_inc(free, 1)
            drained(dve, k, ("nw", h))
            for i in range(NT + 1):
                n = 128 if i < NT else S
                b, free = full_bank(dve, k, ("ktok", h, i))
                dve.tensor_scalar(kw[0:n, i, :], b[0:n, :], KSCALE, k.cols[0:n, i, COL_W + h:COL_W + h + 1],
                                  ALU.mult, ALU.mult).then_inc(free, 1)
            drained(dve, k, ("ktok", h, NT))
            if h:
                dve.wait_ge(k.km_ready, SB * h)
            split(dve, st, kw[0:S, NT, :], kS, num4[0:S, :], K_BLOCKS)
            dve.wait_ge(k.dve_step, k.steps["dve"])
            dve.sem_inc(k.ks_ready, 1)
            if h:
                sample_variance(h - 1)
            drained(dve, k, ("qk", h, 0, HF - 1, 1))
            st.then(dve.tensor_tensor(qw[:, :, :], qT[:, :, T:TA], nbw[:, S:2 * S].unsqueeze(1).to_broadcast([128, HF, S]), ALU.mult))
            dve.sem_inc(k.qw_ready, 1)
            dve.tensor_tensor(prod[:, :, :].rearrange("p f (b i) -> p f b i", i=SI),
                              qw[:, :, :].rearrange("p f (b i) -> p f b i", i=SI),
                              nT_of(k.nT, h).unsqueeze(3).to_broadcast([128, HF, SB, SI]), ALU.mult).then_inc(k.prod_ready, 1)
            for j in range(NT):
                dve.wait_ge(k.w_ready, 5 * h + j + 1)
                b, free = full_bank(dve, k, ("S", h, j))
                st.then(dve.tensor_tensor(P[:, j, 128 * j:T], P[:, j, 128 * j:T], b[:, 128 * j:T], ALU.mult))
                dve.sem_inc(free, 1)
                dve.sem_inc(k.p_ready, 1)
            dve.wait_ge(k.w_ready, 5 * h + 5)
            b, free = full_bank(dve, k, ("Ss", h))
            st.then(dve.tensor_tensor(pS[:, :], pS[:, :], b[0:S, 0:S], ALU.mult))
            dve.sem_inc(free, 1)
            dve.sem_inc(k.p_ready, 1)
            if h:
                sample_norm(h - 1)
            new_states(h, 0, 2)
            b, free = full_bank(dve, k, ("nn", h))
            nn = b[:, 0:9 * HF].rearrange("p (f c) -> p f c", c=9)
            dve.tensor_copy(nP[:, HF * h:HF * h + HF], nn[:, :, 0])
            dve.wait_ge(k.prod_ready, h + 1)
            st.then(dve.tensor_tensor(ntmp[:, :, :], nT_of(k.nT, h), nbw[:, 2 * S:2 * S + SB].unsqueeze(1).to_broadcast([128, HF, SB]), ALU.mult))
            st.then(dve.tensor_tensor(nT_of(k.nT, h), ntmp[:, :, :], nn[:, :, 1:9], ALU.add))
            dve.sem_inc(free, 1)
            dve.sem_inc(k.n_ready, 1)
            if h:
                mix(h - 1, NT)
            new_states(h, 2, 3)
            em = k.cols[:, 0:NT, COL_EM + h]
            b, free = full_bank(dve, k, ("den", h))
            st.then(dve.tensor_scalar(rr[:, 0, :], b[:, 0:NT], -1.0, None, ALU.mult))
            st.then(dve.tensor_tensor(rr[:, 0, :], rr[:, 0, :], b[:, 0:NT], ALU.max))
            dve.sem_inc(free, 1)
            st.then(dve.tensor_tensor(rr[:, 0, :], rr[:, 0, :], em, ALU.max))
            st.then(dve.reciprocal(rr[:, 0, :], rr[:, 0, :]))
            new_states(h, 3, 5)
            for i in range(NT):
                b, free = full_bank(dve, k, ("num", h, i))
                st.then(dve.bn_stats(stat[:, i, :], b[:, :]))
                st.then(dve.bn_aggr(mv[:, i, :], stat[:, i, :]))
            st.then(dve.tensor_tensor(rr[:, 1, :], mv[:, :, 1], rr[:, 0, :], ALU.mult))
            st.then(dve.tensor_tensor(rr[:, 1, :], rr[:, 1, :], rr[:, 0, :], ALU.mult))
            dve.tensor_scalar(rr[:, 1, :], rr[:, 1, :], EPS, None, ALU.add).then_inc(k.var_ready, 1)
            dve.wait_ge(k.sd_ready, 2 * h + 1)
            st.then(dve.reciprocal(rr[:, 2, :], rr[:, 2, :]))
            st.then(dve.tensor_tensor(rr[:, 3, :], rr[:, 2, :], rr[:, 0, :], ALU.mult))
            for i in range(NT):
                b, free = full_bank(dve, k, ("num", h, i))
                st.then(dve.tensor_scalar(hn_of(h)[:, i, :], b[:, :], mv[:, i, 0:1], rr[:, 3, i:i + 1], ALU.subtract, ALU.mult))
                dve.sem_inc(free, 1)
                dve.sem_inc(k.hn_ready, 1)
            dve.wait_ge(k.skip_ready, HF * (h + 1))
            for i in range(NT):
                if i < SB - 5:
                    new_states(h, 5 + i, 6 + i)
                mix(h, i)
            if h == AH - 1:
                b, free = full_bank(dve, k, "nrows")
                dve.tensor_copy(nrows[:, :], b[:, 0:128])
                dve.tensor_copy(nprow[:, :], b[0:16, 128:256]).then_inc(free, 1)
            b, free = full_bank(dve, k, ("nums", h))
            dve.tensor_copy(hn_of(h)[0:S, 0, :], b[0:S, :]).then_inc(free, 1)
            b, free = full_bank(dve, k, ("dens", h))
            dve.tensor_copy(sden[:, :], b[0:S, 0:1]).then_inc(free, 1)
            drained(dve, k, ("nums", h))
            drained(dve, k, ("dens", h))
        sample_variance(AH - 1)
        sample_norm(AH - 1)
        mix(AH - 1, NT)




def stage_gate(nc, k, ctx):
    def sb(name, shape, dt=F32R):
        return ctx.enter_context(nc.sbuf_tensor(name, shape, dt))
    WS = 5
    xh, xl = sb("xh", [128, KD, TA]), sb("xl", [128, KD, TA])
    wh, wl = sb("wh", [128, WS, KD, 128]), sb("wl", [128, WS, KD, 128])
    zt = k.arena[:, 0:4 * 288].rearrange("p (s t) -> p s t", s=4)
    block = ctx.enter_context(nc.Block())

    def weights(eng, f):
        w = chunk(eng, k, CH_UP + 4 + f // 4)
        return w[:, :, 128 * (f % 4):128 * (f % 4) + 128]

    @block.tensor
    def _(pe):
        for f in range(FT):
            pe.wait_ge(k.w_low, f + 1)
            if f == 0:
                pe.wait_ge(k.x_low, KD)
            for hf, (t0, t1) in enumerate(HALF):
                b, full = open_bank(pe, k, ("z", f, hf))
                out = b[:, 0:t1 - t0]
                for kt in range(KD):
                    w_hi, w_lo = wh[:, f % WS, kt, :], wl[:, f % WS, kt, :]
                    x_hi, x_lo = xh[:, kt, t0:t1], xl[:, kt, t0:t1]
                    pe.matmul(out, w_hi, x_hi, start=kt == 0, stop=False)
                    pe.matmul(out, w_hi, x_lo, start=False, stop=False)
                    m = pe.matmul(out, w_lo, x_hi, start=False, stop=kt == KD - 1)
                m.then_inc(full, 1)
            if f % 4 == 3:
                k.chunk_last[CH_UP + 4 + f // 4] = ("low", f + 1)

    @block.sync
    def _(sp):
        load_chunks(sp, k, CH_UP + 4 + NW, CH_DOWN + NW)

    @block.scalar
    def _(act):
        def upper(f):
            act.activation(wh[:, f % WS, :, :], weights(act, f), ACT.Copy).then_inc(k.w_high, 1)
        for kt in range(KD):
            act.activation(xh[:, kt, :], k.xnT[:, kt, :], ACT.Copy).then_inc(k.x_high, 1)
        for f in range(WS - 1):
            upper(f)
        for u in range(2 * FT):
            f, hf = u // 2, u % 2
            n = HALF[hf][1] - HALF[hf][0]
            b, free = full_bank(act, k, ("z", f, hf))
            if u >= 4:
                act.wait_ge(k.gated, u - 3)
            act.activation(zt[:, u % 4, 0:n], b[:, 0:n], ACT.Silu).then_inc(free, 1)
            if hf == 0 and f + WS - 1 < FT:
                upper(f + WS - 1)

    @block.vector
    def _(dve):
        def lower(f):
            dve.wait_ge(k.w_high, f + 1)
            dve.tensor_tensor(wl[:, f % WS, :, :], weights(dve, f), wh[:, f % WS, :, :], ALU.subtract).then_inc(k.w_low, 1)
        for kt in range(KD):
            dve.wait_ge(k.x_high, kt + 1)
            dve.tensor_tensor(xl[:, kt, :], k.xnT[:, kt, :], xh[:, kt, :], ALU.subtract).then_inc(k.x_low, 1)
        for f in range(WS - 1):
            lower(f)
        for u in range(2 * FT):
            f, hf = u // 2, u % 2
            t0, t1 = HALF[hf]
            drained(dve, k, ("z", f, hf))
            dve.tensor_tensor(k.xcT[:, f, t0:t1], k.xcT[:, f, t0:t1], zt[:, u % 4, 0:t1 - t0], ALU.mult).then_inc(k.gated, 1)
            if hf == 0 and f + WS - 1 < FT:
                lower(f + WS - 1)


def project_rows(pe, k, key, xT, c0, halves, order=TILES, before=None):
    banks = []
    for i in range(NT + 1):
        banks.append(open_bank(pe, k, (key, i)))
    for half in range(halves):
        w = chunk(pe, k, c0 + half)
        for i in order:
            n = 128 if i < NT else S
            b, full = banks[i]
            if i == NT and before:
                before()
            for kt in range(8):
                if i == NT and w.shape[2] == 512:
                    p0 = 32 * (kt % 4)
                    m = pe.matmul(b[p0:p0 + S, :], xT[:, 8 * half + kt, T:TA], w[:, kt, :],
                                  start=half == 0 and kt < 4, stop=half == halves - 1 and kt >= 4)
                    continue
                m = pe.matmul(b[0:n, 0:w.shape[2]], xT[:, 8 * half + kt, 128 * i:128 * i + n], w[:, kt, :],
                              start=half == 0 and kt == 0, stop=half == halves - 1 and kt == 7)
            if half == halves - 1:
                m.then_inc(full, 1)
        if half < halves - 1:
            m.then_inc(k.half_done, 1)
            k.halves += 1
            k.chunk_last[c0 + half] = ("half", k.halves)
        else:
            k.chunk_last[c0 + half] = k.bank_of[(key, order[-1])]


def fold(dve, k, st, key, out):
    b, free = full_bank(dve, k, (key, NT))
    st.then(dve.tensor_copy(out, b[0:S, :]))
    for j in range(1, 4):
        m = dve.tensor_tensor(out, out, b[32 * j:32 * j + S, :], ALU.add)
        if j < 3:
            st.then(m)
    m.then_inc(free, 1)


def rows_of(t, i):
    return t[0:128 if i < NT else S, :]


def norm_residual(k, dve, st, y, xr, npost, rstd_i, i):
    r = 128 if i < NT else S
    st.then(dve.scalar_tensor_tensor(out=y[0:r, i, :], in0=y[0:r, i, :], scalar=rstd_i, in1=npost[0:r, :],
                                     op0=ALU.mult, op1=ALU.mult))
    st.then(dve.tensor_tensor(xr[0:r, i, :], xr[0:r, i, :], y[0:r, i, :], ALU.add))
    dve.sem_inc(k.res_ready, 1)


def stage_down(nc, k, ctx):
    def sb(name, shape, dt=F32):
        return ctx.enter_context(nc.sbuf_tensor(name, shape, dt))
    y = sb("y_down", [128, NT + 1, D])
    npost = sb("npost", [128, D])
    sq = sb("sq2", [128, D])
    ssq = sb("ssq2", [128, 2 * (NT + 1)])
    rstd = sb("rstd2", [128, 2 * (NT + 1)])
    x1 = k.x1
    block = ctx.enter_context(nc.Block())
    DK = D // 512
    norms = RowNorms(k, [("y", TILES[0])] + [key for n in range(NT) for key in (("y", TILES[n + 1]), ("x1", TILES[n]))]
                     + [("x1", TILES[NT])],
                     ssq, rstd, NT + 1)

    @block.tensor
    def _(pe):
        for n in range(DK):
            project_rows(pe, k, ("down", n), k.xcT, CH_DOWN + 2 * n, 2)
        pe.wait_ge(k.xn_tok, 2 * (NT + 1))
        for kt in range(KD):
            b, full = open_bank(pe, k, ("x1T", kt))
            for i in range(NT):
                m = pe.transpose(b[:, 128 * i:128 * i + 128], y[:, i, 128 * kt:128 * kt + 128], k.ident[:, :])
            m.then_inc(full, 1)
        b, full = open_bank(pe, k, "x1Ts")
        for kt in range(KD):
            m = pe.transpose(b[:, S * kt:S * kt + S], y[0:S, NT, 128 * kt:128 * kt + 128], k.ident[0:S, 0:S])
        m.then_inc(full, 1)

    @block.sync
    def _(sp):
        sp.dma_start(x1[:, 0:NT, :], k.x_prompt[0].rearrange("(i p) d -> p i d", p=128)).then_inc(k.x_here, 16)
        sp.dma_start(x1[0:S, NT, :], k.x_sample.rearrange("b i d -> (b i) d")).then_inc(k.x_here, 16)
        sp.dma_start(npost[:, :], k.a_norm_post.partition_broadcast(128)).then_inc(k.x_here, 16)
        load_chunks(sp, k, CH_DOWN + NW, CH_KV + NW)
        sp.wait_ge(k.res_ready, NT + 1)
        sp.dma_start(k.o_yp[0].rearrange("(i p) d -> p i d", p=128), x1[:, 0:NT, :]).then_inc(k.stored_x1, 16)
        sp.dma_start(k.o_ys.rearrange("b i d -> (b i) d"), x1[0:S, NT, :]).then_inc(k.stored_x1, 16)
        sp.wait_ge(k.stored_x1, 32)

    @block.scalar
    def _(act):
        def rows(t, i):
            return t[0:128 if i < NT else S, i, :]

        def tile(n):
            i, j = TILES[min(n, NT)], TILES[n - 1]
            if n <= NT:
                norms.square(act, ("y", i), rows(y, i), rows_of(sq, i))
            if n:
                act.wait_ge(k.res_ready, n)
                norms.square(act, ("x1", j), rows(x1, j), rows_of(sq, j))
            if n <= NT:
                norms.root(act, ("y", i))
            if n:
                norms.root(act, ("x1", j))

        for n in range(DK):
            if n == DK - 1:
                drained(act, k, (("down", 0), NT))
                drained(act, k, (("down", 1), NT))
                tile(0)
            for i in range(NT):
                b, free = full_bank(act, k, (("down", n), i))
                act.activation(y[:, i, 512 * n:512 * n + 512], b, ACT.Copy).then_inc(free, 1)
                if n == DK - 1:
                    drained(act, k, (("down", n), i))
                    tile(i + 1)
        tile(NT + 1)
        for kt in range(1, KD, 2):
            b, free = full_bank(act, k, ("x1T", kt))
            act.activation(k.kvT[:, kt, 0:T], b[:, 0:T], ACT.Copy, scale=k.vecs2[:, 8 + kt:9 + kt])
            act.activation(k.xnT[:, kt, 0:T], b[:, 0:T], ACT.Copy, scale=k.vecs2[:, 16 + kt:17 + kt]).then_inc(free, 1)

    @block.vector
    def _(dve):
        st = Steps(dve, k.dve_step, k, "dve")
        for n in range(DK):
            fold(dve, k, st, ("down", n), y[0:S, NT, 512 * n:512 * n + 512])
        dve.wait_ge(k.x_here, 48)
        for n in range(NT + 2):
            i, j = TILES[min(n, NT)], TILES[n - 1]
            if n <= NT:
                norms.mean(dve, ("y", i))
            if n:
                norms.mean(dve, ("x1", j))
            if n <= NT:
                norm_residual(k, dve, st, y, x1, npost, norms.invert(dve, st, ("y", i)), i)
            if n:
                r = 128 if j < NT else S
                dve.tensor_scalar(y[0:r, j, :], x1[0:r, j, :], norms.invert(dve, st, ("x1", j)), None, ALU.mult).then_inc(k.xn_tok, 1)
        for kt in range(0, KD, 2):
            b, free = full_bank(dve, k, ("x1T", kt))
            dve.tensor_scalar(k.kvT[:, kt, 0:T], b[:, 0:T], k.vecs2[:, 8 + kt:9 + kt], None, ALU.mult)
            dve.tensor_scalar(k.xnT[:, kt, 0:T], b[:, 0:T], k.vecs2[:, 16 + kt:17 + kt], None, ALU.mult).then_inc(free, 1)
        b, free = full_bank(dve, k, "x1Ts")
        src = b[:, 0:KD * S].rearrange("p (a b) -> p a b", b=S)
        dve.tensor_tensor(k.kvT[:, :, T:TA], src, k.vecs2[:, 8:16].unsqueeze(2).to_broadcast([128, KD, S]), ALU.mult)
        dve.tensor_tensor(k.xnT[:, :, T:TA], src, k.vecs2[:, 16:24].unsqueeze(2).to_broadcast([128, KD, S]), ALU.mult).then_inc(free, 1)


def cached_pairs(sp, k, q):
    for pg in range(4):
        page = sp.value_load(k.pages[0:1, 4 * q + pg:4 * q + pg + 1], min_val=0, max_val=k.cache_kv.shape[0] - 1)
        src = k.cache_kv[bass.ds(page, 1)].rearrange("o (t a) s g d -> (o t) a (s g d)", a=2)[:, :, 0:512]
        sp.dma_start(k.craw[64 * (pg % 2):64 * (pg % 2) + 64, q % 2, pg // 2, :, :], src).then_inc(k.raw_here[q % 2], 16)


def stage_kv(nc, k, ctx):
    kvt = k.kvt
    block = ctx.enter_context(nc.Block())

    @block.tensor
    def _(pe):
        for c in range(3):
            project_rows(pe, k, ("kv", c), k.kvT, CH_KV + c, 1)
            if c:
                for gp in range(2):
                    b, full = open_bank(pe, k, ("KT", c, gp))
                    for i in range(NT):
                        pe.wait_ge(k.kv_here, (NT + 1) * c + i + 1)
                        m = pe.transpose(b[:, 128 * i:128 * i + 128], kvt[:, c % 2, i, 128 * gp:128 * gp + 128], k.ident[:, :])
                    m.then_inc(full, 1)
                b, full = open_bank(pe, k, ("KTs", c))
                pe.wait_ge(k.kv_here, (NT + 1) * (c + 1))
                for gp in range(2):
                    m = pe.transpose(b[:, S * gp:S * gp + S], kvt[0:S, c % 2, NT, 128 * gp:128 * gp + 128], k.ident[0:S, 0:S])
                m.then_inc(full, 1)

    @block.sync
    def _(sp):
        sp.dma_start(k.posr[:, :], k.cmp_pos.rearrange("s (j a) d -> (s j) (a d)", a=2)).then_inc(k.cw_here, 16)
        sp.dma_start(k.cw2[:, 0, :, :], k.cmp_w2[0].rearrange("(h p) d -> p h d", p=128)).then_inc(k.cw_here, 16)
        sp.dma_start(k.cw2[:, 1, :, :], k.cmp_w2[1].rearrange("(h p) d -> p h d", p=128)).then_inc(k.cw_here, 16)
        sp.dma_start(k.cb2k[0:64, :], k.cmp_b2[0].unsqueeze(1)).then_inc(k.cw_here, 16)
        sp.dma_start(k.cb2k[64:128, :], k.cmp_b2[0].unsqueeze(1)).then_inc(k.cw_here, 16)
        sp.dma_start(k.cb2v[:, :], k.cmp_b2[1].partition_broadcast(NCMP)).then_inc(k.cw_here, 16)
        sp.wait_ge(k.pages_here, 16)
        for q in range(2):
            cached_pairs(sp, k, q)
        load_chunks(sp, k, CH_KV + NW, CH_CMP + NW)

    @block.gpsimd
    def _(pool):
        for s in range(SB):
            pool.dma_start(k.o_ws[s, 0:512 - SI].rearrange("t a g d -> t (a g d)"),
                           k.cache_win[s, SI:512].rearrange("t a g d -> t (a g d)")).then_inc(k.stored_win, 16)
        for c in range(2):
            pool.wait_ge(k.kv_here, (NT + 1) * (c + 1))
            pool.dma_start(k.o_kvp[0].rearrange("(i p) s g d -> p i (s g d)", p=128)[:, :, 512 * c:512 * c + 512],
                           kvt[:, c % 2, 0:NT, :]).then_inc(k.stored_kv, 16)
            pool.dma_start(k.o_kvs.rearrange("b i s g d -> (b i) (s g d)")[:, 512 * c:512 * c + 512],
                           kvt[0:S, c % 2, NT, :]).then_inc(k.stored_kv, 16)
            if c == 0:
                pool.wait_ge(k.stored_kv, 32)
                pool.sem_inc(k.kvt_free, 1)
        pool.wait_ge(k.stored_kv, 16 * 4)

    @block.scalar
    def _(act):
        for c in range(3):
            if c == 2:
                act.wait_ge(k.kvt_free, 1)
            for i in range(NT + 1):
                if i < NT:
                    b, free = full_bank(act, k, (("kv", c), i))
                    act.activation(kvt[:, c % 2, i, :], b, ACT.Copy).then_inc(free, 1)
                drained(act, k, (("kv", c), i))
                act.sem_inc(k.kv_here, 1)

    @block.vector
    def _(dve):
        st = Steps(dve, k.dve_step, k, "dve")
        for c in range(3):
            if c == 2:
                dve.wait_ge(k.kvt_free, 1)
            fold(dve, k, st, ("kv", c), kvt[0:S, c % 2, NT, :])
            if c == 0:
                continue
            for gp in range(2):
                b, free = full_bank(dve, k, ("KT", c, gp))
                dve.tensor_copy(k.KT[:, c - 1, gp, 0:T], b[:, 0:T]).then_inc(free, 1)
            b, free = full_bank(dve, k, ("KTs", c))
            dve.tensor_copy(k.KT[:, c - 1, :, T:TA], b[:, 0:2 * S].rearrange("p (a b) -> p a b", b=S)).then_inc(free, 1)
            for i in range(NT + 1):
                r = 128 if i < NT else S
                dve.wait_ge(k.kv_here, (NT + 1) * c + i + 1)
                dve.tensor_copy(k.V[0:r, c - 1, i, :], kvt[0:r, c % 2, i, SLOT:2 * SLOT])


def stage_compress(nc, k, ctx):
    def sb(name, shape, dt=F32):
        return ctx.enter_context(nc.sbuf_tensor(name, shape, dt))
    NS = SB + 1
    raw, w2, b2k, b2v, posr = k.craw, k.cw2, k.cb2k, k.cb2v, k.posr
    pair = sb("cpair", [128, 2, 2, G, 2, DH])
    R = sb("cR", [128, 2, 2, G, 256])
    
    hid = sb("chid", [128, 2, 2, 2, G * NCMP])
    posT = sb("posT", [128, 32])
    pb = sb("cpb", [128, 4])
    block = ctx.enter_context(nc.Block())

    @block.tensor
    def _(pe):
        pe.wait_ge(k.cw_here, 16 * 6)
        b, full = open_bank(pe, k, "posT")
        pe.transpose(b[:, 0:32], posr[:, :], k.ident[0:32, 0:32]).then_inc(full, 1)

        def turn_pairs(q):
            pe.wait_ge(k.pair_ready, 2 * (q + 1))
            for s in range(2):
                for gp in range(2):
                    b, full = open_bank(pe, k, ("R", q, s, gp))
                    for g in range(2):
                        for j in range(2):
                            m = pe.transpose(b[:, 256 * g + 128 * j:256 * g + 128 * j + 128],
                                             pair[:, j, s, 2 * gp + g, :, :].rearrange("p a d -> p (a d)"), k.ident[:, :])
                    m.then_inc(full, 1)

        def hidden(q):
            for s in range(2):
                drained(pe, k, ("R", q, s, 0))
                drained(pe, k, ("R", q, s, 1))
                b, full = open_bank(pe, k, ("hid", q, s))
                for hh in range(2):
                    for j in range(16):
                        m = pe.matmul(b[:, G * NCMP * hh:G * NCMP * (hh + 1)].rearrange("p (g n) -> p g n", g=G),
                                      w1[s][:, j, 128 * hh:128 * hh + 128],
                                      R[:, q % 2, s, :, j:j + 8 * (NCMP - 1) + 1:8], start=j == 0, stop=j == 15)
                m.then_inc(full, 1)
            k.chunk_last[CH_CMP], k.chunk_last[CH_CMP + 1] = k.bank_of[("hid", q, 0)], k.bank_of[("hid", q, 1)]

        def output(q):
            drained(pe, k, ("hid", q, 1))
            drained(pe, k, ("hid", q, 0))
            b, full = open_bank(pe, k, ("kc", q))
            for g in range(G):
                p0 = 64 * (g % 2)
                for hh in range(2):
                    m = pe.matmul(b[p0:p0 + DH, NCMP * (g // 2):NCMP * (g // 2) + NCMP], w2[:, 0, hh, :],
                                  hid[:, q % 2, 0, hh, NCMP * g:NCMP * g + NCMP], start=hh == 0, stop=hh == 1)
            m.then_inc(full, 1)
            b, full = open_bank(pe, k, ("vc", q))
            for g in range(G):
                for hh in range(2):
                    m = pe.matmul(b[0:NCMP, DH * g:DH * g + DH], hid[:, q % 2, 1, hh, NCMP * g:NCMP * g + NCMP], w2[:, 1, hh, :],
                                  start=hh == 0, stop=hh == 1)
            m.then_inc(full, 1)

        turn_pairs(0)
        drained(pe, k, "posT")
        w1 = []
        b, full = open_bank(pe, k, "pb")
        for s in range(2):
            w1.append(chunk(pe, k, CH_CMP + s))
            for hh in range(2):
                for j in range(16):
                    m = pe.matmul(b[:, 2 * s + hh:2 * s + hh + 1], w1[s][:, j, 128 * hh:128 * hh + 128],
                                  posT[:, 16 * s + j:16 * s + j + 1], start=j == 0, stop=j == 15)
        m.then_inc(full, 1)
        for q in range(NS):
            if q + 1 < NS:
                turn_pairs(q + 1)
            hidden(q)
            if q:
                output(q - 1)
        output(NS - 1)

    @block.sync
    def _(sp):
        for q in range(2, NS):
            sp.wait_ge(k.pair_ready, 2 * (q - 1))
            if q < SB:
                cached_pairs(sp, k, q)
            else:
                for j in range(2):
                    src = k.o_kvp[0, 256 * j:256 * j + 256].rearrange("(t a) s g d -> t a (s g d)", a=2)[:, :, 0:512]
                    sp.dma_start(raw[:, q % 2, j, :, :], src).then_inc(k.raw_here[q % 2], 32)
        load_chunks(sp, k, CH_CMP + NW, CH_IN + NW)

    @block.scalar
    def _(act):
        drained(act, k, "pb")
        for q in range(NS):
            for s in range(2):
                if q >= 2:
                    bank, n = k.bank_of[("vc" if s else "kc", q - 2)]
                    act.wait_ge(k.bank_full[bank], n)
                b, free = full_bank(act, k, ("hid", q, s))
                for hh in range(2):
                    m = act.activation(hid[:, q % 2, s, hh, :], b[:, G * NCMP * hh:G * NCMP * (hh + 1)], ACT.Silu,
                                       bias=pb[:, 2 * s + hh:2 * s + hh + 1])
                m.then_inc(free, 1)

    @block.gpsimd
    def _(pool):
        pool.dma_start(k.o_wp[0].rearrange("(i p) s g d -> p i (s g d)", p=128), k.kvt[:, 0, 0:NT, :]).then_inc(k.stored_win, 16)
        for s in range(SB):
            pool.dma_start(k.o_ws[s, 512 - SI:512].rearrange("t a g d -> t (a g d)"),
                           k.kvt[SI * s:SI * s + SI, 0, NT, :]).then_inc(k.stored_win, 16)
        pool.wait_ge(k.stored_win, 16 * (1 + 2 * SB))

    @block.vector
    def _(dve):
        dve.wait_ge(k.cw_here, 16 * 6)
        b, free = full_bank(dve, k, "posT")
        dve.tensor_copy(posT[:, :], b[:, 0:32]).then_inc(free, 1)

        def pairs(q):
            dve.wait_ge(k.raw_here[q % 2], 64 * (q // 2 + 1))
            if q:
                bank, n = k.bank_of[("R", q - 1, 1, 1)]
                dve.wait_ge(k.bank_full[bank], n)
            for s in range(2):
                src = raw[:, q % 2, :, :, 256 * s:256 * s + 256]
                for a in range(2):
                    m = dve.tensor_copy(pair[:, :, s, :, a, :], src[:, :, a, :].rearrange("p j (g d) -> p j g d", g=G))
                m.then_inc(k.pair_ready, 1)

        def keep_pairs(q):
            for s in range(2):
                if q >= 2:
                    bank, n = k.bank_of[("hid", q - 2, s)]
                    dve.wait_ge(k.bank_full[bank], n)
                for gp in range(2):
                    b, free = full_bank(dve, k, ("R", q, s, gp))
                    dve.tensor_copy(R[:, q % 2, s, 2 * gp:2 * gp + 2, :], b.rearrange("p (g t) -> p g t", g=2)).then_inc(free, 1)

        def keep_output(q):
            b, free = full_bank(dve, k, ("kc", q))
            dve.tensor_scalar(k.kcT[:, q, :, :], b[:, 0:2 * NCMP].rearrange("p (a n) -> p a n", a=2), b2k[:, :], None, ALU.add).then_inc(free, 1)
            b, free = full_bank(dve, k, ("vc", q))
            bias = b2v[:, :].unsqueeze(1).to_broadcast([NCMP, G, DH])
            src = b[0:NCMP, 0:SLOT].rearrange("p (g d) -> p g d", g=G)
            if q < SB:
                p0 = 32 * (q % 4)
                dve.tensor_tensor(k.vcS[p0:p0 + NCMP, q // 4, :].rearrange("p (g d) -> p g d", g=G), src, bias, ALU.add).then_inc(free, 1)
            else:
                for hh in range(HPG):
                    m = dve.tensor_tensor(k.VBD[32 * hh:32 * hh + NCMP, :, DH * hh:DH * hh + DH], src, bias, ALU.add)
                m.then_inc(free, 1)

        pairs(0)
        keep_pairs(0)
        pairs(1)
        b, free = full_bank(dve, k, "pb")
        dve.tensor_tensor(pb[:, :], b[:, 0:4], k.vecs2[:, 24:28], ALU.add).then_inc(free, 1)
        dve.memset(k.VBD[:, :, :], 0.0).then_inc(k.vbd_clear, 1)
        dve.wait_ge(k.vbd_clear, 1)
        for q in range(NS):
            if q + 1 < NS:
                keep_pairs(q + 1)
            if q + 2 < NS:
                pairs(q + 2)
            if q:
                keep_output(q - 1)
        keep_output(NS - 1)




def stage_query(nc, k, ctx):
    block = ctx.enter_context(nc.Block())
    SCALE = float(DH) ** -0.5

    @block.tensor
    def _(pe):
        for c in range(2):
            w = chunk(pe, k, CH_IN + c)
            for m4 in range(4):
                for hf, (t0, t1) in enumerate(HALF):
                    b, full = open_bank(pe, k, ("q", 4 * c + m4, hf))
                    for kt in range(KD):
                        m = pe.matmul(b[:, 0:t1 - t0], w[:, kt, 128 * m4:128 * m4 + 128], k.xnT[:, kt, t0:t1],
                                      start=kt == 0, stop=kt == KD - 1)
                    m.then_inc(full, 1)
            k.chunk_last[CH_IN + c] = k.bank_of[("q", 4 * c + 3, 1)]
        project_rows(pe, k, "bg", k.xnT, CH_IN + 2, 1)

    @block.sync
    def _(sp):
        load_chunks(sp, k, CH_IN + NW, CH_IN + 3 + NW)

    @block.gpsimd
    def _(pool):
        st = Steps(pool, k.pool_step, k, "pool")
        st.then(pool.memset(k.cmask[:, :, :], 0.0))
        st.then(pool.affine_select(out=k.cmask[:, :, :], in_=k.cmask[:, :, :], compare_op=ALU.is_ge, fill=NEG, base=-31,
                                   pattern=[[128, NT], [-16, 32]], channel_multiplier=1))
        st.then(pool.memset(k.mtmp[:, :], 0.0))
        st.then(pool.affine_select(out=k.mtmp[:, 0:128], in_=k.mtmp[:, 0:128], compare_op=ALU.is_ge, fill=NEG, base=0,
                                   pattern=[[-1, 128]], channel_multiplier=1))
        new = k.mtmp[0:32, 128:128 + SB * S].rearrange("p (b t) -> p b t", b=SB)
        st.then(pool.affine_select(out=new, in_=new, compare_op=ALU.is_ge, fill=NEG, base=0,
                                   pattern=[[-4, SB], [1, S]], channel_multiplier=0))
        st.then(pool.affine_select(out=new, in_=new, compare_op=ALU.is_ge, fill=NEG, base=0,
                                   pattern=[[16, SB], [-4, S]], channel_multiplier=1))
        old = k.mtmp[0:32, 128 + SB * S:132 + SB * S]
        st.then(pool.affine_select(out=old, in_=old, compare_op=ALU.is_ge, fill=NEG, base=-1,
                                   pattern=[[4, 4]], channel_multiplier=-1))
        pool.tensor_copy(k.identb[:, :], k.ident[:, :])
        pool.tensor_copy(k.causb[:, :], k.mtmp[:, 0:128])
        for g in range(G):
            st.then(pool.tensor_copy(k.newb[32 * g:32 * g + 32, :], k.mtmp[0:32, 128:132 + SB * S]))

    @block.scalar
    def _(act):
        act.wait_ge(k.q_clear, 3)
        for m in range(8):
            g = m // 2
            d0 = 64 * (g % 2)
            for hf in range(2):
                b, free = full_bank(act, k, ("q", m, hf))
                for a in range(2):
                    x = act.activation(k.Qp[d0:d0 + 64, 2 * m + a, 256 * hf:256 * hf + 256], b[64 * a:64 * a + 64, 0:256],
                                       ACT.Copy, scale=SCALE)
                    if hf:
                        hh = (2 * m + a) % HPG
                        x = act.activation(k.QS[d0:d0 + 64, :, g, hh:16:HPG],
                                           b[64 * a:64 * a + 64, 256:288].rearrange("p (b i) -> p b i", i=SI), ACT.Copy, scale=SCALE)
                x.then_inc(free, 1)
        for i in range(NT + 1):
            r = 128 if i < NT else S
            b, free = full_bank(act, k, ("bg", i))
            act.activation(k.gt[0:r, i, :], b[0:r, 0:3 * H], ACT.Sigmoid).then_inc(free, 1)

    @block.vector
    def _(dve):
        q = k.Qp[:, :, :].rearrange("p (a g h) t -> p a g (h t)", a=2, g=2)
        dve.memset(q[64:128, :, 0, :], 0.0).then_inc(k.q_clear, 1)
        dve.memset(q[0:64, :, 1, :], 0.0).then_inc(k.q_clear, 1)
        dve.memset(k.QS[:, :, :, :], 0.0).then_inc(k.q_clear, 1)


def z_rows(pe, k, br):
    for c in range(2):
        project_rows(pe, k, ("zb", br, c), k.xnT, CH_IN + 3 + 2 * br + c, 1)


def z_silu(act, k, br):
    for c in range(2):
        for i in range(NT):
            b, free = full_bank(act, k, (("zb", br, c), i))
            act.activation(k.z[:, i, 512 * c:512 * c + 512], b, ACT.Silu).then_inc(free, 1)
        drained(act, k, (("zb", br, c), NT))
        zs = k.z[0:S, NT + (br + 1) % 2, 512 * c:512 * c + 512]
        act.activation(zs, zs, ACT.Silu).then_inc(k.zs_ready, 1)


def z_fold(dve, k, st, br):
    for c in range(2):
        fold(dve, k, st, ("zb", br, c), k.z[0:S, NT + (br + 1) % 2, 512 * c:512 * c + 512])


def z_all(eng, k, br):
    for c in range(2):
        for i in range(NT):
            drained(eng, k, (("zb", br, c), i))


def blend(pool, k, st, br, tmp, z, y):
    if br == 0:
        st.then(pool.tensor_tensor(y, tmp, z, ALU.mult))
    else:
        st.then(pool.tensor_tensor(tmp, tmp, z, ALU.mult))
        st.then(pool.tensor_tensor(y, y, tmp, ALU.add))


def fetch_samples(sp, k, br):
    sp.wait_ge(k.os_stored, 16 * SB * (br + 1))
    for s in range(SB):
        sp.dma_start(k.osall[SI * s:SI * s + SI, :].rearrange("i (g x) -> i g x", g=G),
                     k.scratch[s].rearrange("(g i x) d -> i g (x d)", g=G, i=8)[0:SI]).then_inc(k.os_back, 16)


def finish_samples(pool, k, st, br):
    osall = k.osall
    pool.wait_ge(k.os_back, 16 * SB * (br + 1))
    st.then(pool.tensor_tensor(osall[:, :].rearrange("p (h d) -> p h d", h=H), osall[:, :].rearrange("p (h d) -> p h d", h=H),
                               k.gt[0:S, NT, H * br:H * br + H].unsqueeze(2).to_broadcast([S, H, DH]), ALU.mult))
    pool.wait_ge(k.zs_ready, 2 * (br + 1))
    blend(pool, k, st, br, osall[:, :], k.z[0:S, NT + (br + 1) % 2, :], k.y[0:S, NT, :])


def stage_cmp_branch(nc, k, ctx):
    def sb(name, shape, dt=F32):
        return ctx.enter_context(nc.sbuf_tensor(name, shape, dt))
    Sc = sb("Sc", [128, NT + 1, H, 32])
    Pc = sb("Pc", [128, NT + 1, H, 32])
    PcT = k.kvT.rearrange("p a t -> p (a t)")[:, 0:(NT + 1) * 4 * 128].rearrange("p (i g t) -> p i g t", i=NT + 1, g=4)
    mx = sb("cmx", [128, NT + 1, H])
    sm = sb("csm", [128, NT + 1, H])
    tmp = sb("ctmp", [128, 2, HPG * DH])
    block = ctx.enter_context(nc.Block())
    og0 = k.og

    @block.tensor
    def _(pe):
        for i in range(NT + 1):
            b, full = open_bank(pe, k, ("cS", i))
            if i < NT:
                for h in range(H):
                    m = pe.matmul(b[:, 32 * h:32 * h + NCMP], k.Qp[:, h, 128 * i:128 * i + 128], k.kcT[:, SB, h // 8, :],
                                  start=True, stop=True)
            else:
                for s in range(SB):
                    for g in range(G):
                        m = pe.matmul(b[32 * g:32 * g + 32, 32 * s:32 * s + NCMP], k.QS[:, s, g, :], k.kcT[:, s, g // 2, :],
                                      start=True, stop=True)
            m.then_inc(full, 1)
        project_rows(pe, k, ("zb", 0, 0), k.xnT, CH_IN + 3, 1)
        for i in range(NT + 1):
            pe.wait_ge(k.cp_ready, i + 1)
            b, full = open_bank(pe, k, ("cT", i))
            for g in range(G if i < NT else 2):
                m = pe.transpose(b[:, 128 * g:128 * g + 128], Pc[:, i, 4 * g:4 * g + 4, :].rearrange("p h n -> p (h n)"), k.ident[:, :])
            m.then_inc(full, 1)
        project_rows(pe, k, ("zb", 0, 1), k.xnT, CH_IN + 4, 1)
        drained(pe, k, ("cT", NT))
        for r in range(4):
            b, full = open_bank(pe, k, ("cO", r))
            for a in range(2):
                for g in range(G):
                    m = pe.matmul(b[32 * g:32 * g + 32, DH * a:DH * a + DH], PcT[32 * r:32 * r + NCMP, NT, a, 32 * g:32 * g + 32],
                                  k.vcS[32 * r:32 * r + NCMP, a, DH * g:DH * g + DH], start=True, stop=True)
            m.then_inc(full, 1)
        for i in range(NT):
            drained(pe, k, ("cT", i))
            for g in range(G):
                o = G * i + g
                if og0 + o >= 2:
                    pe.wait_ge(k.o_free, og0 + o - 1)
                pe.matmul(k.ps[:, 6 + o % 2, 0:256], PcT[:, i, g, :], k.VBD[:, g, :],
                          start=True, stop=True).then_inc(k.o_full, 1)

    @block.sync
    def _(sp):
        load_chunks(sp, k, CH_IN + 3 + NW, CH_IN + 5 + NW)
        for r in range(4):
            drained(sp, k, ("cO", r))
        for s in range(SB):
            sp.dma_start(k.scratch[s], k.osb[:, s, :]).then_inc(k.os_stored, 16)

    @block.scalar
    def _(act):
        for i in range(NT + 1):
            act.wait_ge(k.cs_ready, i + 1)
            n = H if i < NT else SB
            act.activation(Pc[:, i, 0:n, :], Sc[:, i, 0:n, :], ACT.Exp).then_inc(k.cp_ready, 1)
        z_silu(act, k, 0)

    @block.vector
    def _(dve):
        st = Steps(dve, k.dve_step, k, "dve")
        st.then(dve.memset(Sc[:, :, :, :], NEG))
        for i in range(NT + 1):
            n = H if i < NT else SB
            b, free = full_bank(dve, k, ("cS", i))
            s_, m_ = Sc[:, i, 0:n, :], mx[:, i, 0:n]
            src = b[:, 0:32 * n].rearrange("p (h n) -> p h n", n=32)[:, :, 0:NCMP]
            if i < NT:
                st.then(dve.tensor_tensor(s_[:, :, 0:NCMP], src, k.cmask[:, i, 0:NCMP].unsqueeze(1).to_broadcast([128, H, NCMP]), ALU.add))
            else:
                st.then(dve.tensor_copy(s_[:, :, 0:NCMP], src))
            dve.sem_inc(free, 1)
            st.then(dve.tensor_reduce(out=m_, in_=s_, axis=AX.X, op=ALU.max))
            st.then(dve.tensor_scalar(m_, m_, NEG / 10, None, ALU.max))
            dve.tensor_tensor(s_, s_, m_.unsqueeze(2).to_broadcast([128, n, 32]), ALU.subtract).then_inc(k.cs_ready, 1)
        for i in range(NT + 1):
            n = H if i < NT else SB
            m_ = sm[:, i, 0:n]
            dve.wait_ge(k.cp_ready, i + 1)
            st.then(dve.tensor_reduce(out=m_, in_=Pc[:, i, 0:n, :], axis=AX.X, op=ALU.add))
            st.then(dve.tensor_scalar(m_, m_, 1.0e-30, None, ALU.max))
            st.then(dve.reciprocal(m_, m_))
            if i < NT:
                st.then(dve.tensor_tensor(m_, m_, k.gt[:, i, 0:H], ALU.mult))
        fold(dve, k, st, ("zb", 0, 0), k.z[0:S, NT + 1, 0:512])
        for i in range(NT + 1):
            n = G if i < NT else 2
            b, free = full_bank(dve, k, ("cT", i))
            dve.tensor_copy(PcT[:, i, 0:n, :], b[:, 0:128 * n].rearrange("p (g t) -> p g t", g=n)).then_inc(free, 1)
        fold(dve, k, st, ("zb", 0, 1), k.z[0:S, NT + 1, 512:1024])
        for r in range(4):
            b, free = full_bank(dve, k, ("cO", r))
            dve.tensor_tensor(k.osb[:, r:SB:4, :], b[:, 0:2 * DH].rearrange("p (a d) -> p a d", d=DH),
                              sm[:, NT, r:SB:4].unsqueeze(2).to_broadcast([128, 2, DH]), ALU.mult).then_inc(free, 1)
        for o in range(G * NT):
            i, g = o // G, o % G
            dve.wait_ge(k.o_full, og0 + o + 1)
            if o >= 2:
                dve.wait_ge(k.blended, og0 + o - 1)
            dve.tensor_tensor(tmp[:, o % 2, :].rearrange("p (h d) -> p h d", h=HPG),
                              k.ps[:, 6 + o % 2, 0:256].rearrange("p (h d) -> p h d", h=HPG),
                              sm[:, i, 4 * g:4 * g + 4].unsqueeze(2).to_broadcast([128, HPG, DH]), ALU.mult).then_inc(k.o_free, 1)

    @block.gpsimd
    def _(pool):
        st = Steps(pool, k.pool_step, k, "pool")
        z_all(pool, k, 0)
        for i in range(NT):
            for g in range(G):
                o = G * i + g
                pool.wait_ge(k.o_free, og0 + o + 1)
                blend(pool, k, st, 0, tmp[:, o % 2, :], k.z[:, i, 256 * g:256 * g + 256], k.y[:, i, 256 * g:256 * g + 256])
                pool.sem_inc(k.blended, 1)
    k.og += G * NT


def stage_key_branch(nc, k, ctx, br):
    def sb(name, shape, dt=F32):
        return ctx.enter_context(nc.sbuf_tensor(f"{name}_{br}", shape, dt))
    TURN, MUL = 2, 4
    P = sb("P", [128, 3, T])
    PT = sb("PT", [128, 3, T])
    nmx = sb("nmx", [128, 4])
    sm = sb("sm", [128, NT, H])
    rc = sb("rc", [128, 2, HPG])
    tmp = sb("tmp", [128, 2, HPG * DH])
    sP = sb("sP", [128, TA])
    sPT = sb("sPT", [128, T + 128])
    snmx = sb("snmx", [128, 3])
    ss = sb("ss", [128, 3])
    KTs = sb("KTs", [128, 2, T])
    raw = k.arena[:, (NT + 1) * D:(NT + 1) * D + 4096].rearrange("p (s r x) -> p s r x", s=2, r=4)
    block = ctx.enter_context(nc.Block())
    og0 = k.og
    items = [(i, h) for i in range(NT) for h in range(H)]
    NI = len(items)
    EVERY = NI // SB
    KEYS, SCORES, TURNS, VALUES = 0, 2, 4, 6
    v = br - 1

    def sequence(n, stage):
        return n // EVERY if n < NI and n % EVERY == stage else None
    max_no = {}
    for n in range(NI):
        max_no["A", n] = k.maxima + len(max_no) + 1
        if sequence(n, SCORES) is not None:
            max_no["sA", sequence(n, SCORES)] = k.maxima + len(max_no) + 1

    @block.tensor
    def _(pe):
        z_rows(pe, k, br)
        for n in range(NI + MUL):
            if n < NI:
                i, h = items[n]
                w = 128 * (i + 1)
                b, full = open_bank(pe, k, ("A", br, n))
                pe.matmul(b[:, 0:w], k.Qp[:, h, 128 * i:128 * i + 128], k.KT[:, v, h // 8, 0:w], start=True, stop=True)
                pe.matmul(b[:, w - 128:w], k.identb[:, :], k.causb[:, :], start=False, stop=True,
                          skip_group_check=True).then_inc(full, 1)
            s = sequence(n, KEYS)
            if s is not None:
                pe.wait_ge(k.raw_slot[s % 2], 16 * k.raw_loads(br, s))
                for gp in range(2):
                    b, full = open_bank(pe, k, ("sK", br, s, gp))
                    for r in range(4):
                        m = pe.transpose(b[:, 128 * r:128 * r + 128], raw[:, s % 2, r, 128 * gp:128 * gp + 128], k.ident[:, :])
                    m.then_inc(full, 1)
            s = sequence(n, SCORES)
            if s is not None:
                drained(pe, k, ("sK", br, s, 0))
                drained(pe, k, ("sK", br, s, 1))
                b, full = open_bank(pe, k, ("sA", br, s))
                for g in range(G):
                    m = pe.matmul(b[32 * g:32 * g + 32, :], k.QS[:, s, g, :], KTs[:, g // 2, :], start=True, stop=True)
                if br == 2:
                    m = pe.matmul(b[:, 0:T:128], k.identb[:, :], k.newb[:, SB * S:SB * S + 4], start=False, stop=True,
                                  skip_group_check=True)
                m.then_inc(full, 1)
                b, full = open_bank(pe, k, ("sN", br, s))
                for g in range(G):
                    pe.matmul(b[32 * g:32 * g + 32, 0:S], k.QS[:, s, g, :], k.KT[:, v, g // 2, T:TA], start=True, stop=True)
                pe.matmul(b[:, 0:S], k.identb[:, :], k.newb[:, S * s:S * s + S], start=False, stop=True,
                          skip_group_check=True).then_inc(full, 1)
            s = sequence(n, TURNS)
            if s is not None:
                drained(pe, k, ("sA", br, s))
                drained(pe, k, ("sN", br, s))
                b, full = open_bank(pe, k, ("sT", br, s))
                for r in range(4):
                    m = pe.transpose(b[:, 128 * r:128 * r + 128], sP[:, 128 * r:128 * r + 128], k.ident[:, :])
                m.then_inc(full, 1)
                b, full = open_bank(pe, k, ("sTn", br, s))
                pe.transpose(b[0:S, 0:128], sP[:, T:TA], k.ident[:, :]).then_inc(full, 1)
            s = sequence(n, VALUES)
            if s is not None:
                drained(pe, k, ("sT", br, s))
                drained(pe, k, ("sTn", br, s))
                b, full = open_bank(pe, k, ("sO", br, s))
                for g in range(G):
                    for r in range(4):
                        pe.matmul(b[32 * g:32 * g + 32, 0:DH], sPT[:, 128 * r + 32 * g:128 * r + 32 * g + 32],
                                  raw[:, s % 2, r, SLOT + DH * g:SLOT + DH * g + DH], start=r == 0, stop=False)
                    m = pe.matmul(b[32 * g:32 * g + 32, 0:DH], sPT[0:S, T + 32 * g:T + 32 * g + 32],
                                  k.V[0:S, v, NT, DH * g:DH * g + DH], start=False, stop=True)
                m.then_inc(full, 1)
            if TURN <= n < NI + TURN:
                i, h = items[n - TURN]
                drained(pe, k, ("A", br, n - TURN))
                b, full = open_bank(pe, k, ("T", br, n - TURN))
                for j in range(i + 1):
                    m = pe.transpose(b[:, 128 * j:128 * j + 128], P[:, (n - TURN) % 3, 128 * j:128 * j + 128], k.ident[:, :])
                m.then_inc(full, 1)
            if n >= MUL:
                i, h = items[n - MUL]
                drained(pe, k, ("T", br, n - MUL))
                o, hh = (n - MUL) // HPG, (n - MUL) % HPG
                if hh == 0 and og0 + o >= 2:
                    pe.wait_ge(k.o_free, og0 + o - 1)
                g = h // HPG
                for j in range(i + 1):
                    m = pe.matmul(k.ps[:, 6 + o % 2, DH * hh:DH * hh + DH], PT[:, (n - MUL) % 3, 128 * j:128 * j + 128],
                                  k.V[:, v, j, DH * g:DH * g + DH], start=j == 0, stop=j == i)
                m.then_inc(k.pv_done, 1)

    @block.sync
    def _(sp):
        for s in range(SB):
            if s == 2:
                fetch_samples(sp, k, br - 1)
                load_chunks(sp, k, CH_IN + 3 + 2 * br + NW, CH_IN + 5 + 2 * br + NW)
            if s >= 2:
                bank, n = k.bank_of[("sO", br, s - 2)]
                sp.wait_ge(k.bank_full[bank], n)
            if br == 1:
                for pg in range(4):
                    page = sp.value_load(k.pages[0:1, 4 * s + pg:4 * s + pg + 1], min_val=0, max_val=k.cache_kv.shape[0] - 1)
                    src = k.cache_kv[bass.ds(page, 1)].rearrange("o (t r) s g d -> (o t) r (s g d)", r=4)[:, :, 2 * SLOT:4 * SLOT]
                    sp.dma_start(raw[32 * pg:32 * pg + 32, s % 2, :, :], src).then_inc(k.raw_slot[s % 2], 16)
            else:
                sp.dma_start(raw[:, s % 2, :, :], k.cache_win[s].rearrange("(t r) a g d -> t r (a g d)", r=4)).then_inc(k.raw_slot[s % 2], 16)
        sp.wait_ge(k.os_back, 16 * SB * br)
        for s in range(SB):
            drained(sp, k, ("sO", br, s))
            sp.dma_start(k.scratch[s], k.osb[:, s, :]).then_inc(k.os_stored, 16)

    @block.scalar
    def _(act):
        z_silu(act, k, br)
        for n in range(NI):
            i, h = items[n]
            w = 128 * (i + 1)
            act.wait_ge(k.mx_ready, max_no["A", n])
            b, free = full_bank(act, k, ("A", br, n))
            if n >= 3:
                bank, c = k.bank_of[("T", br, n - 3)]
                act.wait_ge(k.bank_full[bank], c)
            act.activation(P[:, n % 3, 0:w], b[:, 0:w], ACT.Exp, bias=nmx[:, n % 4:n % 4 + 1], accum_out=sm[:, i, h:h + 1]).then_inc(free, 1)
            s = sequence(n, SCORES)
            if s is not None:
                act.wait_ge(k.mx_ready, max_no["sA", s])
                if s:
                    bank, c = k.bank_of[("sTn", br, s - 1)]
                    act.wait_ge(k.bank_full[bank], c)
                if SB * v + s:
                    act.wait_ge(k.ss_used, SB * v + s)
                b, free = full_bank(act, k, ("sA", br, s))
                act.activation(sP[:, 0:T], b[:, :], ACT.Exp, bias=snmx[:, 2:3], accum_out=ss[:, 0:1]).then_inc(free, 1)
                b, free = full_bank(act, k, ("sN", br, s))
                act.activation(sP[:, T:TA], b[:, 0:S], ACT.Exp, bias=snmx[:, 2:3], accum_out=ss[:, 1:2]).then_inc(free, 1)

    @block.vector
    def _(dve):
        st = Steps(dve, k.dve_step, k, "dve")
        z_fold(dve, k, st, br)

        def maximum(n):
            i, h = items[n]
            b, _ = full_bank(dve, k, ("A", br, n))
            if n >= 4:
                drained(dve, k, ("A", br, n - 4))
            dve.tensor_reduce(out=nmx[:, n % 4:n % 4 + 1], in_=b[:, 0:128 * (i + 1)], axis=AX.X, op=ALU.max, negate=True).then_inc(k.mx_ready, 1)

        def keep(n):
            i, h = items[n]
            if n >= 3:
                dve.wait_ge(k.pv_done, NI * v + n - 2)
            b, free = full_bank(dve, k, ("T", br, n))
            dve.tensor_copy(PT[:, n % 3, 0:128 * (i + 1)], b[:, 0:128 * (i + 1)]).then_inc(free, 1)

        def out(o):
            i, g = o // G, o % G
            drained(dve, k, ("A", br, HPG * o + HPG - 1))
            st.then(dve.reciprocal(rc[:, o % 2, :], sm[:, i, HPG * g:HPG * g + HPG]))
            st.then(dve.tensor_tensor(rc[:, o % 2, :], rc[:, o % 2, :], k.gt[:, i, H * br + HPG * g:H * br + HPG * g + HPG], ALU.mult))
            dve.wait_ge(k.pv_done, NI * v + HPG * (o + 1))
            if o >= 2:
                dve.wait_ge(k.blended, og0 + o - 1)
            dve.tensor_tensor(tmp[:, o % 2, :].rearrange("p (h d) -> p h d", h=HPG),
                              k.ps[:, 6 + o % 2, 0:256].rearrange("p (h d) -> p h d", h=HPG),
                              rc[:, o % 2, :].unsqueeze(2).to_broadcast([128, HPG, DH]), ALU.mult).then_inc(k.o_free, 1)

        for n in range(NI + MUL + 1):
            if n < NI:
                maximum(n)
            s = sequence(n, KEYS)
            if s is not None:
                for gp in range(2):
                    b, free = full_bank(dve, k, ("sK", br, s, gp))
                    if s:
                        bank, c = k.bank_of[("sA", br, s - 1)]
                        dve.wait_ge(k.bank_full[bank], c)
                    dve.tensor_copy(KTs[:, gp, :], b[:, :]).then_inc(free, 1)
            s = sequence(n, SCORES)
            if s is not None:
                if s:
                    drained(dve, k, ("sN", br, s - 1))
                b, _ = full_bank(dve, k, ("sA", br, s))
                dve.tensor_reduce(out=snmx[:, 0:1], in_=b[:, :], axis=AX.X, op=ALU.max)
                b, _ = full_bank(dve, k, ("sN", br, s))
                st.then(dve.tensor_reduce(out=snmx[:, 1:2], in_=b[:, 0:S], axis=AX.X, op=ALU.max))
                dve.tensor_reduce(out=snmx[:, 2:3], in_=snmx[:, 0:2], axis=AX.X, op=ALU.max, negate=True).then_inc(k.mx_ready, 1)
            s = sequence(n, TURNS)
            if s is not None:
                if s:
                    bank, c = k.bank_of[("sO", br, s - 1)]
                    dve.wait_ge(k.bank_full[bank], c)
                b, free = full_bank(dve, k, ("sT", br, s))
                dve.tensor_copy(sPT[:, 0:T], b[:, :]).then_inc(free, 1)
                b, free = full_bank(dve, k, ("sTn", br, s))
                dve.tensor_copy(sPT[0:S, T:T + 128], b[0:S, 0:128]).then_inc(free, 1)
            s = sequence(n, VALUES)
            if s is not None:
                drained(dve, k, ("sN", br, s))
                st.then(dve.tensor_tensor(ss[:, 2:3], ss[:, 0:1], ss[:, 1:2], ALU.add))
                st.then(dve.reciprocal(ss[:, 2:3], ss[:, 2:3]))
                b, free = full_bank(dve, k, ("sO", br, s))
                st.then(dve.tensor_scalar(k.osb[:, s, :], b[:, 0:DH], ss[:, 2:3], None, ALU.mult))
                dve.sem_inc(free, 1)
                dve.sem_inc(k.ss_used, 1)
            if TURN <= n < NI + TURN:
                keep(n - TURN)
            if n > MUL and (n - MUL) % HPG == 0:
                out((n - MUL) // HPG - 1)

    @block.gpsimd
    def _(pool):
        st = Steps(pool, k.pool_step, k, "pool")
        finish_samples(pool, k, st, br - 1)
        z_all(pool, k, br)
        for o in range(NI // HPG):
            i, g = o // G, o % G
            pool.wait_ge(k.o_free, og0 + o + 1)
            blend(pool, k, st, br, tmp[:, o % 2, :], k.z[:, i, 256 * g:256 * g + 256], k.y[:, i, 256 * g:256 * g + 256])
            pool.sem_inc(k.blended, 1)
    k.og += NI // HPG
    k.maxima += NI + SB


def stage_out(nc, k, ctx):
    def sb(name, shape, dt=F32):
        return ctx.enter_context(nc.sbuf_tensor(name, shape, dt))
    yT = sb("yT", [128, KD, TA])
    yo = sb("yo", [128, NT + 1, D])
    xr = k.z[:, 0:NT + 1, :]
    npost = sb("npost2", [128, D])
    sq = sb("sq3", [128, D])
    ssq = sb("ssq3", [128, NT + 1])
    rstd = sb("rstd3", [128, NT + 1])
    norms = RowNorms(k, [("o", i) for i in TILES], ssq, rstd, 3 * (NT + 1))
    block = ctx.enter_context(nc.Block())

    @block.tensor
    def _(pe):
        for kt in range(KD):
            b, full = open_bank(pe, k, ("yT", kt))
            for i in range(NT):
                m = pe.transpose(b[:, 128 * i:128 * i + 128], k.y[:, i, 128 * kt:128 * kt + 128], k.ident[:, :])
            m.then_inc(full, 1)
        for kt in range(KD):
            drained(pe, k, ("yT", kt))

        def samples():
            pe.wait_ge(k.y_ready, 1)
            b, full = open_bank(pe, k, "yTs")
            for kt in range(KD):
                m = pe.transpose(b[:, S * kt:S * kt + S], k.y[0:S, NT, 128 * kt:128 * kt + 128], k.ident[0:S, 0:S])
            m.then_inc(full, 1)
            drained(pe, k, "yTs")
        for n in range(D // 512):
            project_rows(pe, k, ("o", n), yT, CH_OUT + n, 1, order=TILES if n else TILES[1:] + TILES[:1],
                         before=None if n else samples)

    @block.sync
    def _(sp):
        fetch_samples(sp, k, 2)
        sp.dma_start(xr[:, 0:NT, :], k.o_yp[0].rearrange("(i p) d -> p i d", p=128)).then_inc(k.x_here, 16)
        sp.dma_start(xr[0:S, NT, :], k.o_ys.rearrange("b i d -> (b i) d")).then_inc(k.x_here, 16)
        sp.dma_start(npost[:, :], k.b_norm_post.partition_broadcast(128)).then_inc(k.x_here, 16)
        for n, i in enumerate(TILES):
            sp.wait_ge(k.res_ready, NT + 1 + n + 1)
            if i < NT:
                sp.dma_start(k.o_yp[0, 128 * i:128 * i + 128, :], xr[:, i, :]).then_inc(k.stored_y, 16)
            else:
                sp.dma_start(k.o_ys.rearrange("b i d -> (b i) d"), xr[0:S, NT, :]).then_inc(k.stored_y, 16)
        sp.wait_ge(k.stored_y, 16 * (NT + 1))

    @block.scalar
    def _(act):
        for n in range(D // 512):
            if n:
                drained(act, k, (("o", 0), NT))
                drained(act, k, (("o", 1), NT))
                norms.square(act, ("o", NT), yo[0:S, NT, :], sq[0:S, :])
                norms.root(act, ("o", NT))
            for i in range(NT):
                b, free = full_bank(act, k, (("o", n), i))
                act.activation(yo[:, i, 512 * n:512 * n + 512], b, ACT.Copy).then_inc(free, 1)
                if n:
                    drained(act, k, (("o", n), i))
                    norms.square(act, ("o", i), yo[:, i, :], sq[:, :])
                    norms.root(act, ("o", i))

    @block.gpsimd
    def _(pool):
        st = Steps(pool, k.pool_step, k, "pool")
        finish_samples(pool, k, st, 2)
        pool.sem_inc(k.y_ready, 1)

    @block.vector
    def _(dve):
        st = Steps(dve, k.dve_step, k, "dve")
        for kt in range(KD):
            b, free = full_bank(dve, k, ("yT", kt))
            dve.tensor_copy(yT[:, kt, 0:T], b[:, 0:T]).then_inc(free, 1)
        b, free = full_bank(dve, k, "yTs")
        dve.tensor_copy(yT[:, :, T:TA], b[:, 0:KD * S].rearrange("p (a b) -> p a b", b=S)).then_inc(free, 1)
        for n in range(D // 512):
            fold(dve, k, st, ("o", n), yo[0:S, NT, 512 * n:512 * n + 512])
        dve.wait_ge(k.x_here, 16 * 6)
        for i in TILES:
            norms.mean(dve, ("o", i))
            norm_residual(k, dve, st, yo, xr, npost, norms.invert(dve, st, ("o", i)), i)


def stage_attention(nc, k, sb, ctx):
    def raw_loads(br, s):
        return 4 * (s // 2 + 1) if br == 1 else 4 * (SB // 2) + s // 2 + 1
    k.raw_loads = raw_loads
    k.nring = 6
    k.og = k.maxima = 0
    k.y = k.x1
    k.scratch = nc.dram_tensor("sample_rows", [SB, 128, DH], F32, kind="Internal").ap()
    k.gt = sb("gt", [128, NT + 1, 3 * H])
    k.z = sb("z", [128, NT + 2, ATT])
    k.osb = sb("osb", [128, SB, DH])
    k.osall = sb("osall", [S, ATT])
    with ExitStack() as att:
        k.Qp = sb("Qp", [128, H, T], where=att)
        k.QS = sb("QS", [128, SB, G, 32], where=att)
        k.cmask = sb("cmask", [128, NT, 32], where=att)
        k.identb = sb("identb", [128, 128], BF16, where=att)
        k.causb = sb("causb", [128, 128], BF16, where=att)
        k.newb = sb("newb", [128, SB * S + 4], BF16, where=att)
        with ExitStack() as c:
            k.mtmp = sb("mtmp", [128, 132 + SB * S], where=c)
            stage_query(nc, k, c)
        with ExitStack() as c:
            stage_cmp_branch(nc, k, c)
        for br in (1, 2):
            with ExitStack() as c:
                stage_key_branch(nc, k, c, br)
    with ExitStack() as c:
        stage_out(nc, k, c)


def build(nc, a, outs):
    k = Ctx()
    with ExitStack() as ctx:
        def sb(name, shape, dt=F32, where=ctx):
            return where.enter_context(nc.sbuf_tensor(name, shape, dt))

        def sem(name):
            return ctx.enter_context(nc.semaphore(name))
        k.x_prompt, k.x_sample, k.cache_kv, k.page_table, k.cache_win = (a[n] for n in (
            'x_prompt', 'x_sample', 'cache_kv', 'page_table', 'cache_win'))
        k.state_C, k.state_n, k.state_m, k.state_conv = (a[n][0] for n in ('state_C', 'state_n', 'state_m', 'state_conv'))
        k.a_norm_pre, k.w_up, k.conv_b, k.w_q, k.w_k, k.w_v, k.w_if, k.b_if, k.mh_w, k.skip, k.w_down, k.a_norm_post = (
            a[n][0] for n in ('a_norm_pre', 'a_w_up', 'a_conv_b', 'a_w_q', 'a_w_k', 'a_w_v', 'a_w_if', 'a_b_if',
                              'a_mh_w', 'a_skip', 'a_w_down', 'a_norm_post'))
        k.conv_w = a['a_conv_w'][0].rearrange("j c -> (j c)")
        k.kv_norm, k.w_kv, k.cmp_pos, k.cmp_w1, k.cmp_w2, k.cmp_b2 = (
            a[n] for n in ('kv_norm', 'w_kv', 'cmp_pos', 'cmp_w1', 'cmp_w2', 'cmp_b2'))
        k.cmp_b1 = a['cmp_b1'].rearrange("s n -> (s n)")
        k.b_norm_pre, k.w_in, k.w_out, k.b_norm_post = (a[n][0] for n in ('b_norm_pre', 'b_w_in', 'b_w_out', 'b_norm_post'))
        (k.o_yp, k.o_ys, k.o_kvp, k.o_kvs, k.o_wp, k.o_ws, k.o_cp, k.o_cs, k.o_np, k.o_ns, k.o_mp, k.o_ms,
         k.o_conv_p, k.o_conv_s) = outs
        k.o_conv_p, k.o_conv_s = k.o_conv_p[0, 0], k.o_conv_s[0]
        k.chunks = weight_chunks(k)
        k.ps = ctx.enter_context(nc.psum_tensor("ps", [128, 8, 512], F32))
        k.bank_full = [sem(f"bank_full{b}") for b in range(NRING)]
        k.bank_free = [sem(f"bank_free{b}") for b in range(NRING)]
        k.turns, k.bank_turns, k.bank_of, k.steps, k.chunk_last = 0, [0] * NRING, {}, {}, {}
        k.chunk_here = [sem(f"chunk_here{n}") for n in range(NW)]
        k.x_tile = [sem(f"x_tile{n}") for n in range(NT + 1)]
        k.c_here = [sem(f"c_here{n}") for n in range(NCS)]
        k.c_stored = [sem(f"c_stored{n}") for n in range(NCS)]
        k.raw_here = [sem(f"raw_here{n}") for n in range(2)]
        k.raw_slot = [sem(f"raw_slot{n}") for n in range(2)]
        k.cst_stored = [sem(f"cst_stored{n}") for n in range(2)]
        k.x_here = sem("x_here")
        k.vec_here = sem("vec_here")
        k.ssq_ready = sem("ssq_ready")
        k.ms_ready = sem("ms_ready")
        k.std_ready = sem("std_ready")
        k.xn_tok = sem("xn_tok")
        k.ident_ready = sem("ident_ready")
        k.pool_step = sem("pool_step")
        k.dve_step = sem("dve_step")
        k.crow_here = sem("crow_here")
        k.wraw_here = sem("wraw_here")
        k.wif_here = sem("wif_here")
        k.bif_here = sem("bif_here")
        k.m0_here = sem("m0_here")
        k.nraw_here = sem("nraw_here")
        k.bd_ready = sem("bd_ready")
        k.pad_clear = sem("pad_clear")
        k.conv_ready = sem("conv_ready")
        k.xc_ready = sem("xc_ready")
        k.tails_ready = sem("tails_ready")
        k.stored = sem("stored")
        k.rows_ready = sem("rows_ready")
        k.wrow_ready = sem("wrow_ready")
        k.absf_ready = sem("absf_ready")
        k.softplus_ready = sem("softplus_ready")
        k.stored_m = sem("stored_m")
        k.p_ready = sem("p_ready")
        k.qm_ready = sem("qm_ready")
        k.acc_free = sem("acc_free")
        k.acc_full = sem("acc_full")
        k.km_ready = sem("km_ready")
        k.ks_ready = sem("ks_ready")
        k.vs_ready = sem("vs_ready")
        k.hn_ready = sem("hn_ready")
        k.num4_ready = sem("num4_ready")
        k.prod_ready = sem("prod_ready")
        k.n_ready = sem("n_ready")
        k.nbd_ready = sem("nbd_ready")
        k.qw_ready = sem("qw_ready")
        k.skip_ready = sem("skip_ready")
        k.cst_ready = sem("cst_ready")
        k.stored_n = sem("stored_n")
        k.w_ready = sem("w_ready")
        k.var_ready = sem("var_ready")
        k.sd_ready = sem("sd_ready")
        k.gated = sem("gated")
        k.half_done = sem("half_done")
        k.res_ready = sem("res_ready")
        k.stored_x1 = sem("stored_x1")
        k.kv_here = sem("kv_here")
        k.stored_win = sem("stored_win")
        k.stored_kv = sem("stored_kv")
        k.kvt_free = sem("kvt_free")
        k.cw_here = sem("cw_here")
        k.pair_ready = sem("pair_ready")
        k.pages_here = sem("pages_here")
        k.vbd_clear = sem("vbd_clear")
        k.q_clear = sem("q_clear")
        k.os_stored = sem("os_stored")
        k.os_back = sem("os_back")
        k.cp_ready = sem("cp_ready")
        k.cs_ready = sem("cs_ready")
        k.o_full = sem("o_full")
        k.o_free = sem("o_free")
        k.blended = sem("blended")
        k.pv_done = sem("pv_done")
        k.mx_ready = sem("mx_ready")
        k.ss_used = sem("ss_used")
        k.zs_ready = sem("zs_ready")
        k.y_ready = sem("y_ready")
        k.w_high = sem("w_high")
        k.w_low = sem("w_low")
        k.x_high = sem("x_high")
        k.x_low = sem("x_low")
        k.stored_y = sem("stored_y")
        k.wring = sb("wring", [128, NW, WCH])
        k.ident = sb("ident", [128, 128])
        k.ones = sb("ones", [128, 128])
        k.mask32 = sb("mask32", [128, 32])
        k.maskT = sb("maskT", [128, 128])
        k.maskS = sb("maskS", [S, S])
        k.bmask = sb("bmask", [128, SB, S])
        k.tmask = sb("tmask", [128, SB])
        k.fold = sb("fold", [128, S])
        k.pages = sb("pages", [1, SB * 4], I32)
        k.vecs1 = sb("vecs1", [128, 112])
        k.vecs2 = sb("vecs2", [128, 28])
        k.xnT = sb("xnT", [128, KD, TA])
        k.arena = sb("arena", [128, (NT + 1) * D + KD * TA])
        k.x1 = k.arena[:, 0:(NT + 1) * D].rearrange("p (i d) -> p i d", d=D)
        k.kvT = k.arena[:, (NT + 1) * D:].rearrange("p (a t) -> p a t", t=TA)
        k.halves, k.nring = 0, NRING
        with ExitStack() as mlstm:
            k.scan_add = sb("scan_add", [AH, TA], where=mlstm)
            k.scan_mul = sb("scan_mul", [AH, TA], where=mlstm)
            k.headsel = sb("headsel", [AH, AH, 128], where=mlstm)
            with ExitStack() as c:
                stage_norm_in(nc, k, c)
            k.xcT = sb("xcT", [128, FT, TA], where=mlstm)
            with ExitStack() as cell:
                k.xrow = k.arena[:, 0:FT * XPW].rearrange("p (f x) -> p f x", x=XPW)
                k.xp = k.xrow[:, :, 0:XPS]
                k.xs = k.xrow[:, :, XPS:XPW].rearrange("p f (b j) -> p f b j", b=SB)
                k.xms = sb("xms", [128, FT, S], where=cell)
                k.wraw = sb("wraw", [128, 3, FT, 4], where=cell)
                k.bd = sb("bd", [128, 3, 4, 128], where=cell)
                k.bif = sb("bif", [36, 1], where=cell)
                k.m0 = sb("m0", [AH, SB], where=cell)
                k.nT = sb("nT", [128, 128], where=cell)
                k.gates = k.wring[0:AH, 0, 0:2 * TA].rearrange("p (a t) -> p a t", t=TA)
                with ExitStack() as c:
                    stage_up(nc, k, c)
                k.brow = sb("brow", [AH, TA + S + SB], where=cell)
                k.cols = sb("cols", [128, NT + 1, 96], where=cell)
                with ExitStack() as c:
                    stage_gates(nc, k, c)
                with ExitStack() as c:
                    stage_cell(nc, k, c)
            with ExitStack() as c:
                stage_gate(nc, k, c)
            with ExitStack() as c:
                stage_down(nc, k, c)
        k.V = sb("V", [128, 2, NT + 1, SLOT])
        k.KT = sb("KT", [128, 2, 2, TA])
        k.kcT = sb("kcT", [128, SB + 1, 2, NCMP])
        k.vcS = sb("vcS", [128, 2, SLOT])
        k.VBD = sb("VBD", [128, G, HPG * DH])
        with ExitStack() as ahead:
            k.craw = sb("craw", [128, 2, 2, 2, 512], where=ahead)
            k.cw2 = sb("cw2", [128, 2, 2, DH], where=ahead)
            k.cb2k = sb("cb2k", [128, 1], where=ahead)
            k.cb2v = sb("cb2v", [NCMP, DH], where=ahead)
            k.kvt = sb("kvt", [128, 2, NT + 1, 2 * SLOT], where=ahead)
            k.posr = sb("posr", [32, 128], where=ahead)
            with ExitStack() as c:
                stage_kv(nc, k, c)
            with ExitStack() as c:
                stage_compress(nc, k, c)
        stage_attention(nc, k, sb, ctx)


_INS = ['x_prompt', 'x_sample', 'cache_kv', 'page_table', 'cache_win', 'state_C', 'state_n', 'state_m', 'state_conv',
        'a_norm_pre', 'a_w_up', 'a_conv_w', 'a_conv_b', 'a_w_q', 'a_w_k', 'a_w_v', 'a_w_if', 'a_b_if', 'a_mh_w',
        'a_skip', 'a_w_down', 'a_norm_post', 'kv_norm', 'w_kv', 'cmp_pos', 'cmp_w1', 'cmp_b1', 'cmp_w2', 'cmp_b2',
        'b_norm_pre', 'b_w_in', 'b_w_out', 'b_norm_post']
_OUTS = [(1, 512, 1024), (8, 4, 1024), (1, 512, 4, 4, 64), (8, 4, 4, 4, 64), (1, 512, 2, 4, 64), (8, 512, 2, 4, 64),
         (1, 1, 4, 512, 512), (1, 8, 4, 512, 512), (1, 1, 4, 512), (1, 8, 4, 512), (1, 1, 4), (1, 8, 4),
         (1, 1, 3, 2048), (1, 8, 3, 2048)]


def kernel(**inputs):
    import numpy as _np
    import concourse.bacc as _bacc
    from concourse import mybir as _mybir
    from concourse.bass_utils import run_bass_kernel_spmd as _run

    nc = _bacc.Bacc("TRN2", target_bir_lowering=False, num_devices=1)
    arrays, ins, outs = {}, {}, []
    for name in _INS:
        a = _np.ascontiguousarray(inputs[name])
        arrays[f"in_{name}_dram"] = a
        ins[name] = nc.dram_tensor(f"in_{name}_dram", a.shape, _mybir.dt.from_np(a.dtype), kind="ExternalInput").ap()
    for i, shape in enumerate(_OUTS):
        outs.append(nc.dram_tensor(f"out_{i}_dram", shape, _mybir.dt.float32, kind="ExternalOutput").ap())
    build(nc, ins, outs)
    r = _run(nc, [arrays], core_ids=[0])
    return tuple(r.results[0][f"out_{i}_dram"] for i in range(len(_OUTS)))
```
